# Optimizing a Trainium2 kernel written in Bass

```python
import jax, jax.numpy as jnp
from jax import lax
import numpy as np

D_MODEL = 1024
BATCH = 1
SEQ = 1024
DEPTH = 1

SSM_HEADDIM = 64
SSM_HEADS = 16
SSM_INNER = SSM_HEADS * SSM_HEADDIM
SSM_GROUPS = 2
SSM_HPG = SSM_HEADS // SSM_GROUPS
SSM_STATE = 64
CONV_K = 4
CHUNK = 128
CONV_DIM = SSM_INNER + 2 * SSM_GROUPS * SSM_STATE

ATT_HEADS = 8
ATT_HEADDIM = 128
ATT_INNER = ATT_HEADS * ATT_HEADDIM
Q_BLOCK = 128

N_BRANCHES = 2
EPS = 1e-6

IN_SPLITS = (SSM_INNER, CONV_DIM, SSM_HEADS, ATT_INNER, ATT_INNER, ATT_INNER, ATT_INNER, ATT_HEADS, N_BRANCHES * D_MODEL)
IN_COLS = int(sum(IN_SPLITS))


def _rmsnorm(x, w):
    xf = x.astype(jnp.float32)
    y = xf * lax.rsqrt(jnp.mean(xf * xf, axis=-1, keepdims=True) + EPS)
    return (y * w.astype(jnp.float32)).astype(x.dtype)

def _causal_depthwise_conv(u, w, b):
    ch = u.shape[-1]
    out = lax.conv_general_dilated(
        u, w[:, None, :].astype(u.dtype), window_strides=(1,), padding=[(CONV_K - 1, 0)],
        dimension_numbers=("NWC", "WIO", "NWC"), feature_group_count=ch)
    return out + b.astype(u.dtype)

def _ssd_branch(z, xbc, dt_raw, conv_w, conv_b, dt_bias, a_log, d_skip, ssm_norm_w):
    bsz, s, _ = xbc.shape
    g, r, p, n = SSM_GROUPS, SSM_HPG, SSM_HEADDIM, SSM_STATE
    nc = s // CHUNK
    xbc = jax.nn.silu(_causal_depthwise_conv(xbc, conv_w, conv_b))
    xs, bm, cm = jnp.split(xbc, [SSM_INNER, SSM_INNER + g * n], axis=-1)
    xs = xs.reshape(bsz, s, g, r, p)
    dt = jax.nn.softplus(dt_raw.astype(jnp.float32) + dt_bias.astype(jnp.float32)).reshape(bsz, s, g, r)
    a = dt * (-jnp.exp(a_log.astype(jnp.float32))).reshape(g, r)
    xdt = xs.astype(jnp.float32) * dt[..., None]
    xc = xdt.reshape(bsz, nc, CHUNK, g, r, p)
    bc = bm.astype(jnp.float32).reshape(bsz, nc, CHUNK, g, n)
    cc = cm.astype(jnp.float32).reshape(bsz, nc, CHUNK, g, n)
    ac = a.reshape(bsz, nc, CHUNK, g, r).transpose(0, 3, 4, 1, 2)
    a_cs = jnp.cumsum(ac, axis=-1)
    tril = jnp.tril(jnp.ones((CHUNK, CHUNK), dtype=bool))
    seg = a_cs[..., :, None] - a_cs[..., None, :]
    lmat = jnp.exp(jnp.where(tril, seg, -jnp.inf))
    cb = jnp.einsum("bclgn,bcsgn->bgcls", cc, bc)
    y_diag = jnp.einsum("bgrcls,bcsgrp->bclgrp", cb[:, :, None] * lmat, xc)
    decay_states = jnp.exp(a_cs[..., -1:] - a_cs)
    states = jnp.einsum("bclgn,bgrcl,bclgrp->bcgrpn", bc, decay_states, xc)
    states = jnp.concatenate([jnp.zeros_like(states[:, :1]), states], axis=1)
    cs = jnp.cumsum(jnp.pad(a_cs[..., -1], ((0, 0), (0, 0), (0, 0), (1, 0))), axis=-1)
    tril_c = jnp.tril(jnp.ones((nc + 1, nc + 1), dtype=bool))
    decay_chunk = jnp.exp(jnp.where(tril_c, cs[..., :, None] - cs[..., None, :], -jnp.inf))
    new_states = jnp.einsum("bgrzc,bcgrpn->bzgrpn", decay_chunk, states)
    prev_states = new_states[:, :-1]
    y_off = jnp.einsum("bclgn,bcgrpn,bgrcl->bclgrp", cc, prev_states, jnp.exp(a_cs))
    y = (y_diag + y_off).reshape(bsz, s, g, r, p) + d_skip.astype(jnp.float32).reshape(g, r)[..., None] * xs.astype(jnp.float32)
    y = y.reshape(bsz, s, SSM_INNER).astype(z.dtype)
    return _rmsnorm(y * jax.nn.silu(z), ssm_norm_w)

def _fox_branch(q, k, v, z, f_logit, b_f):
    bsz, s, _ = q.shape
    nb = s // Q_BLOCK
    q = q.reshape(bsz, s, ATT_HEADS, ATT_HEADDIM).transpose(0, 2, 1, 3)
    k = k.reshape(bsz, s, ATT_HEADS, ATT_HEADDIM).transpose(0, 2, 1, 3)
    v = v.reshape(bsz, s, ATT_HEADS, ATT_HEADDIM).transpose(0, 2, 1, 3)
    log_f = jax.nn.log_sigmoid(f_logit.astype(jnp.float32) + b_f.astype(jnp.float32))
    f_cum = jnp.cumsum(log_f, axis=1).transpose(0, 2, 1)
    scale = ATT_HEADDIM ** -0.5
    qb = q.reshape(bsz, ATT_HEADS, nb, Q_BLOCK, ATT_HEADDIM).transpose(2, 0, 1, 3, 4)
    fq = f_cum.reshape(bsz, ATT_HEADS, nb, Q_BLOCK).transpose(2, 0, 1, 3)
    qpos = jnp.arange(s, dtype=jnp.int32).reshape(nb, Q_BLOCK)
    kpos = jnp.arange(s, dtype=jnp.int32)

    def one_block(args):
        qi, fi, pi = args
        logits = jnp.einsum("bhqd,bhkd->bhqk", qi, k).astype(jnp.float32) * scale
        logits = logits + fi[..., :, None] - f_cum[..., None, :]
        logits = jnp.where(pi[:, None] >= kpos[None, :], logits, -jnp.inf)
        probs = jax.nn.softmax(logits, axis=-1).astype(v.dtype)
        return jnp.einsum("bhqk,bhkd->bhqd", probs, v)

    o = lax.map(one_block, (qb, fq, qpos))
    o = o.transpose(1, 0, 3, 2, 4).reshape(bsz, s, ATT_INNER)
    return o * jax.nn.silu(z)

def first_inputs(seed: int = 0) -> dict:
    key = jax.random.key(seed)
    ks = jax.random.split(key, 20)
    d = D_MODEL
    x = jax.random.normal(ks[0], (BATCH, SEQ, d), jnp.float32)
    c = jax.random.normal(ks[1], (BATCH, d), jnp.float32)
    w_ada = jax.random.normal(ks[2], (d, 3 * d), jnp.float32) * d ** -0.5 * 0.5
    b_ada = jax.random.normal(ks[3], (3 * d,), jnp.float32) * 0.01
    norm_w = 1.0 + 0.05 * jax.random.normal(ks[4], (d,), jnp.float32)
    w_in = jax.random.normal(ks[5], (d, IN_COLS), jnp.float32) * d ** -0.5
    conv_w = jax.random.normal(ks[6], (CONV_K, CONV_DIM), jnp.float32) * 0.5
    conv_b = jax.random.normal(ks[7], (CONV_DIM,), jnp.float32) * 0.02
    dt0 = jnp.exp(jax.random.uniform(ks[8], (SSM_HEADS,), jnp.float32, np.log(1e-3), np.log(1e-1)))
    dt_bias = dt0 + jnp.log(-jnp.expm1(-dt0))
    a_log = jnp.log(jax.random.uniform(ks[9], (SSM_HEADS,), jnp.float32, 1.0, 16.0))
    d_skip = 1.0 + 0.1 * jax.random.normal(ks[10], (SSM_HEADS,), jnp.float32)
    ssm_norm_w = 1.0 + 0.05 * jax.random.normal(ks[11], (SSM_INNER,), jnp.float32)
    b_f = jnp.linspace(1.0, 6.0, ATT_HEADS, dtype=jnp.float32) + 0.1 * jax.random.normal(ks[12], (ATT_HEADS,), jnp.float32)
    b_gate = jax.random.normal(ks[13], (N_BRANCHES * d,), jnp.float32) * 0.01
    w_proj_ssm = jax.random.normal(ks[14], (SSM_INNER, d), jnp.float32) * SSM_INNER ** -0.5
    w_proj_att = jax.random.normal(ks[15], (ATT_INNER, d), jnp.float32) * ATT_INNER ** -0.5
    w_out = jax.random.normal(ks[16], (d, d), jnp.float32) * d ** -0.5
    final_norm_w = 1.0 + 0.05 * jax.random.normal(ks[17], (d,), jnp.float32)
    return {"x": x, "c": c, "w_ada": w_ada, "b_ada": b_ada, "norm_w": norm_w, "w_in": w_in,
            "conv_w": conv_w, "conv_b": conv_b, "dt_bias": dt_bias, "a_log": a_log, "d_skip": d_skip,
            "ssm_norm_w": ssm_norm_w, "b_f": b_f, "b_gate": b_gate, "w_proj_ssm": w_proj_ssm,
            "w_proj_att": w_proj_att, "w_out": w_out, "final_norm_w": final_norm_w}

def first_block(x, c, w_ada, b_ada, norm_w, w_in, conv_w, conv_b, dt_bias, a_log, d_skip,
              ssm_norm_w, b_f, b_gate, w_proj_ssm, w_proj_att, w_out, final_norm_w):
    ada = jax.nn.silu(c) @ w_ada + b_ada
    shift, scale, gate = jnp.split(ada, 3, axis=-1)
    offsets = [int(o) for o in np.cumsum(IN_SPLITS)[:-1]]
    for _ in range(DEPTH):
        h = _rmsnorm(x, norm_w) * (1.0 + scale[:, None, :]) + shift[:, None, :]
        proj = jnp.einsum("bsd,de->bse", h, w_in)
        z_ssm, xbc, dt_raw, q, k, v, z_att, f_logit, g_logit = jnp.split(proj, offsets, axis=-1)
        y_ssm = _ssd_branch(z_ssm, xbc, dt_raw, conv_w, conv_b, dt_bias, a_log, d_skip, ssm_norm_w)
        y_att = _fox_branch(q, k, v, z_att, f_logit, b_f)
        g_ssm, g_att = jnp.split(jax.nn.sigmoid(g_logit + b_gate), N_BRANCHES, axis=-1)
        merged = g_ssm * jnp.einsum("bse,ed->bsd", y_ssm, w_proj_ssm) + g_att * jnp.einsum("bse,ed->bsd", y_att, w_proj_att)
        x = x + gate[:, None, :] * jnp.einsum("bsd,de->bse", merged, w_out)
    return _rmsnorm(x, final_norm_w)


CHUNK_2 = 64
D_MIX = D_MODEL
HEAD_DIM = 64
ATT_WIDTH = 3 * D_MIX // 8
ATT_HEADS_2 = ATT_WIDTH // HEAD_DIM
ATT_PAST_CHUNKS = 8
ATT_BAND = (ATT_PAST_CHUNKS + 1) * CHUNK_2
REL_CLIP = 128
ML_WIDTH = 3 * D_MIX // 8
ML_HEADS = ML_WIDTH // HEAD_DIM
CONV_WIDTH = 4
GLA_WIDTH = D_MIX - ATT_WIDTH - ML_WIDTH
GLA_HEADS = 4
GLA_DV = GLA_WIDTH // GLA_HEADS
GLA_DK = GLA_DV // 2
GLA_KW = GLA_HEADS * GLA_DK
GLA_RANK = 16
GLA_TAU = 16.0
IN_SPLITS_2 = (ATT_WIDTH, ATT_WIDTH, ATT_WIDTH, ATT_WIDTH,
             ML_WIDTH, ML_WIDTH, ML_WIDTH, ML_WIDTH, ML_HEADS, ML_HEADS, ML_WIDTH,
             GLA_KW, GLA_KW, GLA_WIDTH, GLA_RANK, GLA_WIDTH)
D_IN = sum(IN_SPLITS_2)
NEG = -1e30


def rmsnorm(x, g):
    xf = x.astype(jnp.float32)
    y = xf * lax.rsqrt(jnp.mean(xf * xf, axis=-1, keepdims=True) + EPS)
    return (y * g.astype(jnp.float32)).astype(x.dtype)

def head_rmsnorm(x, g, n_heads):
    b, s, w = x.shape
    y = rmsnorm(x.reshape(b, s, n_heads, w // n_heads), g.reshape(n_heads, w // n_heads))
    return y.reshape(b, s, w)

def causal_conv(x, w):
    k_w = w.shape[0]
    s = x.shape[1]
    xp = jnp.pad(x, ((0, 0), (k_w - 1, 0), (0, 0)))
    return sum(xp[:, j:j + s] * w[j] for j in range(k_w))

def band_chunk_attention(q, k, v, rel_bias):
    bsz, s, h, d = q.shape
    nc = s // CHUNK_2
    pad = ATT_PAST_CHUNKS * CHUNK_2
    qc = q.reshape(bsz, nc, CHUNK_2, h, d)
    kp = jnp.pad(k, ((0, 0), (pad, 0), (0, 0), (0, 0))).reshape(bsz, nc + ATT_PAST_CHUNKS, CHUNK_2, h, d)
    vp = jnp.pad(v, ((0, 0), (pad, 0), (0, 0), (0, 0))).reshape(bsz, nc + ATT_PAST_CHUNKS, CHUNK_2, h, d)
    kb = jnp.concatenate([kp[:, m:m + nc] for m in range(ATT_PAST_CHUNKS + 1)], axis=2)
    vb = jnp.concatenate([vp[:, m:m + nc] for m in range(ATT_PAST_CHUNKS + 1)], axis=2)
    scores = jnp.einsum('bnqhd,bnkhd->bnhqk', qc, kb).astype(jnp.float32) * (d ** -0.5)
    rel = jnp.arange(CHUNK_2)[:, None] + pad - jnp.arange(ATT_BAND)[None, :]
    bias = rel_bias[:, jnp.clip(rel, -REL_CLIP, REL_CLIP) + REL_CLIP].astype(jnp.float32)
    kpos = (jnp.arange(nc)[:, None] - ATT_PAST_CHUNKS) * CHUNK_2 + jnp.arange(ATT_BAND)[None, :]
    valid = kpos >= 0
    scores = jnp.where(valid[None, :, None, None, :], scores + bias[None, None], NEG)
    p = jax.nn.softmax(scores, axis=-1).astype(v.dtype)
    o = jnp.einsum('bnhqk,bnkhd->bnqhd', p, vb)
    return o.reshape(bsz, s, h * d)

def mlstm_chunkwise(q, k, v, i_pre, f_pre):
    bsz, s, h, d = q.shape
    nc = s // CHUNK_2
    L = CHUNK_2
    dt = q.dtype
    qc = q.astype(jnp.float32).reshape(bsz, nc, L, h, d)
    kc = (k.astype(jnp.float32) * (d ** -0.5)).reshape(bsz, nc, L, h, d)
    vc = v.astype(jnp.float32).reshape(bsz, nc, L, h, d)
    ig = i_pre.astype(jnp.float32).reshape(bsz, nc, L, h).transpose(0, 1, 3, 2)
    lf = jax.nn.log_sigmoid(f_pre.astype(jnp.float32)).reshape(bsz, nc, L, h).transpose(0, 1, 3, 2)
    bcum = jnp.cumsum(lf, axis=-1)
    g = bcum[..., -1]
    a = g[..., None] - bcum + ig
    m_loc = jnp.max(a, axis=-1)
    w = jnp.exp(a - m_loc[..., None])
    c_loc = jnp.einsum('bnhj,bnjhv,bnjhk->bnhvk', w, vc, kc)
    n_loc = jnp.einsum('bnhj,bnjhk->bnhk', w, kc)

    def step(carry, xs):
        c_st, n_st, m_st = carry
        g_c, m_l, c_l, n_l = xs
        m_new = jnp.maximum(g_c + m_st, m_l)
        s_old = jnp.exp(g_c + m_st - m_new)
        s_new = jnp.exp(m_l - m_new)
        c_new = s_old[..., None, None] * c_st + s_new[..., None, None] * c_l
        n_new = s_old[..., None] * n_st + s_new[..., None] * n_l
        return (c_new, n_new, m_new), (c_st, n_st, m_st)

    init = (jnp.zeros((bsz, h, d, d), jnp.float32), jnp.zeros((bsz, h, d), jnp.float32),
            jnp.zeros((bsz, h), jnp.float32))
    xs = (jnp.moveaxis(g, 1, 0), jnp.moveaxis(m_loc, 1, 0), jnp.moveaxis(c_loc, 1, 0), jnp.moveaxis(n_loc, 1, 0))
    _, (c_prev, n_prev, m_prev) = lax.scan(step, init, xs)
    c_prev = jnp.moveaxis(c_prev, 0, 1)
    n_prev = jnp.moveaxis(n_prev, 0, 1)
    m_prev = jnp.moveaxis(m_prev, 0, 1)

    causal = jnp.tril(jnp.ones((L, L), dtype=bool))
    log_d = jnp.where(causal, bcum[..., :, None] - bcum[..., None, :] + ig[..., None, :], NEG)
    inter_log = bcum + m_prev[..., None]
    m_row = jnp.maximum(inter_log, jnp.max(log_d, axis=-1))
    d_mat = jnp.exp(log_d - m_row[..., None])
    inter_w = jnp.exp(inter_log - m_row)
    sc = jnp.einsum('bnthd,bnjhd->bnhtj', qc, kc) * d_mat
    num = jnp.einsum('bnhtj,bnjhv->bnthv', sc, vc) + \
        inter_w.transpose(0, 1, 3, 2)[..., None] * jnp.einsum('bnhvk,bnthk->bnthv', c_prev, qc)
    den = jnp.sum(sc, axis=-1) + inter_w * jnp.einsum('bnhk,bnthk->bnht', n_prev, qc)
    den = jnp.maximum(jnp.abs(den), jnp.exp(-m_row))
    out = num / den.transpose(0, 1, 3, 2)[..., None]
    return out.reshape(bsz, s, h * d).astype(dt)

def gla_chunkwise(q, k, v, log_alpha):
    bsz, s, h, dk = q.shape
    dv = v.shape[-1]
    nc = s // CHUNK_2
    L = CHUNK_2
    dt = q.dtype

    def to_chunks(t):
        return jnp.moveaxis(t.astype(jnp.float32).reshape(bsz, nc, L, h, t.shape[-1]), 1, 0)

    xs = (to_chunks(q * (dk ** -0.5)), to_chunks(k), to_chunks(v), to_chunks(log_alpha))
    causal = jnp.tril(jnp.ones((L, L), dtype=bool))

    def step(state, chunk):
        qx, kx, vx, la = chunk
        bcum = jnp.cumsum(la, axis=1)
        diff = bcum[:, :, None] - bcum[:, None, :]
        decay = jnp.where(causal[None, :, :, None, None], jnp.exp(jnp.minimum(diff, 0.0)), 0.0)
        att = jnp.einsum('bthd,bjhd,btjhd->bhtj', qx, kx, decay)
        o_intra = jnp.einsum('bhtj,bjhv->bthv', att, vx)
        o_inter = jnp.einsum('bthd,bhdv->bthv', qx * jnp.exp(bcum), state)
        btot = bcum[:, -1]
        k_dec = kx * jnp.exp(btot[:, None] - bcum)
        state_new = jnp.exp(btot)[..., None] * state + jnp.einsum('bjhd,bjhv->bhdv', k_dec, vx)
        return state_new, o_intra + o_inter

    _, o = lax.scan(step, jnp.zeros((bsz, h, dk, dv), jnp.float32), xs)
    return jnp.moveaxis(o, 0, 1).reshape(bsz, s, h * dv).astype(dt)

def hybrid_layer(x, norm_g, w_in, b_gates, conv_w, w_alpha, b_alpha, rel_bias, ml_norm_g, gla_norm_g, w_out):
    bsz, s, _ = x.shape
    hn = rmsnorm(x, norm_g)
    z = jnp.einsum('bsd,de->bse', hn, w_in)
    split_idx = [int(i) for i in np.cumsum(IN_SPLITS_2)[:-1]]
    (aq, ak, av, ag, mq, mk, mv, mo, mi, mf, mg, gq, gk, gv, ga, gg) = jnp.split(z, split_idx, axis=-1)

    att = band_chunk_attention(aq.reshape(bsz, s, ATT_HEADS_2, HEAD_DIM), ak.reshape(bsz, s, ATT_HEADS_2, HEAD_DIM),
                               av.reshape(bsz, s, ATT_HEADS_2, HEAD_DIM), rel_bias)
    y_a = att * jax.nn.silu(ag)

    qk = jax.nn.silu(causal_conv(jnp.concatenate([mq, mk], axis=-1), conv_w))
    mq_c, mk_c = qk[..., :ML_WIDTH], qk[..., ML_WIDTH:]
    h_ml = mlstm_chunkwise(mq_c.reshape(bsz, s, ML_HEADS, HEAD_DIM), mk_c.reshape(bsz, s, ML_HEADS, HEAD_DIM),
                           mv.reshape(bsz, s, ML_HEADS, HEAD_DIM),
                           mi + b_gates[:ML_HEADS], mf + b_gates[ML_HEADS:])
    y_b = jax.nn.sigmoid(mo) * head_rmsnorm(h_ml, ml_norm_g, ML_HEADS) * jax.nn.silu(mg)

    log_alpha = jax.nn.log_sigmoid((jnp.einsum('bsr,rk->bsk', ga, w_alpha) + b_alpha).astype(jnp.float32)) / GLA_TAU
    h_gla = gla_chunkwise(gq.reshape(bsz, s, GLA_HEADS, GLA_DK), gk.reshape(bsz, s, GLA_HEADS, GLA_DK),
                          gv.reshape(bsz, s, GLA_HEADS, GLA_DV), log_alpha.reshape(bsz, s, GLA_HEADS, GLA_DK))
    y_c = head_rmsnorm(h_gla, gla_norm_g, GLA_HEADS) * jax.nn.silu(gg)

    y = jnp.concatenate([y_a, y_b, y_c], axis=-1)
    return x + jnp.einsum('bse,ed->bsd', y, w_out)

def second_inputs(seed: int = 0) -> dict:
    key = jax.random.key(seed)
    ks = jax.random.split(key, 12)
    f32 = jnp.float32
    x = jax.random.normal(ks[0], (BATCH, SEQ, D_MODEL), f32)
    norm_g = 1.0 + 0.1 * jax.random.normal(ks[1], (DEPTH, D_MODEL), f32)
    w_in = jax.random.normal(ks[2], (DEPTH, D_MODEL, D_IN), f32) * D_MODEL ** -0.5
    f_bias = jnp.broadcast_to(jnp.linspace(3.0, 6.0, ML_HEADS, dtype=f32), (DEPTH, ML_HEADS))
    i_bias = 0.1 * jax.random.normal(ks[3], (DEPTH, ML_HEADS), f32)
    b_gates = jnp.concatenate([i_bias, f_bias + 0.1 * jax.random.normal(ks[4], (DEPTH, ML_HEADS), f32)], axis=-1)
    conv_w = jax.random.normal(ks[5], (DEPTH, CONV_WIDTH, 2 * ML_WIDTH), f32) * CONV_WIDTH ** -0.5
    w_alpha = jax.random.normal(ks[6], (DEPTH, GLA_RANK, GLA_KW), f32) * GLA_RANK ** -0.5
    b_alpha = 0.1 * jax.random.normal(ks[7], (DEPTH, GLA_KW), f32)
    rel_bias = 0.1 * jax.random.normal(ks[8], (DEPTH, ATT_HEADS_2, 2 * REL_CLIP + 1), f32)
    ml_norm_g = 1.0 + 0.1 * jax.random.normal(ks[9], (DEPTH, ML_WIDTH), f32)
    gla_norm_g = 1.0 + 0.1 * jax.random.normal(ks[10], (DEPTH, GLA_WIDTH), f32)
    k_out, k_fin = jax.random.split(ks[11])
    w_out = jax.random.normal(k_out, (DEPTH, D_MIX, D_MODEL), f32) * D_MIX ** -0.5
    final_g = 1.0 + 0.1 * jax.random.normal(k_fin, (D_MODEL,), f32)
    return {"x": x, "norm_g": norm_g, "w_in": w_in, "b_gates": b_gates, "conv_w": conv_w,
            "w_alpha": w_alpha, "b_alpha": b_alpha, "rel_bias": rel_bias, "ml_norm_g": ml_norm_g,
            "gla_norm_g": gla_norm_g, "w_out": w_out, "final_g": final_g}

def second_block(x, norm_g, w_in, b_gates, conv_w, w_alpha, b_alpha, rel_bias, ml_norm_g, gla_norm_g, w_out, final_g):
    for l in range(DEPTH):
        x = hybrid_layer(x, norm_g[l], w_in[l], b_gates[l], conv_w[l], w_alpha[l], b_alpha[l], rel_bias[l],
                         ml_norm_g[l], gla_norm_g[l], w_out[l])
    return rmsnorm(x, final_g)


def setup_inputs(seed=0):
    out = dict(first_inputs(seed))
    for name, value in second_inputs(seed + 1).items():
        if name != "x":
            out[name + "_2"] = value
    return out


def reference(
    x, c, w_ada, b_ada, norm_w, w_in, conv_w, conv_b, dt_bias, a_log, d_skip, ssm_norm_w, b_f,
    b_gate, w_proj_ssm, w_proj_att, w_out, final_norm_w, norm_g_2, w_in_2, b_gates_2, conv_w_2,
    w_alpha_2, b_alpha_2, rel_bias_2, ml_norm_g_2, gla_norm_g_2, w_out_2, final_g_2,
):
    x = first_block(
        x, c, w_ada, b_ada, norm_w, w_in, conv_w, conv_b, dt_bias, a_log, d_skip, ssm_norm_w,
        b_f, b_gate, w_proj_ssm, w_proj_att, w_out, final_norm_w,
    )
    return second_block(
        x, norm_g_2, w_in_2, b_gates_2, conv_w_2, w_alpha_2, b_alpha_2, rel_bias_2, ml_norm_g_2,
        gla_norm_g_2, w_out_2, final_g_2,
    )


_drawn_inputs = setup_inputs


def setup_inputs(seed=0):
    import zlib

    import numpy as np

    out = dict(_drawn_inputs(seed))
    spreads = {}
    factors = {'b_ada': 6.868,
     'norm_w': 3.819,
     'conv_b': 8.0,
     'd_skip': 129.427,
     'ssm_norm_w': 5.922,
     'b_gate': 21.34,
     'b_alpha_2': 4.986,
     'rel_bias_2': 8.0,
     'ml_norm_g_2': 3.247}
    for name, (base, spread) in spreads.items():
        noise = np.random.default_rng([zlib.crc32(name.encode()), seed]).standard_normal(out[name].shape)
        drawn = base * np.exp(spread * noise) if base else spread * noise
        out[name] = __import__('jax').numpy.asarray(drawn.astype(out[name].dtype))
    for name, factor in factors.items():
        out[name] = (out[name] * factor).astype(out[name].dtype)
    return out
```

```python
from contextlib import ExitStack

import concourse.bass as bass
from concourse import mybir

F32 = mybir.dt.float32
F32R = mybir.dt.float32r
ALU = mybir.AluOpType
ACT = mybir.ActivationFunctionType
AX = mybir.AxisListType

P = 128
T = 1024
D = 1024
KT = D // P
NT = T // P
HALF = 512
EPS = 1e-6
MASKED = -1e30

SSM_HEADS, SSM_P, SSM_N, SSM_G = 16, 64, 64, 2
HPG = SSM_HEADS // SSM_G
CHUNK = 128
NCHUNK = T // CHUNK
CONV_K = 4
XBC_TILES = (SSM_HEADS * SSM_P + 2 * SSM_G * SSM_N) // P
FOX_HEADS, FOX_D = 8, 128
Z_OFF = 0
XBC_OFF = D
DT_OFF = XBC_OFF + XBC_TILES * P
Q_OFF = DT_OFF + SSM_HEADS
K_OFF, V_OFF, ZA_OFF = Q_OFF + D, Q_OFF + 2 * D, Q_OFF + 3 * D
F_OFF = Q_OFF + 4 * D
G_OFF = F_OFF + FOX_HEADS

PAIRS = 3
HD = 64
W2 = PAIRS * P
AQ, AK, AV, AG = 0, W2, 2 * W2, 3 * W2
MQ, MK, MV, MO = 4 * W2, 5 * W2, 6 * W2, 7 * W2
ML_HEADS = 6
MI, MF = 8 * W2, 8 * W2 + ML_HEADS
MG = MF + ML_HEADS
GLA_HEADS, GLA_DK, GLA_DV, GLA_RANK = 4, 32, 64, 16
GQ = MG + W2
GK, GV = GQ + P, GQ + 2 * P
GA = GV + 2 * P
GG = GA + GLA_RANK
GLA_TAU = 16.0
SUB = 16
NSUB = CHUNK // SUB
KEY_CAP = 1e30
BAND_TILES = 5
BANDW = BAND_TILES * P
REL = 128

VEC1 = {}
VEC2 = {}


def _count(table, sizes):
    at = 0
    for name, rows in sizes:
        table[name] = (at, at + rows)
        at += rows
    return at


NVEC1 = _count(VEC1, [("b_ada", 24), ("norm_w", 8), ("conv_w", CONV_K * XBC_TILES), ("conv_b", XBC_TILES),
                      ("ssm_norm_w", 8), ("b_gate", 16), ("final_norm_w", 8), ("c", 8)])
NVEC2 = _count(VEC2, [("norm_g_2", 8), ("conv_w_2", CONV_K * 2 * PAIRS), ("b_alpha_2", 1), ("final_g_2", 8),
                      ("ml_norm_g_2", PAIRS), ("gla_norm_g_2", 2)])

N_SMALL1 = 0
N_XBC = 1
N_Z = N_XBC + XBC_TILES
N_MIX1 = N_Z + 8
N_FOX = N_MIX1 + 16
N_MIX2 = N_FOX + 4 * FOX_HEADS
N_OUT1 = N_MIX2 + 16
N_SMALL2 = N_OUT1 + 8
N_BAND = N_SMALL2 + 1
N_ML = N_BAND + 4 * PAIRS
N_MG = N_ML + 4 * PAIRS
N_GLA = N_MG + PAIRS
N_GG = N_GLA + 4
N_OUT2 = N_GG + 2
N_TILES = N_OUT2 + 8


def build(nc, io, out):
    ctx = ExitStack()
    with ctx:
        def psum(name, shape):
            return ctx.enter_context(nc.psum_tensor(name, shape, F32))

        def sem(name):
            return ctx.enter_context(nc.semaphore(name))

        def scratch(name, shape):
            return nc.dram_tensor(name, shape, F32, kind="Internal").ap()

        base = (nc.sbuf_base + 63) // 64 * 64
        big = KT * T * 4
        at_ha, at_ya = base, base + 2 * big
        at_ring = at_ya + 2 * big
        tile_bytes = KT * P * 4
        at_const = at_ring + 6 * tile_bytes
        at_arena = at_const + 5248
        arena_end = nc.sbuf_usable_end

        class Region:

            def __init__(self, at, end):
                self.at, self.end = at, end

            def __call__(self, name, shape, dt=F32):
                size = 4
                for s in shape[1:]:
                    size *= s
                t = nc.alloc_sbuf_tensor_at(name, shape, dt, offset=self.at)
                self.at += (size + 31) // 32 * 32
                assert self.at <= self.end, (name, self.at, self.end)
                return t

        def arena():
            return Region(at_arena, arena_end)

        def ya_region():
            return Region(at_ya, at_ya + 2 * big)

        ha = Region(at_ha, at_ya)
        ha_hi = ha("ha_hi", [P, KT, T], F32R)
        ha_lo = ha("ha_lo", [P, KT, T], F32R)
        ya = ya_region()
        ya_hi = ya("ya_hi", [P, KT, T], F32R)
        ya_lo = ya("ya_lo", [P, KT, T], F32R)
        rg = Region(at_ring, at_const)
        w_raw = rg("w_raw", [P, 2, KT, P])
        w_hi = rg("w_hi", [P, 2, KT, P], F32R)
        w_lo = rg("w_lo", [P, 2, KT, P], F32R)

        cst = Region(at_const, at_arena)
        ident = cst("ident", [P, P])
        ones = cst("ones", [P, P])
        causal01 = cst("causal01", [P, P])
        vec1 = cst("vec1", [P, NVEC1])
        vec2 = cst("vec2", [P, NVEC2])
        ada = cst("ada", [P, 24])
        a1 = cst("a1", [P, 8])
        silu_c = cst("silu_c", [P, 8])
        dskip = cst("dskip", [P, 8])
        zero_col = cst("zero_col", [P, 1])
        eps_col = cst("eps_col", [P, 1])
        sp_bias = cst("sp_bias", [64, 1])
        sp_sign = cst("sp_sign", [64, 1])
        neg_a = cst("neg_a", [SSM_HEADS, 1])
        gate_bias2 = cst("gate_bias2", [64, 1])
        w_alpha = cst("w_alpha", [P, P])

        def col1(name, i=0):
            return vec1[:, VEC1[name][0] + i:VEC1[name][0] + i + 1]

        def row(x, i):
            return x[:, bass.ds(i, 1), :].rearrange("p a t -> p (a t)")

        def dcol(vec, table, name, i):
            return vec[:, table[name][0]:table[name][1]][:, bass.ds(i, 1)]

        acc = psum("acc", [P, 2, 2 * HALF])
        work = psum("work", [P, 4, HALF])
        accf = acc[:, :, :].rearrange("p a b -> p (a b)")

        xt_scr = scratch("xt_scr", [P, KT, T])
        merged_scr = scratch("merged_scr", [P, KT, T])
        acs_scr = scratch("acs_scr", [SSM_HEADS, T])
        fcum_scr = scratch("fcum_scr", [FOX_HEADS, T])
        ml_a_scr = scratch("ml_a_scr", [8, T])
        skew_scr = scratch("skew_scr", [P * 3 * P])
        bias_scr = scratch("bias_scr", [ML_HEADS, P, BANDW])

        w_loaded = [sem("w_loaded0"), sem("w_loaded1")]
        w_part = sem("w_part")
        hi_done = sem("hi_done")
        lo_done = sem("lo_done")
        mm_done = sem("mm_done")
        acc_free = [sem("acc_free0"), sem("acc_free1")]
        stage_done = sem("stage_done")

        def end_stage(eng, i):
            eng.drain().then_inc(stage_done, 1)

        def begin_stage(eng, i):
            eng.wait_ge(stage_done, 4 * i)

        ticks = {}

        def wait_here(eng, s, value):
            eng.wait_ge(s, value)
            if eng not in ticks:
                ticks[eng] = sem(f"tick{len(ticks)}")
            eng.sem_inc(ticks[eng], 1)

        def load_w(sp, n, src, adv=0):
            if n >= 2:
                wait_here(sp, lo_done, n - 1 + 2 * adv)
            sp.dma_start(w_raw[:, n % 2, :, :], src).then_inc(w_loaded[n % 2], 16)

        def split_hi(act, n, adv=0):
            act.wait_ge(w_loaded[n % 2], 16 * (n // 2 + 1) + 16 * adv)
            if n >= 2:
                act.wait_ge(mm_done, n - 1 + 2 * adv)
            act.activation(w_hi[:, n % 2, :, :], w_raw[:, n % 2, :, :], ACT.Copy).then_inc(hi_done, 1)

        def split_lo(dve, n, adv=0):
            dve.wait_ge(hi_done, n + 1 + 2 * adv)
            dve.tensor_tensor(w_lo[:, n % 2, :, :], w_raw[:, n % 2, :, :],
                              w_hi[:, n % 2, :, :].bitcast(F32), ALU.subtract).then_inc(lo_done, 1)

        def project(pe, n, x_hi, x_lo, adv=0):
            pe.wait_ge(lo_done, n + 1 + 2 * adv)
            if n >= 2:
                pe.wait_ge(acc_free[n % 2], n // 2 + adv)
            for k in range(KT):
                passes = [(w_hi, x_hi), (w_hi, x_lo), (w_lo, x_hi)]
                for i, (w, x) in enumerate(passes):
                    for h in range(2):
                        mm = pe.matmul(acc[:, n % 2, h * HALF:(h + 1) * HALF], w[:, n % 2, k, :],
                                       x[:, k, h * HALF:(h + 1) * HALF],
                                       start=(k == 0 and i == 0), stop=(k == KT - 1 and i == 2))
            mm.then_inc(mm_done, 1)

        def projected(eng, n, adv=0):
            eng.wait_ge(mm_done, n + 1 + 2 * adv)

        def cols(w, off, width=P):
            return w.rearrange("(k p) c -> p k c", p=P)[:, :, bass.ds(off, width)]

        w_in, w_in2 = io["w_in"], io["w_in_2"]

        class Norm:
            squared = sem("norm_squared")
            summed = sem("norm_summed")
            rooted = sem("norm_rooted")

            def __init__(self, use):
                self.use = use
                self.tiles = use * KT

            def act(self, act, x, sq, root):
                for f in range(KT):
                    if f >= 2:
                        act.wait_ge(self.summed, self.tiles + f - 1)
                    act.activation(sq[:, f % 2, :], x[:, f, :], ACT.Square).then_inc(self.squared, 1)
                self.act_root(act, root)

            def act_root(self, act, root):
                act.wait_ge(self.summed, self.tiles + KT)
                act.activation(root[:, :], work[:, 0:2, :], ACT.Sqrt,
                               bias=eps_col[:, :], scale=1.0 / D).then_inc(self.rooted, 1)

            def pe(self, pe, sq_of):
                for f in range(KT):
                    pe.wait_ge(self.squared, self.tiles + f + 1)
                    for h in range(2):
                        mm = pe.matmul(work[:, h, :], ones[:, :], sq_of(f)[:, h * HALF:(h + 1) * HALF],
                                       start=(f == 0), stop=(f == KT - 1))
                    mm.then_inc(self.summed, 1)

            def dve(self, dve, root, rstd):
                dve.wait_ge(self.rooted, self.use + 1)
                dve.reciprocal(rstd[:, :], root[:, :])

        class Softplus:
            ready = sem("softplus_u_ready")
            exped = sem("softplus_exped")

            def __init__(self, use):
                self.use = use

            def act(self, act, u, e, relu):
                act.wait_ge(self.ready, self.use + 1)
                act.activation(e, u, ACT.Abs)
                act.activation(relu, u, ACT.Relu)
                act.drain()
                act.activation(e, e, ACT.Exp, scale=-1.0).then_inc(self.exped, 1)

            def dve(self, dve, e, relu, s, s2, p, result):
                dve.wait_ge(self.exped, self.use + 1)
                dve.tensor_scalar(s, e, 2.0, None, ALU.add)
                dve.drain()
                dve.reciprocal(s2, s)
                dve.drain()
                dve.tensor_tensor(s, e, s2, ALU.mult)
                dve.drain()
                dve.tensor_tensor(s2, s, s, ALU.mult)
                dve.drain()
                dve.tensor_scalar(p, s2, 1.0 / 15, None, ALU.mult)
                for c in (13, 11, 9, 7, 5, 3):
                    dve.drain()
                    dve.scalar_tensor_tensor(p, p, 1.0 / c, s2, ALU.add, ALU.mult)
                dve.drain()
                dve.scalar_tensor_tensor(p, p, 1.0, s, ALU.add, ALU.mult)
                dve.drain()
                dve.scalar_tensor_tensor(result, p, 2.0, relu, ALU.mult, ALU.add)

        ar = arena()
        x_tok = ar("x_tok", [P, NT, D])
        sq0 = ar("sq0", [P, 2, T])
        rstd0 = ar("rstd0", [P, T])
        v0 = ar("v0", [P, 1, T])
        root0 = Region(at_arena, arena_end)("root0", [P, T])
        v0b = Region(at_arena + 4096, arena_end)("v0b", [P, 2, T])
        xt = Region(at_ya, at_ya + big)("xt", [P, KT, T])
        w_ada = Region(at_ha, at_ha + 3 * big + big)("w_ada_lo", [P, 5, 3 * D])
        w_ada_b = Region(at_ya + big, at_ya + 2 * big)("w_ada_hi", [P, 2, 3 * D])
        w_ada_c = Region(at_arena, arena_end)("w_ada_last", [P, 1, 3 * D])
        rows1 = Region(at_ya + big + 24576, at_ya + 2 * big)("rows1", [P, P])
        rows2 = Region(at_ya + big + 25088, at_ya + 2 * big)("rows2", [P, P])

        x_loaded = [sem(f"x_loaded{i}") for i in range(4)]
        vec_loaded, col_loaded, ada_loaded = sem("vec_loaded"), sem("col_loaded"), sem("ada_loaded")
        ada_last = sem("ada_last")
        consts = sem("consts")
        zeroed = sem("zeroed")
        vec_turned, vec_ready = sem("vec_turned"), sem("vec_ready")
        xt_turned = sem("xt_turned")
        xt_act, xt_dve = sem("xt_act"), sem("xt_dve")
        silu_c_done, ada_mul = sem("silu_c_done"), sem("ada_mul")
        xt_saved = sem("xt_saved")
        norm0 = Norm(0)
        v0_scaled, v0_shifted, h_hi = sem("v0_scaled"), sem("v0_shifted"), sem("h_hi")
        lo0_done = sem("lo0_done")

        def vec_sources():
            v1 = [("b_ada", io["b_ada"]), ("norm_w", io["norm_w"]),
                  ("conv_w", io["conv_w"].rearrange("j c -> (j c)")), ("conv_b", io["conv_b"]),
                  ("ssm_norm_w", io["ssm_norm_w"]), ("b_gate", io["b_gate"]),
                  ("final_norm_w", io["final_norm_w"]), ("c", io["c"].rearrange("a d -> (a d)"))]
            v2 = [("norm_g_2", io["norm_g_2"].rearrange("a d -> (a d)")),
                  ("conv_w_2", io["conv_w_2"].rearrange("a j c -> (a j c)")),
                  ("b_alpha_2", io["b_alpha_2"].rearrange("a d -> (a d)")), ("final_g_2", io["final_g_2"]),
                  ("ml_norm_g_2", io["ml_norm_g_2"].rearrange("a d -> (a d)")),
                  ("gla_norm_g_2", io["gla_norm_g_2"].rearrange("a d -> (a d)"))]
            for rows, table, vs in ((rows1, VEC1, v1), (rows2, VEC2, v2)):
                for name, src in vs:
                    a, b = table[name]
                    yield rows[a:b, :], src.rearrange("(r p) -> r p", p=P)

        VECS = len(VEC1) + len(VEC2)

        def sp_0(sp):
            x = io["x"].rearrange("a (t p) d -> p (a t) d", p=P)
            for i in range(NT):
                sp.dma_start(x_tok[:, i, :], x[:, i, :]).then_inc(x_loaded[i // 2], 16)
            wa = io["w_ada"].rearrange("(k p) c -> p k c", p=P)
            for k in range(5):
                sp.dma_start(w_ada[:, k, :], wa[:, k, :]).then_inc(ada_loaded, 16)
            for k in range(2):
                sp.dma_start(w_ada_b[:, k, :], wa[:, 5 + k, :]).then_inc(ada_loaded, 16)
            sp.wait_ge(xt_turned, 2 * NT)
            sp.dma_start(w_ada_c[:, 0, :], wa[:, 7, :]).then_inc(ada_last, 16)
            sp.dma_start(w_raw[:, 0, :, 0:32], cols(w_in, DT_OFF, 32)).then_inc(w_loaded[0], 16)
            sp.dma_start(w_raw[:, 0, :, 32:P], cols(w_in, F_OFF, P - 32)).then_inc(w_part, 16)
            load_w(sp, N_XBC, cols(w_in, XBC_OFF))
            sp.wait_ge(xt_act, NT)
            sp.wait_ge(xt_dve, NT)
            sp.dma_start(xt_scr, xt[:, :, :]).then_inc(xt_saved, 16)

        def act_0(act):
            for dst, src in vec_sources():
                act.dma_start(dst, src).then_inc(vec_loaded, 16)
            act.wait_ge(zeroed, 1)
            act.dma_start(sp_bias[0:SSM_HEADS, :], io["dt_bias"].rearrange("(h a) -> h a", a=1)).then_inc(col_loaded, 16)
            act.dma_start(sp_bias[32:32 + FOX_HEADS, :], io["b_f"].rearrange("(h a) -> h a", a=1)).then_inc(col_loaded, 16)
            act.dma_start(neg_a[:, :], io["a_log"].rearrange("(h a) -> h a", a=1)).then_inc(col_loaded, 16)
            bg = io["b_gates_2"].rearrange("a (h b) -> (a h) b", b=1)
            act.dma_start(gate_bias2[0:ML_HEADS, :], bg[0:ML_HEADS, :]).then_inc(col_loaded, 16)
            act.dma_start(gate_bias2[32:32 + ML_HEADS, :], bg[ML_HEADS:2 * ML_HEADS, :]).then_inc(col_loaded, 16)
            act.dma_start(w_alpha[64:64 + GLA_RANK, :], io["w_alpha_2"].rearrange("a r k -> (a r) k")).then_inc(col_loaded, 16)
            for w in range(2):
                ds = io["d_skip"].rearrange("(t w) -> w t", w=2)[w, :]
                act.dma_start(dskip[64 * w:64 * w + 64, :], ds.partition_broadcast(64),
                              allow_slow_non_contiguous=True).then_inc(col_loaded, 16)
            act.wait_ge(vec_turned, 1)
            act.activation(vec1[:, :], work[:, 0, 0:NVEC1], ACT.Copy)
            act.activation(vec2[:, :], work[:, 1, 0:NVEC2], ACT.Copy).then_inc(vec_ready, 1)
            act.drain()
            act.activation(silu_c[:, :], vec1[:, VEC1["c"][0]:VEC1["c"][1]], ACT.Silu).then_inc(silu_c_done, 1)
            act.wait_ge(col_loaded, 16 * 8)
            act.activation(neg_a[:, :], neg_a[:, :], ACT.Exp)
            act.drain()
            act.activation(neg_a[:, :], neg_a[:, :], ACT.Copy, scale=-1.0)
            for i in range(NT):
                act.wait_ge(xt_turned, 2 * i + 1)
                act.activation(xt[:, 0:4, i * P:(i + 1) * P], acc[:, i % 2, 0:HALF], ACT.Copy).then_inc(xt_act, 1)
            act.drain()
            act.wait_ge(xt_dve, NT)
            norm0.act(act, xt, sq0, root0)
            act.wait_ge(w_part, 16)
            split_hi(act, 0)
            for f in range(KT):
                act.wait_ge(v0_scaled, f + 1)
                if f >= 2:
                    act.wait_ge(lo0_done, f - 1)
                act.activation(v0b[:, f % 2, :], v0[:, 0, :], ACT.Identity, bias=ada[:, f:f + 1]).then_inc(v0_shifted, 1)
                act.drain()
                act.activation(ha_hi[:, f, :], v0b[:, f % 2, :], ACT.Copy).then_inc(h_hi, 1)
            end_stage(act, 0)

        def pe_0(pe):
            pe.wait_ge(consts, 1)
            pe.wait_ge(vec_loaded, 16 * VECS)
            pe.transpose(work[:, 0, 0:NVEC1], rows1[0:NVEC1, :], ident[0:NVEC1, 0:NVEC1])
            pe.transpose(work[:, 1, 0:NVEC2], rows2[0:NVEC2, :], ident[0:NVEC2, 0:NVEC2]).then_inc(vec_turned, 1)
            for i in range(NT):
                if i % 2 == 0:
                    pe.wait_ge(x_loaded[i // 2], 32)
                for g in range(2):
                    if i >= 2:
                        pe.wait_ge(xt_dve if g else xt_act, i - 1)
                    for f in range(4):
                        mm = pe.transpose(acc[:, i % 2, g * HALF + f * P:g * HALF + (f + 1) * P],
                                          x_tok[:, i, (4 * g + f) * P:(4 * g + f + 1) * P], ident[:, :])
                    mm.then_inc(xt_turned, 1)
            pe.wait_ge(ada_loaded, 16 * 7)
            pe.wait_ge(ada_last, 16)
            pe.wait_ge(silu_c_done, 1)
            for m in range(24):
                for k in range(KT):
                    w = w_ada[:, k, :] if k < 5 else w_ada_b[:, k - 5, :] if k < 7 else w_ada_c[:, 0, :]
                    mm = pe.matmul(work[:, 2, m:m + 1], w[:, m * P:(m + 1) * P], silu_c[:, k:k + 1],
                                   start=(k == 0), stop=(k == KT - 1))
            mm.then_inc(ada_mul, 1)
            pe.wait_ge(vec_ready, 1)
            norm0.pe(pe, lambda f: sq0[:, f % 2, :])
            end_stage(pe, 0)

        def dve_0(dve):
            for i in range(NT):
                dve.wait_ge(xt_turned, 2 * i + 2)
                dve.tensor_copy(xt[:, 4:8, i * P:(i + 1) * P],
                                acc[:, i % 2, HALF:2 * HALF].rearrange("p (f t) -> p f t", f=4)).then_inc(xt_dve, 1)
            dve.wait_ge(ada_mul, 1)
            dve.wait_ge(vec_ready, 1)
            dve.tensor_tensor(ada[:, :], work[:, 2, 0:24], vec1[:, VEC1["b_ada"][0]:VEC1["b_ada"][1]], ALU.add)
            dve.drain()
            dve.scalar_tensor_tensor(a1[:, :], ada[:, 8:16], 1.0, vec1[:, VEC1["norm_w"][0]:VEC1["norm_w"][1]],
                                     ALU.add, ALU.mult)
            norm0.dve(dve, root0, rstd0)
            dve.drain()
            dve.wait_ge(xt_act, NT)
            split_lo(dve, 0)
            for f in range(KT):
                if f >= 1:
                    dve.wait_ge(v0_shifted, f)
                dve.scalar_tensor_tensor(v0[:, 0, :], xt[:, f, :], a1[:, f:f + 1], rstd0[:, :],
                                         ALU.mult, ALU.mult).then_inc(v0_scaled, 1)
                dve.wait_ge(h_hi, f + 1)
                dve.tensor_tensor(ha_lo[:, f, :], v0b[:, f % 2, :], ha_hi[:, f, :].bitcast(F32),
                                  ALU.subtract).then_inc(lo0_done, 1)
            end_stage(dve, 0)

        def pool_0(pool):
            pool.memset(sp_bias[:, :], 0.0)
            pool.memset(gate_bias2[:, :], 0.0).then_inc(zeroed, 1)
            pool.memset(ident[:, :], 0.0)
            pool.memset(ones[:, :], 1.0)
            pool.memset(causal01[:, :], 1.0)
            pool.memset(zero_col[:, :], 0.0)
            pool.memset(eps_col[:, :], EPS)
            pool.memset(sp_sign[:, :], -1.0)
            pool.drain()
            pool.memset(sp_sign[0:32, :], 1.0)
            pool.affine_select(out=ident[:, :], in_=ident[:, :], compare_op=ALU.not_equal, fill=1.0,
                               base=0, pattern=[[-1, P]], channel_multiplier=1)
            pool.affine_select(out=causal01[:, :], in_=causal01[:, :], compare_op=ALU.is_ge, fill=0.0,
                               base=0, pattern=[[1, P]], channel_multiplier=-1)
            pool.drain().then_inc(consts, 1)
            end_stage(pool, 0)

        ar = arena()
        xbc = ar("xbc", [P, XBC_TILES, T])
        spt = ar("spt", [64, T])
        acs = ar("acs", [SSM_HEADS, T])
        ya = ya_region()
        sp1 = {k: ya(f"sp1_{k}", [64, T]) for k in ("u", "e", "relu", "s", "s2", "p")}
        conv_in = ya("conv_in", [P, 2, T + 8])
        conv_out = ya("conv_out", [P, 2, T])
        fcum = ya("fcum", [64, T])
        softplus1 = Softplus(0)
        pad_zeroed = sem("pad_zeroed")
        conved, conv_silued = sem("conved"), sem("conv_silued")
        sums_ready, sums_saved = sem("sums_ready"), sem("sums_saved")

        def sp_1(sp):
            with sp.Fori(0, XBC_TILES // 2 - 1) as j:
                load_w(sp, N_XBC + 1, cols(w_in, XBC_OFF + P + 2 * P * j), adv=j)
                load_w(sp, N_XBC + 2, cols(w_in, XBC_OFF + 2 * P + 2 * P * j), adv=j)
            load_w(sp, N_Z - 1, cols(w_in, XBC_OFF + (XBC_TILES - 1) * P))

        def act_1(act):
            begin_stage(act, 1)
            act.wait_ge(xt_saved, 16)
            act.drain().then_inc(conv_silued, 2)
            split_hi(act, N_XBC)
            softplus1.act(act, sp1["u"][:, :], sp1["e"][:, :], sp1["relu"][:, :])
            with act.Fori(0, XBC_TILES // 2) as j:
                for b in range(2):
                    n = N_XBC + b
                    split_hi(act, n + 1, adv=j)
                    projected(act, n, adv=j)
                    act.wait_ge(pad_zeroed, 1)
                    act.wait_ge(conved, 2 * j + b + 1)
                    act.activation(conv_in[:, b, 3:3 + T], acc[:, n % 2, :], ACT.Copy).then_inc(acc_free[n % 2], 1)
                    act.wait_ge(conved, 2 * j + b + 3)
                    act.activation(row(xbc, 2 * j + b), conv_out[:, b, :], ACT.Silu,
                                   bias=dcol(vec1, VEC1, "conv_b", 2 * j + b)).then_inc(conv_silued, 1)
            end_stage(act, 1)

        def pe_1(pe):
            begin_stage(pe, 1)
            project(pe, N_SMALL1, ha_hi, ha_lo)
            with pe.Fori(0, XBC_TILES // 2) as j:
                for b in range(2):
                    project(pe, N_XBC + b, ha_hi, ha_lo, adv=j)
            end_stage(pe, 1)

        def conv_taps(dve, dst, src, tap):
            dve.tensor_scalar(dst, src(0), tap(0), None, ALU.mult)
            for j in range(1, CONV_K):
                dve.drain()
                last = dve.scalar_tensor_tensor(dst, src(j), tap(j), dst, ALU.mult, ALU.add)
            return last

        def dve_1(dve):
            begin_stage(dve, 1)
            dve.wait_ge(xt_saved, 16)
            dve.drain().then_inc(conved, 2)
            split_lo(dve, N_XBC)
            projected(dve, N_SMALL1)
            dve.wait_ge(col_loaded, 16 * 8)
            dve.tensor_scalar(sp1["u"][:, :], acc[0:64, 0, :], sp_bias[:, :], sp_sign[:, :], ALU.add,
                              ALU.mult).then_inc(acc_free[0], 1)
            dve.drain().then_inc(softplus1.ready, 1)
            softplus1.dve(dve, *(sp1[k][:, :] for k in ("e", "relu", "s", "s2", "p")), spt[:, :])
            dve.drain()
            a = sp1["u"][0:SSM_HEADS, :]
            dve.tensor_scalar(a, spt[0:SSM_HEADS, :], neg_a[:, :], None, ALU.mult)
            dve.drain()
            for c in range(NCHUNK):
                t = slice(c * CHUNK, (c + 1) * CHUNK)
                dve.tensor_tensor_scan(acs[:, t], a[:, t], zero_col[0:SSM_HEADS, :].to_broadcast([SSM_HEADS, CHUNK]),
                                       0.0, ALU.add, ALU.add)
            f = slice(32, 32 + FOX_HEADS)
            dve.tensor_tensor_scan(fcum[f, :], spt[f, :], zero_col[f, :].to_broadcast([FOX_HEADS, T]),
                                   0.0, ALU.add, ALU.add)
            dve.drain().then_inc(sums_ready, 1)
            with dve.Fori(0, XBC_TILES // 2) as j:
                for b in range(2):
                    n = N_XBC + b
                    split_lo(dve, n + 1, adv=j)
                    dve.wait_ge(acc_free[n % 2], n // 2 + 1 + j)
                    dve.wait_ge(conv_silued, 2 * j + b + 1)
                    conv_taps(dve, conv_out[:, b, :], lambda k: conv_in[:, b, k:k + T],
                              lambda k: vec1[:, VEC1["conv_w"][0] + k * XBC_TILES:][:, bass.ds(2 * j + b, 1)]
                              ).then_inc(conved, 1)
            end_stage(dve, 1)

        def pool_1(pool):
            begin_stage(pool, 1)
            pool.wait_ge(xt_saved, 16)
            pool.memset(conv_in[:, :, 0:3], 0.0).then_inc(pad_zeroed, 1)
            pool.wait_ge(sums_ready, 1)
            pool.dma_start(acs_scr, acs[:, :]).then_inc(sums_saved, 16)
            pool.dma_start(fcum_scr, fcum[32:32 + FOX_HEADS, :]).then_inc(sums_saved, 16)
            pool.wait_ge(sums_saved, 32)
            end_stage(pool, 1)


        ya = ya_region()
        x_st = ya("x_st", [P, 8, CHUNK])
        bc_st = ya("bc_st", [P, 2, CHUNK])
        dtacs_st = ya("dtacs_st", [SSM_HEADS, 2, CHUNK])
        acs_bc = ya("acs_bc", [P, SSM_HEADS, CHUNK])
        acs_n = ya("acs_n", [P, HPG, CHUNK])
        decay = ya("decay", [P, SSM_HEADS, CHUNK])
        tok16 = ya("tok16", [P, 2, SSM_HEADS])
        b_tok = ya("b_tok", [P, P])
        e_acs = ya("e_acs", [P, HPG, CHUNK])
        c_dec = ya("c_dec", [P, HPG, CHUNK])
        xdt = ya("xdt", [P, SSM_HEADS, SSM_P])
        xdec = ya("xdec", [P, SSM_HEADS, SSM_P])
        state = ya("state", [P, HPG, SSM_P])
        xskip = ya("xskip", [P, 8, CHUNK])
        to_end = ya("to_end", [P, 2, SSM_HEADS])
        staged, bc_loaded = sem("staged"), [sem("bc_loaded0"), sem("bc_loaded1")]
        turned2, tok_ready, b_ready = sem("turned2"), sem("tok_ready"), sem("b_ready")
        cb_done, seg_done, masked2, decay_done = sem("cb_done"), sem("seg_done"), sem("masked2"), sem("decay_done")
        end_arg, end_exp, e_acs_done = sem("end_arg"), sem("end_exp"), sem("e_acs_done")
        cdec_done, xdec_done, m_done = sem("cdec_done"), sem("xdec_done"), sem("m_done")
        xskip_done, y_done, kv_done = sem("xskip_done"), sem("y_done"), sem("kv_done")
        chunk_done = sem("chunk_done")
        ypsum = acc[:, 1, :]
        kvpsum = work[:, 3, :]

        def chunk_of(x, c):
            return x[:, :, bass.ds(c * CHUNK, CHUNK)]

        def sp_2(sp):
            pass

        def pool_2(pool):
            begin_stage(pool, 2)
            masked_fill = pool.to_reg(MASKED)
            with pool.Fori(0, NCHUNK) as c:
                pool.wait_ge(chunk_done, c + 1)
                pool.dma_start(acs_bc[:, :, :], acs_scr[:, bass.ds(c * CHUNK, CHUNK)].partition_broadcast(P)
                               ).then_inc(bc_loaded[0], 16)
                for g in range(SSM_G):
                    pool.dma_start(acs_n[g * 64:g * 64 + 64, :, :],
                                   acs_scr[g * HPG:(g + 1) * HPG, bass.ds(c * CHUNK, CHUNK)].partition_broadcast(64)
                                   ).then_inc(bc_loaded[1], 16)
                pool.tensor_copy(x_st[:, :, :], chunk_of(xbc[:, 0:8, :], c))
                pool.tensor_copy(bc_st[:, :, :], chunk_of(xbc[:, 8:10, :], c))
                pool.drain()
                pool.tensor_copy(dtacs_st[:, 0, :], spt[0:SSM_HEADS, bass.ds(c * CHUNK, CHUNK)])
                pool.tensor_copy(dtacs_st[:, 1, :], acs[:, bass.ds(c * CHUNK, CHUNK)])
                pool.drain().then_inc(staged, 1)
                pool.tensor_tensor(xskip[:, :, :], x_st[:, :, :],
                                   dskip[:, :].unsqueeze(2).to_broadcast([P, 8, CHUNK]), ALU.mult).then_inc(xskip_done, 1)
                wait_here(pool, seg_done, c + 1)
                pool.affine_select(out=decay[:, :, :], in_=decay[:, :, :], compare_op=ALU.is_ge, fill=masked_fill,
                                   base=0, pattern=[[0, SSM_HEADS], [1, CHUNK]], channel_multiplier=-1
                                   ).then_inc(masked2, 1)
            end_stage(pool, 2)

        def pe_2(pe):
            begin_stage(pe, 2)
            with pe.Fori(0, NCHUNK) as c:
                pe.wait_ge(staged, c + 1)
                for i in range(8):
                    pe.transpose(work[:, i // 4, (i % 4) * P:(i % 4 + 1) * P], x_st[:, i, :], ident[:, :])
                pe.transpose(work[:, 2, 0:P], bc_st[:, 0, :], ident[:, :])
                for i in range(2):
                    mm = pe.transpose(work[:, 2, P + i * 16:P + i * 16 + 16], dtacs_st[:, i, :], ident[0:16, 0:16])
                mm.then_inc(turned2, 1)
                for g in range(SSM_G):
                    mm = pe.matmul(acc[:, 0, g * HALF:g * HALF + CHUNK], bc_st[g * 64:g * 64 + 64, 0, :],
                                   bc_st[g * 64:g * 64 + 64, 1, :], start=True, stop=True)
                mm.then_inc(cb_done, 1)
                pe.wait_ge(b_ready, c + 1)
                pe.wait_ge(xdec_done, c + 1)
                for g in range(SSM_G):
                    mm = pe.matmul(kvpsum[g * 64:g * 64 + 64, :], b_tok[:, g * 64:g * 64 + 64],
                                   xdec[:, g * HPG:(g + 1) * HPG, :], start=True, stop=True)
                mm.then_inc(kv_done, 1)
                pe.wait_ge(m_done, c + 1)
                pe.wait_ge(cdec_done, c + 1)
                for h in range(SSM_HEADS):
                    g, r = divmod(h, HPG)
                    y = ypsum[(h % 2) * 64:(h % 2) * 64 + 64, (h // 2) * CHUNK:(h // 2 + 1) * CHUNK]
                    pe.matmul(y, xdt[:, h, :], decay[:, h, :], start=True, stop=False)
                    mm = pe.matmul(y, state[g * 64:g * 64 + 64, r, :], c_dec[g * 64:g * 64 + 64, r, :],
                                   start=False, stop=True)
                mm.then_inc(y_done, 1)
            end_stage(pe, 2)

        def act_2(act):
            begin_stage(act, 2)
            with act.Fori(0, NCHUNK) as c:
                act.wait_ge(turned2, c + 1)
                act.activation(tok16[:, :, :], work[:, 2, P:P + 32], ACT.Copy).then_inc(tok_ready, 1)
                act.activation(b_tok[:, :], work[:, 2, 0:P], ACT.Copy).then_inc(b_ready, 1)
                act.wait_ge(bc_loaded[1], 32 * c + 32)
                act.activation(e_acs[:, :, :], acs_n[:, :, :], ACT.Exp).then_inc(e_acs_done, 1)
                act.wait_ge(end_arg, c + 1)
                act.activation(to_end[:, 1, :], to_end[:, 0, :], ACT.Exp).then_inc(end_exp, 1)
                act.wait_ge(masked2, c + 1)
                act.activation(decay[:, :, :], decay[:, :, :], ACT.Exp).then_inc(decay_done, 1)
            end_stage(act, 2)

        def dve_2(dve):
            begin_stage(dve, 2)
            dve.memset(state[:, :, :], 0.0)
            dve.drain().then_inc(chunk_done, 1)
            with dve.Fori(0, NCHUNK) as c:
                dve.wait_ge(tok_ready, c + 1)
                dve.wait_ge(bc_loaded[0], 16 * c + 16)
                dve.tensor_tensor(decay[:, :, :], acs_bc[:, :, :],
                                  tok16[:, 1, :].unsqueeze(2).to_broadcast([P, SSM_HEADS, CHUNK]),
                                  ALU.subtract).then_inc(seg_done, 1)
                dve.tensor_tensor(to_end[:, 0, :], acs_bc[:, :, CHUNK - 1], tok16[:, 1, :],
                                  ALU.subtract).then_inc(end_arg, 1)
                dve.tensor_tensor(xdt[:, :, :], work[:, 0:2, :].rearrange("p b (h d) -> p (b h) d", d=SSM_P),
                                  tok16[:, 0, :].unsqueeze(2).to_broadcast([P, SSM_HEADS, SSM_P]), ALU.mult)
                dve.drain()
                dve.wait_ge(end_exp, c + 1)
                dve.tensor_tensor(xdec[:, :, :], xdt[:, :, :],
                                  to_end[:, 1, :].unsqueeze(2).to_broadcast([P, SSM_HEADS, SSM_P]),
                                  ALU.mult).then_inc(xdec_done, 1)
                dve.wait_ge(e_acs_done, c + 1)
                dve.tensor_tensor(c_dec[:, :, :], e_acs[:, :, :],
                                  bc_st[:, 1, :].unsqueeze(1).to_broadcast([P, HPG, CHUNK]), ALU.mult).then_inc(cdec_done, 1)
                dve.wait_ge(decay_done, c + 1)
                dve.wait_ge(cb_done, c + 1)
                for g in range(SSM_G):
                    m = dve.tensor_tensor(decay[:, g * HPG:(g + 1) * HPG, :], decay[:, g * HPG:(g + 1) * HPG, :],
                                          acc[:, 0, g * HALF:g * HALF + CHUNK].unsqueeze(1).to_broadcast([P, HPG, CHUNK]),
                                          ALU.mult)
                m.then_inc(m_done, 1)
                dve.wait_ge(xskip_done, c + 1)
                dve.wait_ge(y_done, c + 1)
                dve.tensor_tensor(chunk_of(xbc[:, 0:8, :], c), ypsum.rearrange("p (i l) -> p i l", l=CHUNK),
                                  xskip[:, :, :], ALU.add)
                dve.wait_ge(kv_done, c + 1)
                dve.tensor_tensor(state[:, :, :], state[:, :, :],
                                  e_acs[:, :, CHUNK - 1].unsqueeze(2).to_broadcast([P, HPG, SSM_P]), ALU.mult)
                dve.drain()
                dve.tensor_tensor(state[:, :, :], state[:, :, :], kvpsum.rearrange("p (r d) -> p r d", d=SSM_P), ALU.add)
                dve.drain().then_inc(chunk_done, 1)
            end_stage(dve, 2)

        ar = Region(at_arena + XBC_TILES * T * 4, arena_end)
        silu_z = ar("silu_z", [P, 2, T])
        yw = Region(at_arena + 8 * T * 4, arena_end)("yw", [P, 2, T])
        yz_done, yw_done, yw_hi = sem("yz_done"), sem("yw_done"), sem("yw_hi")

        def sp_3(sp):
            with sp.Fori(0, 4) as j:
                for b in range(2):
                    load_w(sp, N_Z + b, cols(w_in, Z_OFF + b * P + 2 * P * j), adv=j)

        def pe_3(pe):
            begin_stage(pe, 3)
            with pe.Fori(0, 4) as j:
                for b in range(2):
                    project(pe, N_Z + b, ha_hi, ha_lo, adv=j)
            end_stage(pe, 3)

        def act_3(act):
            begin_stage(act, 3)
            with act.Fori(0, 4) as j:
                for b in range(2):
                    n = N_Z + b
                    split_hi(act, n + 1, adv=j)
                    projected(act, n, adv=j)
                    act.wait_ge(yz_done, 2 * j + b + 1)
                    act.activation(silu_z[:, b, :], acc[:, n % 2, :], ACT.Silu).then_inc(acc_free[n % 2], 1)
                    act.wait_ge(yw_done, 2 * j + b + 1)
                    act.activation(row(ya_hi, 2 * j + b), yw[:, b, :], ACT.Copy).then_inc(yw_hi, 1)
                    act.activation(row(xbc, 2 * j + b), row(xbc, 2 * j + b), ACT.Square).then_inc(Norm.squared, 1)
            end_stage(act, 3)

        def dve_3(dve):
            begin_stage(dve, 3)
            dve.drain().then_inc(yz_done, 2)
            with dve.Fori(0, 4) as j:
                for b in range(2):
                    n = N_Z + b
                    split_lo(dve, n + 1, adv=j)
                    dve.wait_ge(acc_free[n % 2], n // 2 + 1 + j)
                    dve.tensor_tensor(row(xbc, 2 * j + b), row(xbc, 2 * j + b), silu_z[:, b, :],
                                      ALU.mult).then_inc(yz_done, 1)
                    dve.drain()
                    dve.tensor_scalar(yw[:, b, :], row(xbc, 2 * j + b), dcol(vec1, VEC1, "ssm_norm_w", 2 * j + b), None,
                                      ALU.mult).then_inc(yw_done, 1)
                    dve.wait_ge(yw_hi, 2 * j + b + 1)
                    dve.tensor_tensor(row(ya_lo, 2 * j + b), yw[:, b, :], row(ya_hi, 2 * j + b).bitcast(F32), ALU.subtract)
            end_stage(dve, 3)

        def pool_3(pool):
            begin_stage(pool, 3)
            end_stage(pool, 3)

        ar = Region(at_arena + 8 * T * 4, arena_end)
        root4 = ar("root4", [P, T])
        rstd4 = ar("rstd4", [P, T])
        ar = Region(at_arena + XBC_TILES * T * 4, arena_end)
        gate4 = ar("gate4", [P, T])
        mix4 = ar("mix4", [P, T])
        norm4 = Norm(1)
        gate4_used, mix4_free, mix4_saved = sem("gate4_used"), sem("mix4_free"), sem("mix4_saved")

        def load_mix(sp, n0, w_proj, gate_off):
            with sp.Fori(0, KT) as d:
                load_w(sp, n0, cols(w_in, G_OFF + gate_off + P * d), adv=d)
                load_w(sp, n0 + 1, cols(w_proj, P * d), adv=d)

        def project_mix(pe, n0):
            with pe.Fori(0, KT) as d:
                project(pe, n0, ha_hi, ha_lo, adv=d)
                project(pe, n0 + 1, ya_hi, ya_lo, adv=d)

        def sp_4(sp):
            load_mix(sp, N_MIX1, io["w_proj_ssm"], 0)

        def pe_4(pe):
            begin_stage(pe, 4)
            for f in range(KT):
                for h in range(2):
                    mm = pe.matmul(work[:, h, :], ones[:, :], xbc[:, f, h * HALF:(h + 1) * HALF],
                                   start=(f == 0), stop=(f == KT - 1))
                mm.then_inc(norm4.summed, 1)
            project_mix(pe, N_MIX1)
            end_stage(pe, 4)

        def act_4(act):
            begin_stage(act, 4)
            norm4.act_root(act, root4)
            with act.Fori(0, KT) as d:
                split_hi(act, N_MIX1 + 1, adv=d)
                projected(act, N_MIX1, adv=d)
                act.wait_ge(gate4_used, d + 1)
                act.activation(gate4[:, :], acc[:, N_MIX1 % 2, :], ACT.Sigmoid,
                               bias=dcol(vec1, VEC1, "b_gate", d)).then_inc(acc_free[N_MIX1 % 2], 1)
                split_hi(act, N_MIX1 + 2, adv=d)
            end_stage(act, 4)

        def dve_4(dve):
            begin_stage(dve, 4)
            dve.drain().then_inc(gate4_used, 1)
            norm4.dve(dve, root4, rstd4)
            dve.drain()
            with dve.Fori(0, KT) as d:
                split_lo(dve, N_MIX1 + 1, adv=d)
                dve.wait_ge(acc_free[N_MIX1 % 2], N_MIX1 // 2 + 1 + d)
                dve.tensor_tensor(gate4[:, :], gate4[:, :], rstd4[:, :], ALU.mult)
                split_lo(dve, N_MIX1 + 2, adv=d)
                dve.drain()
                projected(dve, N_MIX1 + 1, adv=d)
                dve.wait_ge(mix4_free, d + 1)
                dve.tensor_tensor(mix4[:, :], acc[:, (N_MIX1 + 1) % 2, :], gate4[:, :],
                                  ALU.mult).then_inc(acc_free[(N_MIX1 + 1) % 2], 1)
                dve.drain().then_inc(gate4_used, 1)
            end_stage(dve, 4)

        def pool_4(pool):
            begin_stage(pool, 4)
            pool.drain().then_inc(mix4_free, 1)
            with pool.Fori(0, KT) as d:
                wait_here(pool, gate4_used, d + 2)
                pool.dma_start(row(merged_scr, d), mix4[:, :]).then_inc(mix4_saved, 16)
                wait_here(pool, mix4_saved, 16 * d + 16)
                pool.drain().then_inc(mix4_free, 1)
            end_stage(pool, 4)

        ar = arena()
        q_t = ar("q_t", [P, T])
        k_t = ar("k_t", [P, T])
        v_t = ar("v_t", [P, T])
        v_tok = ar("v_tok", [P, NT, FOX_D])
        silu_za = ar("silu_za", [P, T])
        f_bc = ar("f_bc", [P, T])
        prob = ar("prob", [P, 2, T])
        prob_t = ar("prob_t", [P, 2, NT, P])
        y_head = ar("y_head", [P, T])
        neg_max = ar("neg_max", [P, 2])
        row_sum = ar("row_sum", [P, 2])
        row_inv = ar("row_inv", [P, 2])
        fbc_loaded, head_done5 = sem("fbc_loaded"), sem("head_done5")
        v_turned, v_ready = sem("v_turned"), sem("v_ready")
        qk_done, logits_done, diag_done, max_done = sem("qk_done"), sem("logits_done"), sem("diag_done"), sem("max_done")
        exp_done, prob_done, p_turned, p_copied = sem("exp_done"), sem("prob_done"), sem("p_turned"), sem("p_copied")
        pv_done, y_gated, y_hi5 = sem("pv_done"), sem("y_gated"), sem("y_hi5")
        FOX_SCALE = float(FOX_D) ** -0.5

        def sp_5(sp):
            with sp.Fori(0, FOX_HEADS) as h:
                for i, off in enumerate((Q_OFF, K_OFF, V_OFF, ZA_OFF)):
                    load_w(sp, N_FOX + i, cols(w_in, off + P * h), adv=2 * h)

        def pool_5(pool):
            begin_stage(pool, 5)
            masked_fill = pool.to_reg(MASKED)
            with pool.Fori(0, FOX_HEADS) as h:
                wait_here(pool, head_done5, h + 1)
                pool.dma_start(f_bc[:, :], fcum_scr[bass.ds(h, 1), :].rearrange("a t -> (a t)").partition_broadcast(P)
                               ).then_inc(fbc_loaded, 16)
                for t in range(NT):
                    wait_here(pool, logits_done, NT * h + t + 1)
                    pool.affine_select(out=prob[:, t % 2, t * P:(t + 1) * P], in_=prob[:, t % 2, t * P:(t + 1) * P],
                                       compare_op=ALU.is_ge, fill=masked_fill, base=0, pattern=[[-1, P]],
                                       channel_multiplier=1).then_inc(diag_done, 1)
            end_stage(pool, 5)

        def pe_5(pe):
            begin_stage(pe, 5)
            with pe.Fori(0, FOX_HEADS) as h:
                for i in range(4):
                    if i == 0:
                        pe.wait_ge(y_gated, 2 * h + 2)
                    project(pe, N_FOX + i, ha_hi, ha_lo, adv=2 * h)

                def scores(t):
                    if t >= 2:
                        pe.wait_ge(logits_done, NT * h + t - 1)
                    w = (t + 1) * P
                    for a in range(0, w, HALF):
                        b = min(w, a + HALF)
                        mm = pe.matmul(work[:, 2 * (1 - t % 2) + a // HALF, 0:b - a], q_t[:, t * P:(t + 1) * P],
                                       k_t[:, a:b], start=True, stop=True)
                    mm.then_inc(qk_done, 1)

                def turn_probs(t):
                    pe.wait_ge(prob_done, NT * h + t + 1)
                    if t >= 1:
                        pe.wait_ge(p_copied, NT * h + t)
                    for b in range(t + 1):
                        mm = pe.transpose(acc[:, 0, b * P:(b + 1) * P], prob[:, t % 2, b * P:(b + 1) * P], ident[:, :])
                    mm.then_inc(p_turned, 1)

                def weigh_values(t):
                    pe.wait_ge(p_copied, NT * h + t + 1)
                    for b in range(t + 1):
                        mm = pe.matmul(acc[:, 1, t * P:(t + 1) * P], v_tok[:, b, :], prob_t[:, t % 2, b, :],
                                       start=(b == 0), stop=(b == t))
                    mm.then_inc(pv_done, 1)

                pe.wait_ge(acc_free[(N_FOX + 2) % 2], (N_FOX + 2) // 2 + 1 + 2 * h)
                for b in range(NT):
                    mm = pe.transpose(work[:, b // 4, (b % 4) * P:(b % 4 + 1) * P], v_t[:, b * P:(b + 1) * P], ident[:, :])
                mm.then_inc(v_turned, 1)
                pe.wait_ge(acc_free[(N_FOX + 3) % 2], (N_FOX + 3) // 2 + 1 + 2 * h)
                scores(0)
                pe.wait_ge(v_ready, h + 1)
                scores(1)
                for t in range(NT):
                    turn_probs(t)
                    if t + 2 < NT:
                        scores(t + 2)
                    weigh_values(t)
            end_stage(pe, 5)

        def act_5(act):
            begin_stage(act, 5)
            with act.Fori(0, FOX_HEADS) as h:
                for i, (dst, func) in enumerate(((q_t, ACT.Copy), (k_t, ACT.Copy), (v_t, ACT.Copy), (silu_za, ACT.Silu))):
                    n = N_FOX + i
                    split_hi(act, n + 1, adv=2 * h)
                    projected(act, n, adv=2 * h)
                    act.activation(dst[:, :], acc[:, n % 2, :], func).then_inc(acc_free[n % 2], 1)
                act.wait_ge(v_turned, h + 1)
                act.activation(v_tok[:, :, :], work[:, 0:2, :], ACT.Copy).then_inc(v_ready, 1)

                def exps(t):
                    act.wait_ge(max_done, NT * h + t + 1)
                    w = (t + 1) * P
                    act.activation(prob[:, t % 2, 0:w], prob[:, t % 2, 0:w], ACT.Exp, bias=neg_max[:, t % 2:t % 2 + 1],
                                   accum_out=row_sum[:, t % 2:t % 2 + 1]).then_inc(exp_done, 1)

                exps(0)
                for t in range(NT):
                    if t + 1 < NT:
                        exps(t + 1)
                    act.wait_ge(p_turned, NT * h + t + 1)
                    act.activation(prob_t[:, t % 2, 0:t + 1, :], acc[:, 0, 0:(t + 1) * P], ACT.Copy).then_inc(p_copied, 1)
                act.wait_ge(y_gated, 2 * h + 4)
                act.activation(row(ya_hi, h), y_head[:, :], ACT.Copy).then_inc(y_hi5, 1)
            end_stage(act, 5)

        def dve_5(dve):
            begin_stage(dve, 5)
            dve.drain().then_inc(y_gated, 2)
            dve.drain().then_inc(head_done5, 1)
            with dve.Fori(0, FOX_HEADS) as h:
                for i in range(4):
                    split_lo(dve, N_FOX + i + 1, adv=2 * h)
                dve.wait_ge(fbc_loaded, 16 * h + 16)

                def logits(t):
                    dve.wait_ge(qk_done, NT * h + t + 1)
                    if t >= 2:
                        dve.wait_ge(p_turned, NT * h + t - 1)
                    w = (t + 1) * P
                    s = work[:, 2 * (1 - t % 2):2 * (1 - t % 2) + 2, :].rearrange("p a b -> p (a b)")
                    dve.scalar_tensor_tensor(prob[:, t % 2, 0:w], s[:, 0:w], FOX_SCALE, f_bc[:, 0:w],
                                             ALU.mult, ALU.add).then_inc(logits_done, 1)
                    dve.wait_ge(diag_done, NT * h + t + 1)
                    dve.tensor_reduce(neg_max[:, t % 2:t % 2 + 1], prob[:, t % 2, 0:w], AX.X, ALU.max,
                                      negate=True).then_inc(max_done, 1)

                def normalise(t):
                    dve.wait_ge(exp_done, NT * h + t + 1)
                    dve.reciprocal(row_inv[:, t % 2:t % 2 + 1], row_sum[:, t % 2:t % 2 + 1])
                    dve.drain()
                    w = (t + 1) * P
                    dve.tensor_scalar(prob[:, t % 2, 0:w], prob[:, t % 2, 0:w], row_inv[:, t % 2:t % 2 + 1], None,
                                      ALU.mult).then_inc(prob_done, 1)

                def gate(half):
                    dve.wait_ge(pv_done, NT * h + 4 * half + 4)
                    s = slice(half * HALF, (half + 1) * HALF)
                    dve.tensor_tensor(y_head[:, s], acc[:, 1, s], silu_za[:, s], ALU.mult).then_inc(y_gated, 1)

                logits(0)
                for t in range(NT):
                    normalise(t)
                    if t + 1 < NT:
                        logits(t + 1)
                    if t == 5:
                        gate(0)
                gate(1)
                dve.wait_ge(y_hi5, h + 1)
                dve.tensor_tensor(row(ya_lo, h), y_head[:, :], row(ya_hi, h).bitcast(F32), ALU.subtract)
                dve.drain().then_inc(head_done5, 1)
            end_stage(dve, 5)

        ar = arena()
        merged = ar("merged", [P, KT, T])
        gate6 = ar("gate6", [P, T])
        mix_before = ar("mix_before", [P, T])
        gate6_used, mix_loaded = sem("gate6_used"), sem("mix_loaded")

        def sp_6(sp):
            load_mix(sp, N_MIX2, io["w_proj_att"], D)

        def pe_6(pe):
            begin_stage(pe, 6)
            project_mix(pe, N_MIX2)
            end_stage(pe, 6)

        def act_6(act):
            begin_stage(act, 6)
            with act.Fori(0, KT) as d:
                split_hi(act, N_MIX2 + 1, adv=d)
                projected(act, N_MIX2, adv=d)
                act.wait_ge(gate6_used, d + 1)
                act.activation(gate6[:, :], acc[:, N_MIX2 % 2, :], ACT.Sigmoid,
                               bias=vec1[:, VEC1["b_gate"][0] + 8:VEC1["b_gate"][1]][:, bass.ds(d, 1)]
                               ).then_inc(acc_free[N_MIX2 % 2], 1)
                split_hi(act, N_MIX2 + 2, adv=d)
            end_stage(act, 6)

        def dve_6(dve):
            begin_stage(dve, 6)
            dve.drain().then_inc(gate6_used, 1)
            with dve.Fori(0, KT) as d:
                split_lo(dve, N_MIX2 + 1, adv=d)
                split_lo(dve, N_MIX2 + 2, adv=d)
                dve.wait_ge(acc_free[N_MIX2 % 2], N_MIX2 // 2 + 1 + d)
                projected(dve, N_MIX2 + 1, adv=d)
                dve.tensor_tensor(gate6[:, :], acc[:, (N_MIX2 + 1) % 2, :], gate6[:, :],
                                  ALU.mult).then_inc(acc_free[(N_MIX2 + 1) % 2], 1)
                dve.drain()
                dve.wait_ge(mix_loaded, 16 * d + 16)
                dve.tensor_tensor(row(merged, d), gate6[:, :], mix_before[:, :], ALU.add)
                dve.drain().then_inc(gate6_used, 1)
            end_stage(dve, 6)

        def pool_6(pool):
            begin_stage(pool, 6)
            with pool.Fori(0, KT) as d:
                wait_here(pool, gate6_used, d + 1)
                pool.dma_start(mix_before[:, :], row(merged_scr, d)).then_inc(mix_loaded, 16)
            end_stage(pool, 6)

        x1 = Region(at_ya, at_ya + big)("x1", [P, KT, T])
        ar = Region(at_arena + big, arena_end)
        xt_tile = ar("xt_tile", [P, 2, T])
        merged_hi, merged_split = sem("merged_hi"), sem("merged_split")
        xt_loaded, res_done = [sem("xt_loaded0"), sem("xt_loaded1")], sem("res_done")

        def sp_7(sp):
            with sp.Fori(0, 4) as j:
                for b in range(2):
                    load_w(sp, N_OUT1 + b, cols(io["w_out"], b * P + 2 * P * j), adv=j)

        def pe_7(pe):
            begin_stage(pe, 7)
            pe.wait_ge(merged_split, KT)
            with pe.Fori(0, 4) as j:
                for b in range(2):
                    project(pe, N_OUT1 + b, ha_hi, ha_lo, adv=j)
            end_stage(pe, 7)

        def act_7(act):
            begin_stage(act, 7)
            for k in range(KT):
                act.activation(ha_hi[:, k, :], merged[:, k, :], ACT.Copy).then_inc(merged_hi, 1)
            with act.Fori(0, 3) as j:
                for b in range(2):
                    split_hi(act, N_OUT1 + b + 1, adv=j)
            split_hi(act, N_SMALL2 - 1)
            act.wait_ge(w_part, 3 * 16)
            split_hi(act, N_SMALL2)
            end_stage(act, 7)

        def dve_7(dve):
            begin_stage(dve, 7)
            dve.drain().then_inc(res_done, 2)
            for k in range(KT):
                dve.wait_ge(merged_hi, k + 1)
                dve.tensor_tensor(ha_lo[:, k, :], merged[:, k, :], ha_hi[:, k, :].bitcast(F32),
                                  ALU.subtract).then_inc(merged_split, 1)
            with dve.Fori(0, 4) as j:
                for b in range(2):
                    n = N_OUT1 + b
                    split_lo(dve, n + 1, adv=j)
                    projected(dve, n, adv=j)
                    dve.wait_ge(xt_loaded[b], 16 * j + 16)
                    dve.scalar_tensor_tensor(row(x1, 2 * j + b), acc[:, n % 2, :], ada[:, 16:24][:, bass.ds(2 * j + b, 1)],
                                             xt_tile[:, b, :], ALU.mult, ALU.add).then_inc(acc_free[n % 2], 1)
                    dve.drain().then_inc(res_done, 1)
            end_stage(dve, 7)

        def pool_7(pool):
            begin_stage(pool, 7)
            with pool.Fori(0, 4) as j:
                for b in range(2):
                    wait_here(pool, res_done, 2 * j + b + 1)
                    pool.dma_start(xt_tile[:, b, :], row(xt_scr, 2 * j + b)).then_inc(xt_loaded[b], 16)
            end_stage(pool, 7)

        ar = arena()
        sq8 = ar("sq8", [P, 2, T])
        root8 = ar("root8", [P, T])
        rstd8 = ar("rstd8", [P, T])
        root9 = ar("root9", [P, T])
        rstd9 = ar("rstd9", [P, T])
        v8 = ar("v8", [P, 2, T])
        norm8, norm9 = Norm(2), Norm(3)
        x1_done, v8_done, h2_hi = sem("x1_done"), sem("v8_done"), sem("h2_hi")

        def sp_8(sp):
            wait_here(sp, lo_done, N_SMALL2 - 1)
            sp.dma_start(w_raw[:, N_SMALL2 % 2, :, 0:32], cols(w_in2f, MI, 32)).then_inc(w_loaded[N_SMALL2 % 2], 16)
            sp.dma_start(w_raw[:, N_SMALL2 % 2, :, 32:64], cols(w_in2f, MF, 32)).then_inc(w_part, 16)
            sp.dma_start(w_raw[:, N_SMALL2 % 2, :, 64:P], cols(w_in2f, GA, 64)).then_inc(w_part, 16)

        w_in2f = w_in2.rearrange("a d c -> (a d) c")

        def pe_8(pe):
            begin_stage(pe, 8)
            norm8.pe(pe, lambda f: sq8[:, f % 2, :])
            pe.wait_ge(norm8.rooted, norm8.use + 1)
            norm9.pe(pe, lambda f: sq8[:, f % 2, :])
            end_stage(pe, 8)

        def act_8(act):
            begin_stage(act, 8)
            norm8.act(act, x1, sq8, root8)
            for f in range(KT):
                act.wait_ge(x1_done, f + 1)
                if f >= 2:
                    act.wait_ge(norm9.summed, norm9.tiles + f - 1)
                act.activation(sq8[:, f % 2, :], x1[:, f, :], ACT.Square).then_inc(norm9.squared, 1)
            norm9.act_root(act, root9)
            for f in range(KT):
                act.wait_ge(v8_done, f + 1)
                act.activation(ha_hi[:, f, :], v8[:, f % 2, :], ACT.Copy).then_inc(h2_hi, 1)
            end_stage(act, 8)

        def dve_8(dve):
            begin_stage(dve, 8)
            norm8.dve(dve, root8, rstd8)
            dve.drain()
            for f in range(KT):
                dve.scalar_tensor_tensor(x1[:, f, :], x1[:, f, :], col1("final_norm_w", f), rstd8[:, :],
                                         ALU.mult, ALU.mult).then_inc(x1_done, 1)
            norm9.dve(dve, root9, rstd9)
            dve.drain()
            for f in range(KT):
                dve.scalar_tensor_tensor(v8[:, f % 2, :], x1[:, f, :], vec2[:, VEC2["norm_g_2"][0] + f:][:, 0:1],
                                         rstd9[:, :], ALU.mult, ALU.mult).then_inc(v8_done, 1)
                dve.wait_ge(h2_hi, f + 1)
                dve.tensor_tensor(ha_lo[:, f, :], v8[:, f % 2, :], ha_hi[:, f, :].bitcast(F32), ALU.subtract)
                dve.drain()
            end_stage(dve, 8)

        ar = Region(v8_end := ar.at, arena_end)
        bias_rows = ar("bias_rows", [P, 3 * P])
        bias_tile = ar("bias_tile", [P, BANDW])
        rel_loaded, skew_saved, skew_loaded, bias_saved = sem("rel_loaded"), sem("skew_saved"), sem("skew_loaded"), sem("bias_saved")
        rel_rev = io["rel_bias_2"].rearrange("a h r -> (a h) r")

        def pool_8(pool):
            begin_stage(pool, 8)
            with pool.Fori(0, ML_HEADS) as h:
                pool.dma_start(bias_rows[:, P - 1:3 * P - 1],
                               rel_rev[bass.ds(h, 1), 0:2 * P].rearrange("a r -> (a r)").partition_broadcast(P)
                               ).then_inc(rel_loaded, 16)
                wait_here(pool, rel_loaded, 16 * h + 16)
                pool.tensor_copy(bias_rows[:, 0:P - 1], bias_rows[:, P - 1:P].to_broadcast([P, P - 1]))
                pool.tensor_copy(bias_rows[:, 3 * P - 1:3 * P], bias_rows[:, P - 1:P])
                pool.tensor_copy(bias_tile[:, 0:3 * P], bias_rows[:, P - 1:P].to_broadcast([P, 3 * P]))
                pool.drain()
                pool.dma_start(skew_scr.rearrange("(q w) -> q w", w=3 * P), bias_rows[:, :]).then_inc(skew_saved, 16)
                wait_here(pool, skew_saved, 16 * h + 16)
                pool.dma_start(bias_tile[:, 3 * P:BANDW],
                               skew_scr[P - 1:P - 1 + P * (3 * P - 1)].rearrange("(q w) -> q w", w=3 * P - 1)[:, 0:2 * P]
                               ).then_inc(skew_loaded, 16)
                wait_here(pool, skew_loaded, 16 * h + 16)
                pool.memset(bias_tile[0:HD, BANDW - HD:BANDW], MASKED)
                pool.memset(bias_tile[HD:P, 0:HD], MASKED)
                pool.drain()
                pool.dma_start(bias_scr[bass.ds(h, 1), :, :].rearrange("a q w -> q (a w)"), bias_tile[:, :]
                               ).then_inc(bias_saved, 16)
                wait_here(pool, bias_saved, 16 * h + 16)
            end_stage(pool, 8)

        b_gla = Region(at_arena, arena_end)("b_gla", [P, NCHUNK, 1 + CHUNK])
        keep = Region(at_arena + (NCHUNK * (1 + CHUNK) * 4 + 31) // 32 * 32, arena_end)
        B_tok = keep("B_tok", [P, NT, 8])
        em_tok = keep("em_tok", [P, NT, 8])
        at_arena2 = keep.at
        ar = Region(at_arena2, arena_end)
        spa = {k: ar(f"spa_{k}", [P, T]) for k in ("u", "e", "relu", "s", "s2", "p")}
        ga_t = ar("ga_t", [P, T])
        m9 = ar("m9", [32, T])
        em9 = ar("em9", [32, T])
        ar = Region(at_ya + big, at_ya + 2 * big)
        spm = {k: ar(f"spm_{k}", [32, T]) for k in ("u", "e", "relu", "s", "s2", "p")}
        ig9 = ar("ig9", [32, T])
        f9 = ar("f9", [32, T])
        softplus_ml, softplus_al = Softplus(1), Softplus(2)
        gates_read, alpha_mul, m_ready, em_ready = sem("gates_read"), sem("alpha_mul"), sem("m_ready"), sem("em_ready")
        ab_ready, turned9, a_saved = sem("ab_ready"), sem("turned9"), sem("a_saved")

        def sp_9(sp):
            pass

        def act_9(act):
            begin_stage(act, 9)
            split_hi(act, N_BAND)
            projected(act, N_SMALL2)
            act.activation(ig9[:, :], acc[0:32, N_SMALL2 % 2, :], ACT.Identity, bias=gate_bias2[0:32, :])
            act.activation(ga_t[64:64 + GLA_RANK, :], acc[64:64 + GLA_RANK, N_SMALL2 % 2, :], ACT.Copy)
            act.drain().then_inc(gates_read, 1)
            softplus_ml.act(act, spm["u"][:, :], spm["e"][:, :], spm["relu"][:, :])
            softplus_al.act(act, spa["u"][:, :], spa["e"][:, :], spa["relu"][:, :])
            act.wait_ge(m_ready, 1)
            act.activation(em9[:, :], m9[:, :], ACT.Exp, scale=-1.0).then_inc(em_ready, 1)
            act.wait_ge(turned9, 1)
            for dst, bank in ((B_tok, 2), (em_tok, 3)):
                act.activation(dst[:, :, :], work[:, bank, 0:NT * 32].rearrange("p (t h) -> p t h", h=32)[:, :, 0:8], ACT.Copy)
            end_stage(act, 9)

        def pe_9(pe):
            begin_stage(pe, 9)
            project(pe, N_SMALL2, ha_hi, ha_lo)
            pe.wait_ge(gates_read, 1)
            for h in range(2):
                mm = pe.matmul(work[:, h, :], w_alpha[64:64 + GLA_RANK, :],
                               ga_t[64:64 + GLA_RANK, h * HALF:(h + 1) * HALF], start=True, stop=True)
            mm.then_inc(alpha_mul, 1)
            pe.wait_ge(ab_ready, 1)
            pe.wait_ge(em_ready, 1)
            for src, bank in ((spm["u"], 2), (em9, 3)):
                for i in range(NT):
                    mm = pe.transpose(work[:, bank, i * 32:(i + 1) * 32], src[:, i * P:(i + 1) * P], ident[0:32, 0:32])
            mm.then_inc(turned9, 1)
            end_stage(pe, 9)

        def dve_9(dve):
            begin_stage(dve, 9)
            split_lo(dve, N_BAND)
            projected(dve, N_SMALL2)
            dve.wait_ge(gates_read, 1)
            dve.tensor_scalar(spm["u"][:, :], acc[32:64, N_SMALL2 % 2, :], gate_bias2[32:64, :], -1.0, ALU.add,
                              ALU.mult).then_inc(acc_free[N_SMALL2 % 2], 1)
            dve.drain().then_inc(softplus_ml.ready, 1)
            dve.wait_ge(alpha_mul, 1)
            dve.tensor_scalar(spa["u"][:, :], work[:, 0:2, :].rearrange("p a b -> p (a b)"),
                              vec2[:, VEC2["b_alpha_2"][0]:VEC2["b_alpha_2"][1]], -1.0, ALU.add, ALU.mult)
            dve.drain().then_inc(softplus_al.ready, 1)
            sp = spm["e"]
            softplus_ml.dve(dve, *(spm[k][:, :] for k in ("e", "relu", "s", "s2", "p")), spm["p"][:, :])
            dve.drain()
            dve.tensor_scalar(sp[:, :], spm["p"][:, :], -1.0, None, ALU.mult)
            dve.drain()
            dve.tensor_tensor_scan(f9[:, :], sp[:, :], zero_col[0:32, :].to_broadcast([32, T]), 0.0, ALU.add, ALU.add)
            dve.tensor_tensor_scan(m9[:, :], sp[:, :], ig9[:, :], 0.0, ALU.add, ALU.max).then_inc(m_ready, 1)
            dve.drain()
            dve.tensor_tensor(spm["u"][:, :], ig9[:, :], f9[:, :], ALU.subtract)
            dve.tensor_tensor(spm["s"][:, :], f9[:, :], m9[:, :], ALU.subtract)
            dve.drain().then_inc(ab_ready, 1)
            softplus_al.dve(dve, *(spa[k][:, :] for k in ("e", "relu", "s", "s2", "p")), spa["p"][:, :])
            dve.drain()
            la = spa["u"]
            dve.tensor_scalar(la[:, :], spa["p"][:, :], -1.0 / GLA_TAU, None, ALU.mult)
            dve.drain()
            for c in range(NCHUNK):
                dve.tensor_tensor_scan(b_gla[:, c, 1:1 + CHUNK], la[:, c * CHUNK:(c + 1) * CHUNK],
                                       zero_col[:, :].to_broadcast([P, CHUNK]), 0.0, ALU.add, ALU.add)
            end_stage(dve, 9)

        def pool_9(pool):
            begin_stage(pool, 9)
            pool.memset(b_gla[:, :, 0:1], 0.0)
            pool.wait_ge(ab_ready, 1)
            pool.dma_start(ml_a_scr, spm["s"][0:8, :]).then_inc(a_saved, 16)
            pool.wait_ge(a_saved, 16)
            end_stage(pool, 9)

        y2 = Region(at_ya + big, at_ya + 2 * big)("y2", [P, KT, T])
        ar = Region(at_arena2, arena_end)
        bq = ar("bq", [P, T])
        bk = ar("bk", [P, T])
        bv = ar("bv", [P, T])
        bv_tok = ar("bv_tok", [P, NT, P])
        band_bias = ar("band_bias", [P, 2, BANDW])
        band_p = ar("band_p", [P, 2, BANDW])
        band_pt = ar("band_pt", [P, 2, BAND_TILES, P])
        att_tok = ar("att_tok", [P, 2 * NT, HD])
        band_max = ar("band_max", [P, 2 * NT])
        band_sum = ar("band_sum", [P, 2 * NT])
        band_inv = ar("band_inv", [P, 2 * NT])
        BU = 2 * NT
        bias_loaded, band_gated = sem("bias_loaded"), sem("band_gated")
        V5, U5 = FOX_HEADS, FOX_HEADS * NT
        att_ready, att_turned = sem("att_ready"), sem("att_turned")
        HD_SCALE = float(HD) ** -0.5

        def band_width(m):
            return (min(m, BAND_TILES - 1) + 1) * P

        def sp_10(sp):
            with sp.Fori(0, PAIRS) as p:
                for i, off in enumerate((AQ, AK, AV, AG)):
                    load_w(sp, N_BAND + i, cols(w_in2f, off + P * p), adv=2 * p)

        def pool_10(pool):
            begin_stage(pool, 10)
            with pool.Fori(0, PAIRS) as p:
                wait_here(pool, band_gated, p + 1)
                pool.dma_start(band_bias[:, :, :], bias_scr[bass.ds(2 * p, 2), :, :].rearrange("h q w -> q h w")
                               ).then_inc(bias_loaded, 16)
            end_stage(pool, 10)

        def pe_10(pe):
            begin_stage(pe, 10)
            with pe.Fori(0, PAIRS) as p:
                pe.wait_ge(band_gated, p + 1)
                for i in range(4):
                    project(pe, N_BAND + i, ha_hi, ha_lo, adv=2 * p)

                def scores(u):
                    if u >= 2:
                        pe.wait_ge(logits_done, U5 + BU * p + u - 1)
                    m, r = divmod(u, 2)
                    w = band_width(m)
                    k0 = (m + 1) * P - w
                    for a in range(0, w, HALF):
                        b = min(w, a + HALF)
                        mm = pe.matmul(work[:, 2 * (1 - u % 2) + a // HALF, 0:b - a],
                                       bq[r * HD:(r + 1) * HD, m * P:(m + 1) * P],
                                       bk[r * HD:(r + 1) * HD, k0 + a:k0 + b], start=True, stop=True)
                    mm.then_inc(qk_done, 1)

                def turn_probs(u):
                    pe.wait_ge(exp_done, U5 + BU * p + u + 1)
                    if u >= 1:
                        pe.wait_ge(p_copied, U5 + BU * p + u)
                    for b in range(band_width(u // 2) // P):
                        mm = pe.transpose(acc[:, 0, b * P:(b + 1) * P], band_p[:, u % 2, b * P:(b + 1) * P], ident[:, :])
                    mm.then_inc(p_turned, 1)

                def weigh_values(u):
                    pe.wait_ge(p_copied, U5 + BU * p + u + 1)
                    m, r = divmod(u, 2)
                    nb = band_width(m) // P
                    for b in range(nb):
                        mm = pe.matmul(acc[:, 1, u * HD:(u + 1) * HD], band_pt[:, u % 2, b, :],
                                       bv_tok[:, m + 1 - nb + b, r * HD:(r + 1) * HD], start=(b == 0), stop=(b == nb - 1))
                    mm.then_inc(pv_done, 1)

                pe.wait_ge(acc_free[(N_BAND + 2) % 2], (N_BAND + 2) // 2 + 1 + 2 * p)
                for b in range(NT):
                    mm = pe.transpose(work[:, b // 4, (b % 4) * P:(b % 4 + 1) * P], bv[:, b * P:(b + 1) * P], ident[:, :])
                mm.then_inc(v_turned, 1)
                pe.wait_ge(acc_free[(N_BAND + 3) % 2], (N_BAND + 3) // 2 + 1 + 2 * p)
                scores(0)
                pe.wait_ge(v_ready, V5 + p + 1)
                scores(1)
                for u in range(BU):
                    turn_probs(u)
                    if u + 2 < BU:
                        scores(u + 2)
                    weigh_values(u)
                pe.wait_ge(att_ready, p + 1)
                for b in range(NT):
                    mm = pe.transpose(acc[:, 0, b * P:(b + 1) * P], att_tok[:, 2 * b:2 * b + 2, :], ident[:, :])
                mm.then_inc(att_turned, 1)
            end_stage(pe, 10)

        def act_10(act):
            begin_stage(act, 10)
            with act.Fori(0, PAIRS) as p:
                for i, (dst, func) in enumerate(((bq[:, :], ACT.Copy), (bk[:, :], ACT.Copy), (bv[:, :], ACT.Copy),
                                                 (row(y2, p), ACT.Silu))):
                    n = N_BAND + i
                    split_hi(act, n + 1, adv=2 * p)
                    projected(act, n, adv=2 * p)
                    act.activation(dst, acc[:, n % 2, :], func).then_inc(acc_free[n % 2], 1)
                act.wait_ge(v_turned, V5 + p + 1)
                act.activation(bv_tok[:, :, :], work[:, 0:2, :], ACT.Copy).then_inc(v_ready, 1)

                def exps(u):
                    act.wait_ge(max_done, U5 + BU * p + u + 1)
                    w = band_width(u // 2)
                    act.activation(band_p[:, u % 2, 0:w], band_p[:, u % 2, 0:w], ACT.Exp, bias=band_max[:, u:u + 1],
                                   accum_out=band_sum[:, u:u + 1]).then_inc(exp_done, 1)

                exps(0)
                for u in range(BU):
                    if u + 1 < BU:
                        exps(u + 1)
                    act.wait_ge(p_turned, U5 + BU * p + u + 1)
                    nb = band_width(u // 2) // P
                    act.activation(band_pt[:, u % 2, 0:nb, :], acc[:, 0, 0:nb * P], ACT.Copy).then_inc(p_copied, 1)
            end_stage(act, 10)

        def dve_10(dve):
            begin_stage(dve, 10)
            dve.drain().then_inc(band_gated, 1)
            with dve.Fori(0, PAIRS) as p:
                for i in range(4):
                    split_lo(dve, N_BAND + i + 1, adv=2 * p)
                dve.wait_ge(bias_loaded, 16 * p + 16)
                for u in range(BU):
                    dve.wait_ge(qk_done, U5 + BU * p + u + 1)
                    if u >= 2:
                        dve.wait_ge(p_turned, U5 + BU * p + u - 1)
                    w = band_width(u // 2)
                    s = work[:, 2 * (1 - u % 2):2 * (1 - u % 2) + 2, :].rearrange("p a b -> p (a b)")
                    dve.scalar_tensor_tensor(band_p[:, u % 2, 0:w], s[:, 0:w], HD_SCALE,
                                             band_bias[:, u % 2, BANDW - w:BANDW], ALU.mult, ALU.add).then_inc(logits_done, 1)
                    dve.drain()
                    dve.tensor_reduce(band_max[:, u:u + 1], band_p[:, u % 2, 0:w], AX.X, ALU.max,
                                      negate=True).then_inc(max_done, 1)
                dve.wait_ge(pv_done, U5 + BU * p + BU)
                dve.reciprocal(band_inv[:, :], band_sum[:, :])
                dve.drain()
                dve.tensor_tensor(att_tok[:, :, :], acc[:, 1, :].rearrange("p (u d) -> p u d", d=HD),
                                  band_inv[:, :].unsqueeze(2).to_broadcast([P, BU, HD]), ALU.mult).then_inc(att_ready, 1)
                dve.wait_ge(att_turned, p + 1)
                dve.tensor_tensor(row(y2, p), acc[:, 0, :], row(y2, p), ALU.mult)
                dve.drain().then_inc(band_gated, 1)
            end_stage(dve, 10)

        ar = Region(at_arena2, arena_end)
        at_pt = ar.at
        BLOCKS = NT * (NT + 1) // 2
        ml_pt = ar("ml_pt", [P, BLOCKS, P])
        ov = Region(at_pt, ar.at)
        ml_in = ov("ml_in", [P, 2, T + 8])
        ml_conv = ov("ml_conv", [P, 2, T])
        h_sq = Region(at_pt, ar.at)("h_sq", [P, 2 * NT, HD])
        mq_t = ar("mq_t", [P, T])
        mk_t = ar("mk_t", [P, T])
        at_mv = ar.at
        mv_t = ar("mv_t", [P, T])
        h_tok = Region(at_mv, ar.at)("h_tok", [P, 2 * NT, HD])
        mv_tok = ar("mv_tok", [P, 2 * NT, HD + 1])
        a_bc = ar("a_bc", [P, 2, T])
        den = ar("den", [P, 2 * NT])
        den_abs = ar("den_abs", [P, 2 * NT])
        ss11 = ar("ss11", [P, 2 * NT])
        root11 = ar("root11", [P, 2 * NT])
        a_diag = Region(at_ya + big + 6 * T * 4, at_ya + 2 * big)("a_diag", [P, 2, T])
        silu_mg = Region(at_pt, at_mv)("silu_mg", [P, 2, T])
        abc_loaded, adiag_done, ml_gated = sem("abc_loaded"), sem("adiag_done"), sem("ml_gated")
        ml_padded, ml_conved = sem("ml_padded"), sem("ml_conved")
        mqk_ready = sem("mqk_ready")
        d_done, pt_done = sem("d_done"), sem("pt_done")
        V10, U10 = V5 + PAIRS, U5 + PAIRS * BU
        ss_ready, root_ready, htok_ready, h_turned = sem("ss_ready"), sem("root_ready"), sem("htok_ready"), sem("h_turned")
        mg_used = sem("mg_used")
        SLOTS = HALF // (HD + 1)

        def pt_row(jb):
            at = jb * NT - jb * (jb - 1) // 2
            return ml_pt[:, at:at + NT - jb, :].rearrange("p a b -> p (a b)")

        def slot_groups():
            for g in range(0, 2 * NT, SLOTS):
                n = min(SLOTS, 2 * NT - g)
                at = g // SLOTS * HALF
                yield slice(g, g + n), n, accf[:, at:at + n * (HD + 1)].rearrange("p (u e) -> p u e", e=HD + 1)

        def sp_11(sp):
            with sp.Fori(0, PAIRS) as p:
                for i, off in enumerate((MQ, MK, MV, MO)):
                    load_w(sp, N_ML + i, cols(w_in2f, off + P * p), adv=2 * p)
            for j in range(PAIRS):
                load_w(sp, N_MG + j, cols(w_in2f, MG + P * j))

        def pool_11(pool):
            begin_stage(pool, 11)
            masked_fill = pool.to_reg(MASKED)
            pool.memset(mv_tok[:, :, HD:HD + 1], 1.0)
            with pool.Fori(0, PAIRS) as p:
                wait_here(pool, ml_gated, p + 1)
                pool.memset(ml_in[:, :, 0:3], 0.0)
                pool.drain().then_inc(ml_padded, 1)
                for r in range(2):
                    pool.dma_start(a_bc[:, r, :], ml_a_scr[bass.ds(2 * p + r, 1), :].rearrange("a t -> (a t)").partition_broadcast(P)
                                   ).then_inc(abc_loaded, 16)
                wait_here(pool, abc_loaded, 32 * p + 32)
                pool.affine_select(out=a_diag[:, :, :], in_=a_bc[:, :, :], compare_op=ALU.is_ge, fill=masked_fill, base=0,
                                   pattern=[[0, 2 * NT], [1, P]], channel_multiplier=-1).then_inc(adiag_done, 1)
            end_stage(pool, 11)

        def pe_11(pe):
            begin_stage(pe, 11)
            with pe.Fori(0, PAIRS) as p:
                pe.wait_ge(ml_gated, p + 1)
                for i in range(4):
                    project(pe, N_ML + i, ha_hi, ha_lo, adv=2 * p)

                def scores(u):
                    if u >= 2:
                        pe.wait_ge(pt_done, BU * p + u - 1)
                    r, jb = divmod(u, NT)
                    for t0 in range(jb * P, T, HALF):
                        t1 = min(T, t0 + HALF)
                        mm = pe.matmul(work[:, 2 * (1 - u % 2) + (t0 - jb * P) // HALF, 0:t1 - t0],
                                       mk_t[r * HD:(r + 1) * HD, jb * P:(jb + 1) * P],
                                       mq_t[r * HD:(r + 1) * HD, t0:t1], start=True, stop=True)
                    mm.then_inc(qk_done, 1)

                def weigh_values(u):
                    r, tb = divmod(u, NT)
                    s = 2 * tb + r
                    at = s // SLOTS * HALF + s % SLOTS * (HD + 1)
                    for jb in range(tb + 1):
                        mm = pe.matmul(accf[:, at:at + HD + 1], pt_row(jb)[:, (tb - jb) * P:(tb - jb + 1) * P],
                                       mv_tok[:, 2 * jb + r, :], start=(jb == 0), stop=(jb == tb))
                    mm.then_inc(pv_done, 1)

                pe.wait_ge(acc_free[(N_ML + 2) % 2], (N_ML + 2) // 2 + 1 + 2 * p)
                for b in range(NT):
                    mm = pe.transpose(work[:, b // 4, (b % 4) * P:(b % 4 + 1) * P], mv_t[:, b * P:(b + 1) * P], ident[:, :])
                mm.then_inc(v_turned, 1)
                pe.wait_ge(acc_free[(N_ML + 3) % 2], (N_ML + 3) // 2 + 1 + 2 * p)
                pe.wait_ge(mqk_ready, 2 * p + 2)
                scores(0)
                pe.wait_ge(v_ready, V10 + p + 1)
                scores(1)
                for u in range(BU):
                    pe.wait_ge(pt_done, BU * p + u + 1)
                    if u + 2 < BU:
                        scores(u + 2)
                    weigh_values(u)
                pe.wait_ge(htok_ready, p + 1)
                for b in range(NT):
                    mm = pe.transpose(acc[:, 0, b * P:(b + 1) * P], h_tok[:, 2 * b:2 * b + 2, :], ident[:, :])
                mm.then_inc(h_turned, 1)
            pe.wait_ge(ml_gated, PAIRS + 1)
            for j in range(PAIRS):
                project(pe, N_MG + j, ha_hi, ha_lo)
            end_stage(pe, 11)

        def act_11(act):
            begin_stage(act, 11)
            with act.Fori(0, PAIRS) as p:
                act.wait_ge(ml_gated, p + 1)
                for i in range(2):
                    n = N_ML + i
                    split_hi(act, n + 1, adv=2 * p)
                    projected(act, n, adv=2 * p)
                    act.activation(ml_in[:, i, 3:3 + T], acc[:, n % 2, :], ACT.Copy).then_inc(acc_free[n % 2], 1)
                n = N_ML + 2
                split_hi(act, n + 1, adv=2 * p)
                projected(act, n, adv=2 * p)
                act.activation(mv_t[:, :], acc[:, n % 2, :], ACT.Copy).then_inc(acc_free[n % 2], 1)
                for i, dst in enumerate((mq_t, mk_t)):
                    act.wait_ge(ml_conved, 2 * p + i + 1)
                    act.activation(dst[:, :], ml_conv[:, i, :], ACT.Silu).then_inc(mqk_ready, 1)
                act.wait_ge(v_turned, V10 + p + 1)
                act.activation(mv_tok[:, :, 0:HD], work[:, 0:2, :].rearrange("p a (b d) -> p (a b) d", d=HD),
                               ACT.Copy).then_inc(v_ready, 1)
                n = N_ML + 3
                split_hi(act, n + 1, adv=2 * p)
                projected(act, n, adv=2 * p)
                act.activation(row(y2, 3 + p), acc[:, n % 2, :], ACT.Sigmoid).then_inc(acc_free[n % 2], 1)
                act.drain()
                act.wait_ge(adiag_done, p + 1)
                for u in range(BU):
                    r, jb = divmod(u, NT)
                    if u == NT:
                        act.wait_ge(pv_done, U10 + BU * p + NT)
                    b_col = B_tok[:, jb, :][:, bass.ds(2 * p + r, 1)]
                    pt = pt_row(jb)
                    e = act.activation(pt[:, 0:P], a_diag[:, r, jb * P:(jb + 1) * P], ACT.Exp, bias=b_col)
                    if jb + 1 < NT:
                        e = act.activation(pt[:, P:], a_bc[:, r, (jb + 1) * P:], ACT.Exp, bias=b_col)
                    e.then_inc(d_done, 1)
                act.wait_ge(ss_ready, p + 1)
                act.activation(root11[:, :], ss11[:, :], ACT.Sqrt, bias=eps_col[:, :], scale=1.0 / HD).then_inc(root_ready, 1)
            for j in range(PAIRS):
                n = N_MG + j
                split_hi(act, n + 1)
                projected(act, n)
                if j >= 2:
                    act.wait_ge(mg_used, j - 1)
                act.activation(silu_mg[:, j % 2, :], acc[:, n % 2, :], ACT.Silu).then_inc(acc_free[n % 2], 1)
            end_stage(act, 11)

        def dve_11(dve):
            begin_stage(dve, 11)
            dve.drain().then_inc(ml_gated, 1)
            with dve.Fori(0, PAIRS) as p:
                split_lo(dve, N_ML + 1, adv=2 * p)
                dve.wait_ge(ml_padded, p + 1)
                for i in range(2):
                    split_lo(dve, N_ML + 2 + i, adv=2 * p)
                    dve.wait_ge(acc_free[(N_ML + i) % 2], (N_ML + i) // 2 + 1 + 2 * p)
                    conv_taps(dve, ml_conv[:, i, :], lambda k: ml_in[:, i, k:k + T],
                              lambda k: vec2[:, VEC2["conv_w_2"][0] + 2 * PAIRS * k + PAIRS * i:][:, bass.ds(p, 1)]
                              ).then_inc(ml_conved, 1)
                split_lo(dve, N_ML + 4, adv=2 * p)
                for u in range(BU):
                    dve.wait_ge(qk_done, U10 + BU * p + u + 1)
                    dve.wait_ge(d_done, BU * p + u + 1)
                    pt = pt_row(u % NT)
                    s = work[:, 2 * (1 - u % 2):2 * (1 - u % 2) + 2, :].rearrange("p a b -> p (a b)")
                    dve.scalar_tensor_tensor(pt, s[:, 0:(NT - u % NT) * P], HD_SCALE, pt, ALU.mult, ALU.mult
                                             ).then_inc(pt_done, 1)
                dve.wait_ge(pv_done, U10 + BU * p + BU)
                for us, n, out11 in slot_groups():
                    dve.tensor_copy(den[:, us], out11[:, :, HD])
                dve.drain()
                dve.scalar_tensor_tensor(den_abs[:, :], den[:, :], -1.0, den[:, :], ALU.mult, ALU.max)
                dve.drain()
                dve.tensor_tensor(den[:, :].rearrange("p (t r) -> p t r", r=2), den_abs[:, :].rearrange("p (t r) -> p t r", r=2),
                                  em_tok[:, :, bass.ds(2 * p, 2)], ALU.max)
                dve.drain()
                dve.reciprocal(den_abs[:, :], den[:, :])
                dve.drain()
                for us, n, out11 in slot_groups():
                    dve.tensor_tensor(h_tok[:, us, :], out11[:, :, 0:HD],
                                      den_abs[:, us].unsqueeze(2).to_broadcast([P, n, HD]), ALU.mult)
                dve.drain()
                dve.tensor_tensor(h_sq[:, :, :], h_tok[:, :, :], h_tok[:, :, :], ALU.mult)
                dve.drain()
                dve.tensor_reduce(ss11[:, :], h_sq[:, :, :], AX.X, ALU.add).then_inc(ss_ready, 1)
                dve.wait_ge(root_ready, p + 1)
                dve.reciprocal(den[:, :], root11[:, :])
                dve.drain()
                dve.tensor_tensor(h_tok[:, :, :], h_tok[:, :, :], den[:, :].unsqueeze(2).to_broadcast([P, 2 * NT, HD]),
                                  ALU.mult).then_inc(htok_ready, 1)
                dve.wait_ge(h_turned, p + 1)
                dve.scalar_tensor_tensor(row(y2, 3 + p), acc[:, 0, :], dcol(vec2, VEC2, "ml_norm_g_2", p), row(y2, 3 + p),
                                         ALU.mult, ALU.mult)
                dve.drain().then_inc(ml_gated, 1)
            for j in range(PAIRS):
                n = N_MG + j
                split_lo(dve, n + 1)
                dve.wait_ge(acc_free[n % 2], n // 2 + 1)
                dve.tensor_tensor(y2[:, 3 + j, :], y2[:, 3 + j, :], silu_mg[:, j % 2, :], ALU.mult).then_inc(mg_used, 1)
            end_stage(dve, 11)

        ar = Region(at_arena2, arena_end)
        gq_t = ar("gq_t", [P, T])
        gk_t = ar("gk_t", [P, T])
        gv_tok = ar("gv_tok", [P, NCHUNK, GLA_HEADS * GLA_DV])
        at_decay = ar.at
        e_b = ar("e_b", [P, T])
        e_q = ar("e_q", [P, T])
        e_end = ar("e_end", [P, T])
        silu_gg = Region(at_decay, ar.at)("silu_gg", [P, 2, T])
        e_k = ar("e_k", [P, NSUB, CHUNK])
        k_ref = ar("k_ref", [P, NSUB, CHUNK])
        q_ref = ar("q_ref", [P, CHUNK])
        q_dec = ar("q_dec", [P, CHUNK])
        k_dec = ar("k_dec", [P, CHUNK])
        k_tok = ar("k_tok", [P, P])
        att_gla = ar("att_gla", [P, GLA_HEADS, CHUNK])
        s_gla = ar("s_gla", [P, GLA_HEADS * GLA_DV])
        kv_own = ar("kv_own", [P, GLA_HEADS * GLA_DV])
        own = ar("own", [P, GLA_HEADS * GLA_DV])
        ss12 = ar("ss12", [P, NCHUNK * GLA_HEADS])
        root12 = ar("root12", [P, NCHUNK * GLA_HEADS])
        inv12 = ar("inv12", [P, NCHUNK * GLA_HEADS])
        o_sq = Region(Region(at_arena2, arena_end).at, at_decay)("o_sq", [P, NCHUNK, GLA_HEADS * GLA_DV])
        y6 = Region(at_ya + big + 6 * T * 4, at_ya + 2 * big)
        gv_t = y6("gv_t", [P, 2, T])
        o_tok = Region(at_ya + big + 6 * T * 4, at_ya + 2 * big)("o_tok", [P, NCHUNK, GLA_HEADS * GLA_DV])
        own_ready, decay_args, decays_ready = sem("own_ready"), sem("decay_args"), sem("decays_ready")
        karg_done, kexp_done, chunk_ready, kdec_ready = sem("karg_done"), sem("kexp_done"), sem("chunk_ready"), sem("kdec_ready")
        kdec_turned, ktok_ready, gkv_done = sem("kdec_turned"), sem("ktok_ready"), sem("gkv_done")
        gatt_done, gatt_masked, go_done, gstate_done, go_copied = (sem("gatt_done"), sem("gatt_masked"), sem("go_done"),
                                                                   sem("gstate_done"), sem("go_copied"))
        osq_done, ss12_ready, root12_ready, otok_ready, o_turned = (sem("osq_done"), sem("ss12_ready"), sem("root12_ready"),
                                                                    sem("otok_ready"), sem("o_turned"))
        V11 = V10 + PAIRS
        b_now = b_gla[:, :, 1:1 + CHUNK]
        b_ref = b_gla[:, :, 0:CHUNK].rearrange("p c (s t) -> p c s t", t=SUB)[:, :, :, 0:1]
        GLA_TILES = ((GQ, gq_t[:, :], float(GLA_DK) ** -0.5), (GK, gk_t[:, :], 1.0),
                     (GV, gv_t[:, 0, :], 1.0), (GV + P, gv_t[:, 1, :], 1.0))

        def at_chunk(x, c):
            return x[:, bass.ds(c * CHUNK, CHUNK)]

        def sp_12(sp):
            for i, (off, _, _) in enumerate(GLA_TILES):
                load_w(sp, N_GLA + i, cols(w_in2f, off))
            for i in range(2):
                load_w(sp, N_GG + i, cols(w_in2f, GG + i * P))

        def pool_12(pool):
            begin_stage(pool, 12)
            pool.memset(own[:, :], 0.0)
            pool.memset(s_gla[:, :], 0.0)
            pool.drain()
            for h in range(GLA_HEADS):
                pool.memset(own[h * GLA_DK:(h + 1) * GLA_DK, h * GLA_DV:(h + 1) * GLA_DV], 1.0)
                pool.drain()
            pool.drain().then_inc(own_ready, 1)
            end_stage(pool, 12)

        def pe_12(pe):
            begin_stage(pe, 12)
            for i in range(4):
                project(pe, N_GLA + i, ha_hi, ha_lo)
            for i in range(2):
                n = N_GLA + 2 + i
                pe.wait_ge(acc_free[n % 2], n // 2 + 1)
            for c in range(NCHUNK):
                for i in range(2):
                    at = c * 2 + i
                    mm = pe.transpose(work[:, at // 4, at % 4 * P:(at % 4 + 1) * P], gv_t[:, i, c * P:(c + 1) * P], ident[:, :])
            mm.then_inc(v_turned, 1)
            pe.wait_ge(v_ready, V11 + 1)
            with pe.Fori(0, NCHUNK) as c:
                pe.wait_ge(kdec_ready, c + 1)
                pe.transpose(work[:, 3, 0:P], k_dec[:, :], ident[:, :]).then_inc(kdec_turned, 1)
                pe.wait_ge(chunk_ready, c + 1)
                for h in range(GLA_HEADS):
                    d = slice(h * GLA_DK, (h + 1) * GLA_DK)
                    for s in range(NSUB):
                        t = slice(s * SUB, (s + 1) * SUB)
                        mm = pe.matmul(accf[:, h * HALF + s * SUB:h * HALF + (s + 1) * SUB], k_ref[d, s, :], q_ref[d, t],
                                       start=True, stop=True)
                mm.then_inc(gatt_done, 1)
                pe.wait_ge(ktok_ready, c + 1)
                pe.wait_ge(gstate_done, c + 1)
                pe.matmul(work[:, 2, 0:GLA_HEADS * GLA_DV], k_tok[:, :], row(gv_tok, c), start=True, stop=True
                          ).then_inc(gkv_done, 1)
                pe.wait_ge(gatt_masked, c + 1)
                pe.wait_ge(go_copied, c + 1)
                o = work[:, 1, 0:GLA_HEADS * GLA_DV]
                for h in range(GLA_HEADS):
                    v = slice(h * GLA_DV, (h + 1) * GLA_DV)
                    pe.matmul(o[:, v], q_dec[:, :], s_gla[:, v], start=True, stop=False)
                    mm = pe.matmul(o[:, v], att_gla[:, h, :], row(gv_tok, c)[:, v], start=False, stop=True)
                mm.then_inc(go_done, 1)
            for i in range(2):
                project(pe, N_GG + i, ha_hi, ha_lo)
            pe.wait_ge(otok_ready, 1)
            for i in range(2):
                for c in range(NCHUNK):
                    mm = pe.transpose(work[:, 2 * i + c // 4, c % 4 * P:(c % 4 + 1) * P], o_tok[:, c, i * P:(i + 1) * P], ident[:, :])
            mm.then_inc(o_turned, 1)
            end_stage(pe, 12)

        def act_12(act):
            begin_stage(act, 12)
            act.drain().then_inc(go_copied, 1)
            for i, (_, dst, scale) in enumerate(GLA_TILES):
                n = N_GLA + i
                split_hi(act, n + 1)
                projected(act, n)
                act.activation(dst, acc[:, n % 2, :], ACT.Copy, scale=scale).then_inc(acc_free[n % 2], 1)
            act.wait_ge(v_turned, V11 + 1)
            act.activation(gv_tok[:, :, :], work[:, :, :], ACT.Copy).then_inc(v_ready, 1)
            act.activation(e_b[:, :].rearrange("p (c t) -> p c t", t=CHUNK), b_now, ACT.Exp)
            act.wait_ge(decay_args, 2)
            act.activation(e_q[:, :], e_q[:, :], ACT.Exp)
            act.activation(e_end[:, :], e_end[:, :], ACT.Exp)
            act.drain().then_inc(decays_ready, 1)
            with act.Fori(0, NCHUNK) as c:
                act.wait_ge(karg_done, c + 1)
                act.activation(e_k[:, :, :], e_k[:, :, :], ACT.Exp).then_inc(kexp_done, 1)
                act.wait_ge(kdec_turned, c + 1)
                act.activation(k_tok[:, :], work[:, 3, 0:P], ACT.Copy).then_inc(ktok_ready, 1)
                act.wait_ge(go_done, c + 1)
                act.activation(row(o_tok, c), work[:, 1, 0:GLA_HEADS * GLA_DV], ACT.Copy).then_inc(go_copied, 1)
            act.drain()
            act.activation(o_sq[:, :, :], o_tok[:, :, :], ACT.Square).then_inc(osq_done, 1)
            split_hi(act, N_GG + 1)
            act.wait_ge(ss12_ready, 1)
            act.activation(root12[:, :], ss12[:, :], ACT.Sqrt, bias=eps_col[:, :], scale=1.0 / GLA_DV).then_inc(root12_ready, 1)
            for i in range(2):
                n = N_GG + i
                if i == 1:
                    split_hi(act, n + 1)
                projected(act, n)
                act.activation(silu_gg[:, i, :], acc[:, n % 2, :], ACT.Silu).then_inc(acc_free[n % 2], 1)
            end_stage(act, 12)

        def dve_12(dve):
            begin_stage(dve, 12)
            dve.drain().then_inc(gstate_done, 1)
            for i in range(4):
                split_lo(dve, N_GLA + i + 1)
            sub = dict(t=SUB)
            dve.tensor_tensor(e_q[:, :].rearrange("p (c s t) -> p c s t", s=NSUB, **sub), b_now.rearrange("p c (s t) -> p c s t", **sub),
                              b_ref.to_broadcast([P, NCHUNK, NSUB, SUB]), ALU.subtract).then_inc(decay_args, 1)
            dve.tensor_tensor(e_end[:, :].rearrange("p (c t) -> p c t", t=CHUNK), b_gla[:, :, CHUNK:CHUNK + 1].to_broadcast([P, NCHUNK, CHUNK]),
                              b_now, ALU.subtract).then_inc(decay_args, 1)
            dve.wait_ge(own_ready, 1)
            dve.wait_ge(decays_ready, 1)
            with dve.Fori(0, NCHUNK) as c:
                b_c = b_gla[:, bass.ds(c, 1), :].rearrange("p a t -> p (a t)")
                r_c = b_c[:, 0:CHUNK].rearrange("p (s t) -> p s t", t=SUB)[:, :, 0:1]
                dve.tensor_tensor(e_k[:, :, :], r_c.to_broadcast([P, NSUB, CHUNK]),
                                  b_c[:, 1:1 + CHUNK].unsqueeze(1).to_broadcast([P, NSUB, CHUNK]), ALU.subtract).then_inc(karg_done, 1)
                dve.tensor_tensor(k_dec[:, :], at_chunk(gk_t, c), at_chunk(e_end, c), ALU.mult).then_inc(kdec_ready, 1)
                dve.tensor_tensor(q_ref[:, :], at_chunk(gq_t, c), at_chunk(e_q, c), ALU.mult)
                dve.tensor_tensor(q_dec[:, :], at_chunk(gq_t, c), at_chunk(e_b, c), ALU.mult)
                dve.wait_ge(kexp_done, c + 1)
                dve.scalar_tensor_tensor(k_ref[:, :, :], e_k[:, :, :], KEY_CAP, at_chunk(gk_t, c).unsqueeze(1).to_broadcast([P, NSUB, CHUNK]),
                                         ALU.min, ALU.mult)
                dve.drain().then_inc(chunk_ready, 1)
                dve.wait_ge(gatt_done, c + 1)
                dve.tensor_tensor(att_gla[:, :, :], accf.rearrange("p (h t) -> p h t", t=HALF)[:, :, 0:CHUNK],
                                  causal01[:, :].unsqueeze(1).to_broadcast([P, GLA_HEADS, CHUNK]), ALU.mult).then_inc(gatt_masked, 1)
                dve.wait_ge(gkv_done, c + 1)
                dve.tensor_tensor(kv_own[:, :], work[:, 2, 0:GLA_HEADS * GLA_DV], own[:, :], ALU.mult)
                dve.drain()
                dve.wait_ge(go_done, c + 1)
                dve.scalar_tensor_tensor(s_gla[:, :], s_gla[:, :], at_chunk(e_b, c)[:, CHUNK - 1:CHUNK], kv_own[:, :],
                                         ALU.mult, ALU.add)
                dve.drain().then_inc(gstate_done, 1)
            split_lo(dve, N_GG + 1)
            dve.wait_ge(osq_done, 1)
            heads = dict(d=GLA_DV)
            dve.tensor_reduce(ss12[:, :], o_sq[:, :, :].rearrange("p c (h d) -> p (c h) d", **heads), AX.X, ALU.add).then_inc(ss12_ready, 1)
            dve.wait_ge(root12_ready, 1)
            dve.reciprocal(inv12[:, :], root12[:, :])
            dve.drain()
            o_h = o_tok[:, :, :].rearrange("p c (h d) -> p (c h) d", **heads)
            dve.tensor_tensor(o_h, o_h, inv12[:, :].unsqueeze(2).to_broadcast([P, NCHUNK * GLA_HEADS, GLA_DV]), ALU.mult
                              ).then_inc(otok_ready, 1)
            split_lo(dve, N_GG + 2)
            dve.wait_ge(o_turned, 1)
            for i in range(2):
                n = N_GG + i
                dve.wait_ge(acc_free[n % 2], n // 2 + 1)
                g_col = vec2[:, VEC2["gla_norm_g_2"][0] + i:][:, 0:1]
                dve.scalar_tensor_tensor(y2[:, 6 + i, :], work[:, 2 * i:2 * i + 2, :].rearrange("p a b -> p (a b)"), g_col,
                                         silu_gg[:, i, :], ALU.mult, ALU.mult)
            end_stage(dve, 12)

        y2_hi, y2_split = sem("y2_hi"), sem("y2_split")

        def sp_13(sp):
            with sp.Fori(0, 4) as j:
                for b in range(2):
                    load_w(sp, N_OUT2 + b, cols(io["w_out_2"].rearrange("a e d -> (a e) d"), b * P + 2 * P * j), adv=j)

        def pool_13(pool):
            begin_stage(pool, 13)
            pool.dma_start(final_g[:, :], io["final_g_2"].partition_broadcast(P)).then_inc(g_loaded, 16)
            end_stage(pool, 13)

        def pe_13(pe):
            begin_stage(pe, 13)
            pe.wait_ge(y2_split, KT)
            with pe.Fori(0, 4) as j:
                for b in range(2):
                    project(pe, N_OUT2 + b, ha_hi, ha_lo, adv=j)
            end_stage(pe, 13)

        def act_13(act):
            begin_stage(act, 13)
            for k in range(KT):
                act.activation(ha_hi[:, k, :], y2[:, k, :], ACT.Copy).then_inc(y2_hi, 1)
            with act.Fori(0, 3) as j:
                for b in range(2):
                    split_hi(act, N_OUT2 + b + 1, adv=j)
            split_hi(act, N_TILES - 1)
            end_stage(act, 13)

        def dve_13(dve):
            begin_stage(dve, 13)
            for k in range(KT):
                dve.wait_ge(y2_hi, k + 1)
                dve.tensor_tensor(ha_lo[:, k, :], y2[:, k, :], ha_hi[:, k, :].bitcast(F32), ALU.subtract).then_inc(y2_split, 1)

            def add_residual(n, x, adv=0):
                projected(dve, n, adv=adv)
                dve.tensor_tensor(x, acc[:, n % 2, :], x, ALU.add).then_inc(acc_free[n % 2], 1)

            with dve.Fori(0, 3) as j:
                for b in range(2):
                    split_lo(dve, N_OUT2 + b + 1, adv=j)
                    add_residual(N_OUT2 + b, row(x1, 2 * j + b), adv=j)
            split_lo(dve, N_TILES - 1)
            add_residual(N_TILES - 2, x1[:, KT - 2, :])
            add_residual(N_TILES - 1, x1[:, KT - 1, :])
            end_stage(dve, 13)

        ar = Region(at_arena, arena_end)
        final_g = ar("final_g", [P, D])
        x2_sq = ar("x2_sq", [P, 2, D])
        ss14 = ar("ss14", [P, NT])
        root14 = ar("root14", [P, NT])
        inv14 = ar("inv14", [P, NT])
        out_tok = Region(at_ya + big, at_ya + 2 * big)("out_tok", [P, NT, D])
        g_loaded, x2_turned, x2_rooted, out_ready, stored = (sem("g_loaded"), sem("x2_turned"),
                                                                        sem("x2_rooted"), sem("out_ready"), sem("stored"))
        banks14 = [acc[:, 0, :], acc[:, 1, :], work[:, 0:2, :].rearrange("p a b -> p (a b)"),
                   work[:, 2:4, :].rearrange("p a b -> p (a b)")]

        def sp_14(sp):
            dst = out.rearrange("a (t p) d -> p (a t) d", p=P)
            for i in range(NT):
                sp.wait_ge(out_ready, i + 1)
                sp.dma_start(dst[:, i, :], out_tok[:, i, :]).then_inc(stored, 16)
            sp.wait_ge(stored, 16 * NT)

        def pool_14(pool):
            begin_stage(pool, 14)
            end_stage(pool, 14)

        def pe_14(pe):
            begin_stage(pe, 14)
            for i in range(NT):
                if i >= 4:
                    pe.wait_ge(out_ready, i - 3)
                for f in range(KT):
                    mm = pe.transpose(banks14[i % 4][:, f * P:(f + 1) * P], x1[:, f, i * P:(i + 1) * P], ident[:, :])
                mm.then_inc(x2_turned, 1)
            end_stage(pe, 14)

        def act_14(act):
            begin_stage(act, 14)
            for i in range(NT):
                act.wait_ge(x2_turned, i + 1)
                act.activation(x2_sq[:, i % 2, :], banks14[i % 4], ACT.Square, accum_out=ss14[:, i:i + 1])
                act.drain()
                act.activation(root14[:, i:i + 1], ss14[:, i:i + 1], ACT.Sqrt, bias=eps_col[:, :], scale=1.0 / D).then_inc(x2_rooted, 1)
            end_stage(act, 14)

        def dve_14(dve):
            begin_stage(dve, 14)
            dve.wait_ge(g_loaded, 16)
            for i in range(NT):
                dve.wait_ge(x2_rooted, i + 1)
                dve.reciprocal(inv14[:, i:i + 1], root14[:, i:i + 1])
                dve.drain()
                dve.scalar_tensor_tensor(out_tok[:, i, :], banks14[i % 4], inv14[:, i:i + 1], final_g[:, :],
                                         ALU.mult, ALU.mult).then_inc(out_ready, 1)
            end_stage(dve, 14)

        block = ctx.enter_context(nc.Block())

        @block.sync
        def _(sp):
            sp_0(sp)
            sp_1(sp)
            sp_2(sp)
            sp_3(sp)
            sp_4(sp)
            sp_5(sp)
            sp_6(sp)
            sp_7(sp)
            sp_8(sp)
            sp_9(sp)
            sp_10(sp)
            sp_11(sp)
            sp_12(sp)
            sp_13(sp)
            sp_14(sp)

        @block.scalar
        def _(act):
            act_0(act)
            act_1(act)
            act_2(act)
            act_3(act)
            act_4(act)
            act_5(act)
            act_6(act)
            act_7(act)
            act_8(act)
            act_9(act)
            act_10(act)
            act_11(act)
            act_12(act)
            act_13(act)
            act_14(act)

        @block.tensor
        def _(pe):
            pe_0(pe)
            pe_1(pe)
            pe_2(pe)
            pe_3(pe)
            pe_4(pe)
            pe_5(pe)
            pe_6(pe)
            pe_7(pe)
            pe_8(pe)
            pe_9(pe)
            pe_10(pe)
            pe_11(pe)
            pe_12(pe)
            pe_13(pe)
            pe_14(pe)

        @block.vector
        def _(dve):
            dve_0(dve)
            dve_1(dve)
            dve_2(dve)
            dve_3(dve)
            dve_4(dve)
            dve_5(dve)
            dve_6(dve)
            dve_7(dve)
            dve_8(dve)
            dve_9(dve)
            dve_10(dve)
            dve_11(dve)
            dve_12(dve)
            dve_13(dve)
            dve_14(dve)

        @block.gpsimd
        def _(pool):
            pool_0(pool)
            pool_1(pool)
            pool_2(pool)
            pool_3(pool)
            pool_4(pool)
            pool_5(pool)
            pool_6(pool)
            pool_7(pool)
            pool_8(pool)
            pool_9(pool)
            pool_10(pool)
            pool_11(pool)
            pool_12(pool)
            pool_13(pool)
            pool_14(pool)


_INS = ["x", "c", "w_ada", "b_ada", "norm_w", "w_in", "conv_w", "conv_b", "dt_bias", "a_log", "d_skip",
        "ssm_norm_w", "b_f", "b_gate", "w_proj_ssm", "w_proj_att", "w_out", "final_norm_w", "norm_g_2",
        "w_in_2", "b_gates_2", "conv_w_2", "w_alpha_2", "b_alpha_2", "rel_bias_2", "ml_norm_g_2",
        "gla_norm_g_2", "w_out_2", "final_g_2"]


def kernel(**inputs):
    import numpy as np
    import concourse.bacc as bacc
    from concourse.bass_utils import run_bass_kernel_spmd

    arrays = {name: np.ascontiguousarray(inputs[name]) for name in _INS}
    arrays["rel_bias_2"] = np.ascontiguousarray(arrays["rel_bias_2"][:, :, ::-1])
    nc = bacc.Bacc("TRN2", target_bir_lowering=False, num_devices=1)
    io = {name: nc.dram_tensor(f"in_{name}", a.shape, F32, kind="ExternalInput").ap() for name, a in arrays.items()}
    out = nc.dram_tensor("out", [1, T, D], F32, kind="ExternalOutput").ap()
    build(nc, io, out)
    r = run_bass_kernel_spmd(nc, [{f"in_{name}": a for name, a in arrays.items()}], core_ids=[0])
    return r.results[0]["out"]
```

```python
from contextlib import ExitStack

import concourse.bass as bass
from concourse import mybir

F32 = mybir.dt.float32
F32R = mybir.dt.float32r
ALU = mybir.AluOpType
ACT = mybir.ActivationFunctionType
AX = mybir.AxisListType

P = 128
T = 1024
D = 1024
KT = D // P
NT = T // P
HALF = 512
EPS = 1e-6
MASKED = -1e30

SSM_HEADS, SSM_P, SSM_N, SSM_G = 16, 64, 64, 2
HPG = SSM_HEADS // SSM_G
CHUNK = 128
NCHUNK = T // CHUNK
CONV_K = 4
XBC_TILES = (SSM_HEADS * SSM_P + 2 * SSM_G * SSM_N) // P
FOX_HEADS, FOX_D = 8, 128
Z_OFF = 0
XBC_OFF = D
DT_OFF = XBC_OFF + XBC_TILES * P
Q_OFF = DT_OFF + SSM_HEADS
K_OFF, V_OFF, ZA_OFF = Q_OFF + D, Q_OFF + 2 * D, Q_OFF + 3 * D
F_OFF = Q_OFF + 4 * D
G_OFF = F_OFF + FOX_HEADS

PAIRS = 3
HD = 64
W2 = PAIRS * P
AQ, AK, AV, AG = 0, W2, 2 * W2, 3 * W2
MQ, MK, MV, MO = 4 * W2, 5 * W2, 6 * W2, 7 * W2
ML_HEADS = 6
MI, MF = 8 * W2, 8 * W2 + ML_HEADS
MG = MF + ML_HEADS
GLA_HEADS, GLA_DK, GLA_DV, GLA_RANK = 4, 32, 64, 16
GQ = MG + W2
GK, GV = GQ + P, GQ + 2 * P
GA = GV + 2 * P
GG = GA + GLA_RANK
GLA_TAU = 16.0
SUB = 16
NSUB = CHUNK // SUB
KEY_CAP = 1e30
BAND_TILES = 5
BANDW = BAND_TILES * P
REL = 128

VEC1 = {}
VEC2 = {}


def _count(table, sizes):
    at = 0
    for name, rows in sizes:
        table[name] = (at, at + rows)
        at += rows
    return at


NVEC1 = _count(VEC1, [("b_ada", 24), ("norm_w", 8), ("conv_w", CONV_K * XBC_TILES), ("conv_b", XBC_TILES),
                      ("ssm_norm_w", 8), ("b_gate", 16), ("final_norm_w", 8), ("c", 8)])
NVEC2 = _count(VEC2, [("norm_g_2", 8), ("conv_w_2", CONV_K * 2 * PAIRS), ("b_alpha_2", 1), ("final_g_2", 8),
                      ("ml_norm_g_2", PAIRS), ("gla_norm_g_2", 2)])

N_SMALL1 = 0
N_XBC = 1
N_Z = N_XBC + XBC_TILES
N_GATT = N_Z + 16
N_MIX1 = N_GATT + 8
N_FOX = N_MIX1 + 8
N_MIX2 = N_FOX + 4 * FOX_HEADS
N_OUT1 = N_MIX2 + 8
N_SMALL2 = N_OUT1 + 8
N_MG = N_SMALL2 + 1
N_GG = N_MG + PAIRS
N_BAND = N_GG + 2
N_ML = N_BAND + 4 * PAIRS
N_GLA = N_ML + 4 * PAIRS
N_OUT2 = N_GLA + 4
N_TILES = N_OUT2 + 8


def build(nc, io, out):
    ctx = ExitStack()
    with ctx:
        def psum(name, shape):
            return ctx.enter_context(nc.psum_tensor(name, shape, F32))

        def sem(name):
            return ctx.enter_context(nc.semaphore(name))

        def scratch(name, shape):
            return nc.dram_tensor(name, shape, F32, kind="Internal").ap()

        base = (nc.sbuf_base + 63) // 64 * 64
        big = KT * T * 4
        at_ha, at_ya = base, base + 2 * big
        at_ring = at_ya + 2 * big
        tile_bytes = KT * P * 4
        at_const = at_ring + 6 * tile_bytes
        at_arena = at_const + 5248
        arena_end = nc.sbuf_usable_end

        class Region:

            def __init__(self, at, end):
                self.at, self.end = at, end

            def __call__(self, name, shape, dt=F32):
                size = 4
                for s in shape[1:]:
                    size *= s
                t = nc.alloc_sbuf_tensor_at(name, shape, dt, offset=self.at)
                self.at += (size + 31) // 32 * 32
                assert self.at <= self.end, (name, self.at, self.end)
                return t

        def arena():
            return Region(at_arena, arena_end)

        def ya_region():
            return Region(at_ya, at_ya + 2 * big)

        ha = Region(at_ha, at_ya)
        ha_hi = ha("ha_hi", [P, KT, T], F32R)
        ha_lo = ha("ha_lo", [P, KT, T], F32R)
        ya = ya_region()
        ya_hi = ya("ya_hi", [P, KT, T], F32R)
        ya_lo = ya("ya_lo", [P, KT, T], F32R)
        rg = Region(at_ring, at_const)
        w_raw = rg("w_raw", [P, 2, KT, P])
        w_hi = rg("w_hi", [P, 2, KT, P], F32R)
        w_lo = rg("w_lo", [P, 2, KT, P], F32R)

        cst = Region(at_const, at_arena)
        ident = cst("ident", [P, P])
        ones = cst("ones", [P, P])
        causal01 = cst("causal01", [P, P])
        vec1 = cst("vec1", [P, NVEC1])
        vec2 = cst("vec2", [P, NVEC2])
        ada = cst("ada", [P, 24])
        a1 = cst("a1", [P, 8])
        silu_c = cst("silu_c", [P, 8])
        dskip = cst("dskip", [P, 8])
        zero_col = cst("zero_col", [P, 1])
        eps_col = cst("eps_col", [P, 1])
        sp_bias = cst("sp_bias", [64, 1])
        sp_sign = cst("sp_sign", [64, 1])
        neg_a = cst("neg_a", [SSM_HEADS, 1])
        gate_bias2 = cst("gate_bias2", [64, 1])
        w_alpha = cst("w_alpha", [P, P])

        def col1(name, i=0):
            return vec1[:, VEC1[name][0] + i:VEC1[name][0] + i + 1]

        def row(x, i):
            return x[:, bass.ds(i, 1), :].rearrange("p a t -> p (a t)")

        def dcol(vec, table, name, i):
            return vec[:, table[name][0]:table[name][1]][:, bass.ds(i, 1)]

        acc = psum("acc", [P, 2, 2 * HALF])
        work = psum("work", [P, 4, HALF])
        accf = acc[:, :, :].rearrange("p a b -> p (a b)")

        xt_scr = scratch("xt_scr", [P, KT, T])
        x1_scr = scratch("x1_scr", [P, KT, T])
        merged_scr = scratch("merged_scr", [P, KT, T])
        z_scr = scratch("z_scr", [P, KT, T])
        g_scr = scratch("g_scr", [P, KT, T])
        ga_scr = scratch("ga_scr", [P, KT, T])
        acs_scr = scratch("acs_scr", [SSM_HEADS, T])
        fcum_scr = scratch("fcum_scr", [FOX_HEADS, T])
        ml_a_scr = scratch("ml_a_scr", [8, T])
        skew_scr = scratch("skew_scr", [P * 3 * P])
        bias_scr = scratch("bias_scr", [ML_HEADS, P, BANDW])

        w_loaded = [sem("w_loaded0"), sem("w_loaded1")]
        w_part = sem("w_part")
        hi_done = sem("hi_done")
        lo_done = sem("lo_done")
        mm_done = sem("mm_done")
        acc_free = [sem("acc_free0"), sem("acc_free1")]
        SPLITS = {0: 0, 3: KT, 5: 2 * KT, 7: 3 * KT, 8: 4 * KT, 13: 5 * KT}
        x_hi_done = sem("x_hi_done")
        LO_SPLITS = {0: 0, 7: KT, 13: 2 * KT}
        x_lo_done = sem("x_lo_done")
        half_done = sem("half_done")
        fill_free = sem("fill_free")
        stage_done = sem("stage_done")

        def end_stage(eng, i):
            eng.drain().then_inc(stage_done, 1)

        def begin_stage(eng, i):
            eng.wait_ge(stage_done, 4 * i)

        ticks = {}

        def wait_here(eng, s, value):
            eng.wait_ge(s, value)
            if eng not in ticks:
                ticks[eng] = sem(f"tick{len(ticks)}")
            eng.sem_inc(ticks[eng], 1)

        def load_w(sp, n, src, adv=0):
            if n >= 2:
                wait_here(sp, lo_done, n - 1 + 2 * adv)
            sp.dma_start(w_raw[:, n % 2, :, :], src).then_inc(w_loaded[n % 2], 16)

        def split_hi(act, n, adv=0):
            act.wait_ge(w_loaded[n % 2], 16 * (n // 2 + 1) + 16 * adv)
            if n >= 2:
                act.wait_ge(mm_done, n - 1 + 2 * adv)
            act.activation(w_hi[:, n % 2, :, :], w_raw[:, n % 2, :, :], ACT.Copy).then_inc(hi_done, 1)

        def split_lo(dve, n, adv=0):
            dve.wait_ge(hi_done, n + 1 + 2 * adv)
            dve.tensor_tensor(w_lo[:, n % 2, :, :], w_raw[:, n % 2, :, :],
                              w_hi[:, n % 2, :, :].bitcast(F32), ALU.subtract).then_inc(lo_done, 1)

        def project(pe, n, x_hi, x_lo, adv=0):
            pe.wait_ge(lo_done, n + 1 + 2 * adv)
            if n >= 2:
                pe.wait_ge(acc_free[n % 2], n // 2 + adv)
            for k in range(KT):
                passes = [(w_hi, x_hi), (w_hi, x_lo), (w_lo, x_hi)]
                for i, (w, x) in enumerate(passes):
                    for h in range(2):
                        mm = pe.matmul(acc[:, n % 2, h * HALF:(h + 1) * HALF], w[:, n % 2, k, :],
                                       x[:, k, h * HALF:(h + 1) * HALF],
                                       start=(k == 0 and i == 0), stop=(k == KT - 1 and i == 2))
            mm.then_inc(mm_done, 1)

        def project_part(pe, n, part, m, adv=0):
            half, kpart = divmod(part, 2)
            if part == 0:
                pe.wait_ge(lo_done, n + 1 + 2 * adv)
            if kpart == 0:
                pe.wait_ge(fill_free, 2 * m + half + 1)
            for k in range(kpart * KT // 2, (kpart + 1) * KT // 2):
                passes = [(w_hi, ha_hi), (w_hi, ha_lo), (w_lo, ha_hi)]
                for i, (w, x) in enumerate(passes):
                    mm = pe.matmul(acc[:, 0, half * HALF:(half + 1) * HALF], w[:, n % 2, k, :],
                                   x[:, k, half * HALF:(half + 1) * HALF],
                                   start=(k == 0 and i == 0), stop=(k == KT - 1 and i == 2))
            if kpart:
                mm.then_inc(mm_done if half else half_done, 1)

        def read_half(act, n, half, m, dst, adv=0):
            if half:
                projected(act, n, adv=adv)
            else:
                act.wait_ge(half_done, m + 1)
            s = slice(half * HALF, (half + 1) * HALF)
            return act.activation(dst[:, s], acc[:, 0, s], ACT.Copy).then_inc(fill_free, 1)

        def projected(eng, n, adv=0):
            eng.wait_ge(mm_done, n + 1 + 2 * adv)

        def cols(w, off, width=P):
            return w.rearrange("(k p) c -> p k c", p=P)[:, :, bass.ds(off, width)]

        w_in, w_in2 = io["w_in"], io["w_in_2"]

        class Norm:
            squared = sem("norm_squared")
            summed = sem("norm_summed")
            rooted = sem("norm_rooted")

            def __init__(self, use):
                self.use = use
                self.tiles = use * KT

            def act(self, act, x, sq, root):
                for f in range(KT):
                    if f >= 2:
                        act.wait_ge(self.summed, self.tiles + f - 1)
                    act.activation(sq[:, f % 2, :], x[:, f, :], ACT.Square).then_inc(self.squared, 1)
                self.act_root(act, root)

            def act_root(self, act, root):
                act.wait_ge(self.summed, self.tiles + KT)
                act.activation(root[:, :], work[:, 0:2, :], ACT.Sqrt,
                               bias=eps_col[:, :], scale=1.0 / D).then_inc(self.rooted, 1)

            def pe(self, pe, sq_of):
                for f in range(KT):
                    pe.wait_ge(self.squared, self.tiles + f + 1)
                    for h in range(2):
                        mm = pe.matmul(work[:, h, :], ones[:, :], sq_of(f)[:, h * HALF:(h + 1) * HALF],
                                       start=(f == 0), stop=(f == KT - 1))
                    mm.then_inc(self.summed, 1)

            def dve(self, dve, root, rstd):
                dve.wait_ge(self.rooted, self.use + 1)
                dve.reciprocal(rstd[:, :], root[:, :])

        class Softplus:
            ready = sem("softplus_u_ready")
            exped = sem("softplus_exped")

            def __init__(self, use):
                self.use = use

            def act(self, act, u, e, relu):
                act.wait_ge(self.ready, self.use + 1)
                act.activation(e, u, ACT.Abs)
                act.activation(relu, u, ACT.Relu)
                act.drain()
                act.activation(e, e, ACT.Exp, scale=-1.0).then_inc(self.exped, 1)

            def dve_ratio(self, dve, e, s, s2):
                dve.wait_ge(self.exped, self.use + 1)
                dve.tensor_scalar(s, e, 2.0, None, ALU.add)
                dve.drain()
                dve.reciprocal(s2, s)
                dve.drain()
                dve.tensor_tensor(s, e, s2, ALU.mult)
                dve.drain()
                dve.tensor_tensor(s2, s, s, ALU.mult)
                dve.drain()

            def dve_series(self, dve, relu, s, s2, p):
                dve.tensor_scalar(p, s2, 1.0 / 15, None, ALU.mult)
                for c in (13, 11, 9, 7, 5, 3):
                    dve.drain()
                    dve.scalar_tensor_tensor(p, p, 1.0 / c, s2, ALU.add, ALU.mult)
                dve.drain()
                dve.scalar_tensor_tensor(p, p, 1.0, s, ALU.add, ALU.mult)
                dve.drain()
                dve.scalar_tensor_tensor(p, p, 2.0, relu, ALU.mult, ALU.add)

        ar = arena()
        x_tok = ar("x_tok", [P, NT, D])
        sq0 = ar("sq0", [P, 2, T])
        rstd0 = ar("rstd0", [P, T])
        v0 = ar("v0", [P, 1, T])
        root0 = Region(at_arena, arena_end)("root0", [P, T])
        v0b = Region(at_arena + 4096, arena_end)("v0b", [P, 2, T])
        xt = Region(at_ya, at_ya + big)("xt", [P, KT, T])
        w_ada = Region(at_ha, at_ha + 3 * big + big)("w_ada_lo", [P, 5, 3 * D])
        w_ada_b = Region(at_ya + big, at_ya + 2 * big)("w_ada_hi", [P, 2, 3 * D])
        w_ada_c = Region(at_arena, arena_end)("w_ada_last", [P, 1, 3 * D])
        rows1 = Region(at_ya + big + 24576, at_ya + 2 * big)("rows1", [P, P])
        rows2 = Region(at_ya + big + 25088, at_ya + 2 * big)("rows2", [P, P])

        x_loaded = [sem(f"x_loaded{i}") for i in range(4)]
        vec_loaded, col_loaded, ada_loaded = sem("vec_loaded"), sem("col_loaded"), sem("ada_loaded")
        ada_last = sem("ada_last")
        consts = sem("consts")
        zeroed = sem("zeroed")
        vec_turned, vec_ready = sem("vec_turned"), sem("vec_ready")
        xt_turned = sem("xt_turned")
        xt_act, xt_dve = sem("xt_act"), sem("xt_dve")
        silu_c_done, ada_mul = sem("silu_c_done"), sem("ada_mul")
        xt_saved = sem("xt_saved")
        norm0 = Norm(0)
        v0_scaled, v0_shifted = sem("v0_scaled"), sem("v0_shifted")

        def vec_sources():
            v1 = [("b_ada", io["b_ada"]), ("norm_w", io["norm_w"]),
                  ("conv_w", io["conv_w"].rearrange("j c -> (j c)")), ("conv_b", io["conv_b"]),
                  ("ssm_norm_w", io["ssm_norm_w"]), ("b_gate", io["b_gate"]),
                  ("final_norm_w", io["final_norm_w"]), ("c", io["c"].rearrange("a d -> (a d)"))]
            v2 = [("norm_g_2", io["norm_g_2"].rearrange("a d -> (a d)")),
                  ("conv_w_2", io["conv_w_2"].rearrange("a j c -> (a j c)")),
                  ("b_alpha_2", io["b_alpha_2"].rearrange("a d -> (a d)")), ("final_g_2", io["final_g_2"]),
                  ("ml_norm_g_2", io["ml_norm_g_2"].rearrange("a d -> (a d)")),
                  ("gla_norm_g_2", io["gla_norm_g_2"].rearrange("a d -> (a d)"))]
            for rows, table, vs in ((rows1, VEC1, v1), (rows2, VEC2, v2)):
                for name, src in vs:
                    a, b = table[name]
                    yield rows[a:b, :], src.rearrange("(r p) -> r p", p=P)

        VECS = len(VEC1) + len(VEC2)

        def sp_0(sp):
            x = io["x"].rearrange("a (t p) d -> p (a t) d", p=P)
            for i in range(NT):
                sp.dma_start(x_tok[:, i, :], x[:, i, :]).then_inc(x_loaded[i // 2], 16)
            wa = io["w_ada"].rearrange("(k p) c -> p k c", p=P)
            for k in range(5):
                sp.dma_start(w_ada[:, k, :], wa[:, k, :]).then_inc(ada_loaded, 16)
            for k in range(2):
                sp.dma_start(w_ada_b[:, k, :], wa[:, 5 + k, :]).then_inc(ada_loaded, 16)
            sp.wait_ge(xt_turned, 2 * NT)
            sp.dma_start(w_ada_c[:, 0, :], wa[:, 7, :]).then_inc(ada_last, 16)
            sp.dma_start(w_raw[:, 0, :, 0:32], cols(w_in, DT_OFF, 32)).then_inc(w_loaded[0], 16)
            sp.dma_start(w_raw[:, 0, :, 32:P], cols(w_in, F_OFF, P - 32)).then_inc(w_part, 16)
            load_w(sp, N_XBC, cols(w_in, XBC_OFF))
            sp.wait_ge(xt_act, NT)
            sp.wait_ge(xt_dve, NT)
            sp.dma_start(xt_scr, xt[:, :, :]).then_inc(xt_saved, 16)

        def act_0(act):
            for dst, src in vec_sources():
                act.dma_start(dst, src).then_inc(vec_loaded, 16)
            act.wait_ge(zeroed, 1)
            act.dma_start(sp_bias[0:SSM_HEADS, :], io["dt_bias"].rearrange("(h a) -> h a", a=1)).then_inc(col_loaded, 16)
            act.dma_start(sp_bias[32:32 + FOX_HEADS, :], io["b_f"].rearrange("(h a) -> h a", a=1)).then_inc(col_loaded, 16)
            act.dma_start(neg_a[:, :], io["a_log"].rearrange("(h a) -> h a", a=1)).then_inc(col_loaded, 16)
            bg = io["b_gates_2"].rearrange("a (h b) -> (a h) b", b=1)
            act.dma_start(gate_bias2[0:ML_HEADS, :], bg[0:ML_HEADS, :]).then_inc(col_loaded, 16)
            act.dma_start(gate_bias2[32:32 + ML_HEADS, :], bg[ML_HEADS:2 * ML_HEADS, :]).then_inc(col_loaded, 16)
            act.dma_start(w_alpha[64:64 + GLA_RANK, :], io["w_alpha_2"].rearrange("a r k -> (a r) k")).then_inc(col_loaded, 16)
            for w in range(2):
                ds = io["d_skip"].rearrange("(t w) -> w t", w=2)[w, :]
                act.dma_start(dskip[64 * w:64 * w + 64, :], ds.partition_broadcast(64),
                              allow_slow_non_contiguous=True).then_inc(col_loaded, 16)
            act.wait_ge(vec_turned, 1)
            act.activation(vec1[:, :], work[:, 0, 0:NVEC1], ACT.Copy)
            act.activation(vec2[:, :], work[:, 1, 0:NVEC2], ACT.Copy).then_inc(vec_ready, 1)
            act.drain()
            act.activation(silu_c[:, :], vec1[:, VEC1["c"][0]:VEC1["c"][1]], ACT.Silu).then_inc(silu_c_done, 1)
            act.wait_ge(col_loaded, 16 * 8)
            act.activation(neg_a[:, :], neg_a[:, :], ACT.Exp)
            act.drain()
            act.activation(neg_a[:, :], neg_a[:, :], ACT.Copy, scale=-1.0)
            for i in range(NT):
                act.wait_ge(xt_turned, 2 * i + 1)
                act.activation(xt[:, 0:4, i * P:(i + 1) * P], acc[:, i % 2, 0:HALF], ACT.Copy).then_inc(xt_act, 1)
            act.drain()
            act.wait_ge(xt_dve, NT)
            norm0.act(act, xt, sq0, root0)
            act.wait_ge(w_part, 16)
            split_hi(act, 0)
            for f in range(KT):
                act.wait_ge(v0_scaled, f + 1)
                if f >= 2:
                    act.wait_ge(x_lo_done, f - 1)
                act.activation(v0b[:, f % 2, :], v0[:, 0, :], ACT.Identity, bias=ada[:, f:f + 1]).then_inc(v0_shifted, 1)
                act.drain()
                act.activation(ha_hi[:, f, :], v0b[:, f % 2, :], ACT.Copy).then_inc(x_hi_done, 1)
            end_stage(act, 0)

        def pe_0(pe):
            pe.wait_ge(consts, 1)
            pe.wait_ge(vec_loaded, 16 * VECS)
            pe.transpose(work[:, 0, 0:NVEC1], rows1[0:NVEC1, :], ident[0:NVEC1, 0:NVEC1])
            pe.transpose(work[:, 1, 0:NVEC2], rows2[0:NVEC2, :], ident[0:NVEC2, 0:NVEC2]).then_inc(vec_turned, 1)
            for i in range(NT):
                if i % 2 == 0:
                    pe.wait_ge(x_loaded[i // 2], 32)
                for g in range(2):
                    if i >= 2:
                        pe.wait_ge(xt_dve if g else xt_act, i - 1)
                    for f in range(4):
                        mm = pe.transpose(acc[:, i % 2, g * HALF + f * P:g * HALF + (f + 1) * P],
                                          x_tok[:, i, (4 * g + f) * P:(4 * g + f + 1) * P], ident[:, :])
                    mm.then_inc(xt_turned, 1)
            pe.wait_ge(ada_loaded, 16 * 7)
            pe.wait_ge(ada_last, 16)
            pe.wait_ge(silu_c_done, 1)
            for m in range(24):
                for k in range(KT):
                    w = w_ada[:, k, :] if k < 5 else w_ada_b[:, k - 5, :] if k < 7 else w_ada_c[:, 0, :]
                    mm = pe.matmul(work[:, 2, m:m + 1], w[:, m * P:(m + 1) * P], silu_c[:, k:k + 1],
                                   start=(k == 0), stop=(k == KT - 1))
            mm.then_inc(ada_mul, 1)
            pe.wait_ge(vec_ready, 1)
            norm0.pe(pe, lambda f: sq0[:, f % 2, :])
            end_stage(pe, 0)

        def dve_0(dve):
            for i in range(NT):
                dve.wait_ge(xt_turned, 2 * i + 2)
                dve.tensor_copy(xt[:, 4:8, i * P:(i + 1) * P],
                                acc[:, i % 2, HALF:2 * HALF].rearrange("p (f t) -> p f t", f=4)).then_inc(xt_dve, 1)
            dve.wait_ge(ada_mul, 1)
            dve.wait_ge(vec_ready, 1)
            dve.tensor_tensor(ada[:, :], work[:, 2, 0:24], vec1[:, VEC1["b_ada"][0]:VEC1["b_ada"][1]], ALU.add)
            dve.drain()
            dve.scalar_tensor_tensor(a1[:, :], ada[:, 8:16], 1.0, vec1[:, VEC1["norm_w"][0]:VEC1["norm_w"][1]],
                                     ALU.add, ALU.mult)
            norm0.dve(dve, root0, rstd0)
            dve.drain()
            dve.wait_ge(xt_act, NT)
            split_lo(dve, 0)
            for f in range(KT):
                if f >= 1:
                    dve.wait_ge(v0_shifted, f)
                dve.scalar_tensor_tensor(v0[:, 0, :], xt[:, f, :], a1[:, f:f + 1], rstd0[:, :],
                                         ALU.mult, ALU.mult).then_inc(v0_scaled, 1)
                dve.wait_ge(x_hi_done, f + 1)
                dve.tensor_tensor(ha_lo[:, f, :], v0b[:, f % 2, :], ha_hi[:, f, :].bitcast(F32),
                                  ALU.subtract).then_inc(x_lo_done, 1)
            end_stage(dve, 0)

        def pool_0(pool):
            pool.memset(sp_bias[:, :], 0.0)
            pool.memset(gate_bias2[:, :], 0.0).then_inc(zeroed, 1)
            pool.memset(ident[:, :], 0.0)
            pool.memset(ones[:, :], 1.0)
            pool.memset(causal01[:, :], 1.0)
            pool.memset(zero_col[:, :], 0.0)
            pool.memset(eps_col[:, :], EPS)
            pool.memset(sp_sign[:, :], -1.0)
            pool.drain()
            pool.memset(sp_sign[0:32, :], 1.0)
            pool.affine_select(out=ident[:, :], in_=ident[:, :], compare_op=ALU.not_equal, fill=1.0,
                               base=0, pattern=[[-1, P]], channel_multiplier=1)
            pool.affine_select(out=causal01[:, :], in_=causal01[:, :], compare_op=ALU.is_ge, fill=0.0,
                               base=0, pattern=[[1, P]], channel_multiplier=-1)
            pool.drain().then_inc(consts, 1)
            end_stage(pool, 0)

        ar = arena()
        xbc = ar("xbc", [P, XBC_TILES, T])
        spt = ar("spt", [64, T])
        acs = ar("acs", [SSM_HEADS, T])
        ya = ya_region()
        sp1 = {k: ya(f"sp1_{k}", [64, T]) for k in ("u", "e", "relu", "s", "s2", "p")}
        conv_in = ya("conv_in", [P, 2, T + 8])
        conv_out = ya("conv_out", [P, 2, T])
        fcum = ya("fcum", [64, T])
        softplus1 = Softplus(0)
        pad_zeroed = sem("pad_zeroed")
        conved, conv_silued = sem("conved"), sem("conv_silued")
        sums_ready, sums_saved = sem("sums_ready"), sem("sums_saved")

        def sp_1(sp):
            with sp.Fori(0, XBC_TILES // 2 - 1) as j:
                load_w(sp, N_XBC + 1, cols(w_in, XBC_OFF + P + 2 * P * j), adv=j)
                load_w(sp, N_XBC + 2, cols(w_in, XBC_OFF + 2 * P + 2 * P * j), adv=j)
            load_w(sp, N_Z - 1, cols(w_in, XBC_OFF + (XBC_TILES - 1) * P))

        def act_1(act):
            begin_stage(act, 1)
            act.wait_ge(xt_saved, 16)
            act.drain().then_inc(conv_silued, 2)
            split_hi(act, N_XBC)
            softplus1.act(act, sp1["u"][:, :], sp1["e"][:, :], sp1["relu"][:, :])
            with act.Fori(0, XBC_TILES // 2) as j:
                for b in range(2):
                    n = N_XBC + b
                    split_hi(act, n + 1, adv=j)
                    projected(act, n, adv=j)
                    act.wait_ge(pad_zeroed, 1)
                    act.wait_ge(conved, 2 * j + b + 1)
                    act.activation(conv_in[:, b, 3:3 + T], acc[:, n % 2, :], ACT.Copy).then_inc(acc_free[n % 2], 1)
                    act.wait_ge(conved, 2 * j + b + 3)
                    act.activation(row(xbc, 2 * j + b), conv_out[:, b, :], ACT.Silu,
                                   bias=dcol(vec1, VEC1, "conv_b", 2 * j + b)).then_inc(conv_silued, 1)
            end_stage(act, 1)

        def pe_1(pe):
            begin_stage(pe, 1)
            project(pe, N_SMALL1, ha_hi, ha_lo)
            with pe.Fori(0, XBC_TILES // 2) as j:
                for b in range(2):
                    project(pe, N_XBC + b, ha_hi, ha_lo, adv=j)
            end_stage(pe, 1)

        def conv_taps(dve, dst, src, tap):
            dve.tensor_scalar(dst, src(0), tap(0), None, ALU.mult)
            for j in range(1, CONV_K):
                dve.drain()
                last = dve.scalar_tensor_tensor(dst, src(j), tap(j), dst, ALU.mult, ALU.add)
            return last

        def dve_1(dve):
            begin_stage(dve, 1)
            dve.wait_ge(xt_saved, 16)
            dve.drain().then_inc(conved, 2)
            split_lo(dve, N_XBC)
            projected(dve, N_SMALL1)
            dve.wait_ge(col_loaded, 16 * 8)
            dve.tensor_scalar(sp1["u"][:, :], acc[0:64, 0, :], sp_bias[:, :], sp_sign[:, :], ALU.add,
                              ALU.mult).then_inc(acc_free[0], 1)
            dve.drain().then_inc(softplus1.ready, 1)
            softplus1.dve_ratio(dve, *(sp1[k][:, :] for k in ("e", "s", "s2")))
            softplus1.dve_series(dve, *(sp1[k][:, :] for k in ("relu", "s", "s2")), spt[:, :])
            dve.drain()
            a = sp1["u"][0:SSM_HEADS, :]
            dve.tensor_scalar(a, spt[0:SSM_HEADS, :], neg_a[:, :], None, ALU.mult)
            dve.drain()
            for c in range(NCHUNK):
                t = slice(c * CHUNK, (c + 1) * CHUNK)
                dve.tensor_tensor_scan(acs[:, t], a[:, t], zero_col[0:SSM_HEADS, :].to_broadcast([SSM_HEADS, CHUNK]),
                                       0.0, ALU.add, ALU.add)
            f = slice(32, 32 + FOX_HEADS)
            dve.tensor_tensor_scan(fcum[f, :], spt[f, :], zero_col[f, :].to_broadcast([FOX_HEADS, T]),
                                   0.0, ALU.add, ALU.add)
            dve.drain().then_inc(sums_ready, 1)
            with dve.Fori(0, XBC_TILES // 2) as j:
                for b in range(2):
                    n = N_XBC + b
                    split_lo(dve, n + 1, adv=j)
                    dve.wait_ge(acc_free[n % 2], n // 2 + 1 + j)
                    dve.wait_ge(conv_silued, 2 * j + b + 1)
                    conv_taps(dve, conv_out[:, b, :], lambda k: conv_in[:, b, k:k + T],
                              lambda k: vec1[:, VEC1["conv_w"][0] + k * XBC_TILES:][:, bass.ds(2 * j + b, 1)]
                              ).then_inc(conved, 1)
            end_stage(dve, 1)

        def pool_1(pool):
            begin_stage(pool, 1)
            pool.wait_ge(xt_saved, 16)
            pool.memset(conv_in[:, :, 0:3], 0.0).then_inc(pad_zeroed, 1)
            pool.wait_ge(sums_ready, 1)
            pool.dma_start(acs_scr, acs[:, :]).then_inc(sums_saved, 16)
            pool.dma_start(fcum_scr, fcum[32:32 + FOX_HEADS, :]).then_inc(sums_saved, 16)
            pool.wait_ge(sums_saved, 32)
            end_stage(pool, 1)


        ya = ya_region()
        x_st = ya("x_st", [P, 8, CHUNK])
        bc_st = ya("bc_st", [P, 2, CHUNK])
        dtacs_st = ya("dtacs_st", [SSM_HEADS, 2, CHUNK])
        acs_bc = ya("acs_bc", [P, SSM_HEADS, CHUNK])
        acs_n = ya("acs_n", [P, HPG, CHUNK])
        decay = ya("decay", [P, SSM_HEADS, CHUNK])
        tok16 = ya("tok16", [P, 2, SSM_HEADS])
        b_tok = ya("b_tok", [P, P])
        e_acs = ya("e_acs", [P, HPG, CHUNK])
        c_dec = ya("c_dec", [P, HPG, CHUNK])
        xdt = ya("xdt", [P, SSM_HEADS, SSM_P])
        xdec = ya("xdec", [P, SSM_HEADS, SSM_P])
        state = ya("state", [P, HPG, SSM_P])
        xskip = ya("xskip", [P, 8, CHUNK])
        to_end = ya("to_end", [P, 2, SSM_HEADS])
        staged, bc_loaded = sem("staged"), [sem("bc_loaded0"), sem("bc_loaded1")]
        turned2, tok_ready, b_ready = sem("turned2"), sem("tok_ready"), sem("b_ready")
        cb_done, seg_done, masked2, decay_done = sem("cb_done"), sem("seg_done"), sem("masked2"), sem("decay_done")
        end_arg, end_exp, e_acs_done = sem("end_arg"), sem("end_exp"), sem("e_acs_done")
        cdec_done, xdec_done, m_done = sem("cdec_done"), sem("xdec_done"), sem("m_done")
        xskip_done, y_done, kv_done = sem("xskip_done"), sem("y_done"), sem("kv_done")
        chunk_done = sem("chunk_done")
        b_own = ya("b_own", [P, SSM_G, CHUNK])
        stash = ya("stash", [P, 2, T])
        stash_ready, stash_saved = [sem("z_ready"), sem("g_ready")], [sem("z_saved"), sem("g_saved")]
        ypsum = acc[:, 1, :]
        cbpsum = work[:, 2, 256:256 + SSM_G * CHUNK]
        kvpsum = work[:, 3, :]

        def chunk_of(x, c):
            return x[:, :, bass.ds(c * CHUNK, CHUNK)]

        def sp_2(sp):
            load_w(sp, N_Z, cols(w_in, Z_OFF))
            load_w(sp, N_Z + 1, cols(w_in, G_OFF))

            def save(i, c, scr):
                wait_here(sp, stash_ready[i], c + 1)
                sp.dma_start(row(scr, c), stash[:, i, :]).then_inc(stash_saved[i], 16)

            with sp.Fori(0, NCHUNK - 1) as c:
                load_w(sp, N_Z + 2, cols(w_in, Z_OFF + P + P * c), adv=c)
                save(0, c, z_scr)
                load_w(sp, N_Z + 3, cols(w_in, G_OFF + P + P * c), adv=c)
                save(1, c, g_scr)
            for i, scr in ((0, z_scr), (1, g_scr)):
                load_w(sp, N_GATT + i, cols(w_in, G_OFF + D + i * P))
                sp.wait_ge(stash_ready[i], NCHUNK)
                sp.dma_start(scr[:, NCHUNK - 1, :], stash[:, i, :]).then_inc(stash_saved[i], 16)

        def pool_2(pool):
            begin_stage(pool, 2)
            masked_fill = pool.to_reg(MASKED)
            pool.memset(b_own[:, :, :], 0.0)
            pool.drain()
            with pool.Fori(0, NCHUNK) as c:
                pool.wait_ge(chunk_done, c + 1)
                pool.dma_start(acs_bc[:, :, :], acs_scr[:, bass.ds(c * CHUNK, CHUNK)].partition_broadcast(P)
                               ).then_inc(bc_loaded[0], 16)
                for g in range(SSM_G):
                    pool.dma_start(acs_n[g * 64:g * 64 + 64, :, :],
                                   acs_scr[g * HPG:(g + 1) * HPG, bass.ds(c * CHUNK, CHUNK)].partition_broadcast(64)
                                   ).then_inc(bc_loaded[1], 16)
                pool.tensor_copy(x_st[:, :, :], chunk_of(xbc[:, 0:8, :], c))
                pool.tensor_copy(bc_st[:, :, :], chunk_of(xbc[:, 8:10, :], c))
                for g in range(SSM_G):
                    gp = slice(g * 64, g * 64 + 64)
                    pool.drain()
                    pool.tensor_copy(b_own[gp, g, :], xbc[gp, 8, bass.ds(c * CHUNK, CHUNK)])
                pool.drain()
                pool.tensor_copy(dtacs_st[:, 0, :], spt[0:SSM_HEADS, bass.ds(c * CHUNK, CHUNK)])
                pool.tensor_copy(dtacs_st[:, 1, :], acs[:, bass.ds(c * CHUNK, CHUNK)])
                pool.drain().then_inc(staged, 1)
                pool.tensor_tensor(xskip[:, :, :], x_st[:, :, :],
                                   dskip[:, :].unsqueeze(2).to_broadcast([P, 8, CHUNK]), ALU.mult).then_inc(xskip_done, 1)
                wait_here(pool, seg_done, c + 1)
                pool.affine_select(out=decay[:, :, :], in_=decay[:, :, :], compare_op=ALU.is_ge, fill=masked_fill,
                                   base=0, pattern=[[0, SSM_HEADS], [1, CHUNK]], channel_multiplier=-1
                                   ).then_inc(masked2, 1)
            end_stage(pool, 2)

        def pe_2(pe):
            begin_stage(pe, 2)
            with pe.Fori(0, NCHUNK) as c:
                pe.wait_ge(staged, c + 1)
                for i in range(8):
                    pe.transpose(work[:, i // 4, (i % 4) * P:(i % 4 + 1) * P], x_st[:, i, :], ident[:, :])
                pe.transpose(work[:, 2, 0:P], bc_st[:, 0, :], ident[:, :])
                for i in range(2):
                    mm = pe.transpose(work[:, 2, P + i * 16:P + i * 16 + 16], dtacs_st[:, i, :], ident[0:16, 0:16])
                mm.then_inc(turned2, 1)
                for part in range(2):
                    project_part(pe, N_Z, part, 2 * c, adv=c)
                pe.wait_ge(b_ready, c + 1)
                for g in range(SSM_G):
                    mm = pe.matmul(cbpsum[:, g * CHUNK:(g + 1) * CHUNK], b_own[:, g, :], bc_st[:, 1, :], start=True, stop=True)
                mm.then_inc(cb_done, 1)
                for part in range(2, 4):
                    project_part(pe, N_Z, part, 2 * c, adv=c)
                pe.wait_ge(xdec_done, c + 1)
                for g in range(SSM_G):
                    mm = pe.matmul(kvpsum[g * 64:g * 64 + 64, :], b_tok[:, g * 64:g * 64 + 64],
                                   xdec[:, g * HPG:(g + 1) * HPG, :], start=True, stop=True)
                mm.then_inc(kv_done, 1)
                pe.wait_ge(m_done, c + 1)
                pe.wait_ge(cdec_done, c + 1)
                for h in range(SSM_HEADS):
                    g, r = divmod(h, HPG)
                    y = ypsum[(h % 2) * 64:(h % 2) * 64 + 64, (h // 2) * CHUNK:(h // 2 + 1) * CHUNK]
                    pe.matmul(y, xdt[:, h, :], decay[:, h, :], start=True, stop=False)
                    mm = pe.matmul(y, state[g * 64:g * 64 + 64, r, :], c_dec[g * 64:g * 64 + 64, r, :],
                                   start=False, stop=True)
                mm.then_inc(y_done, 1)
                for part in range(4):
                    project_part(pe, N_Z + 1, part, 2 * c + 1, adv=c)
            end_stage(pe, 2)

        def act_2(act):
            begin_stage(act, 2)
            act.drain().then_inc(fill_free, 2)
            for i in range(2):
                act.drain().then_inc(stash_saved[i], 16)
            with act.Fori(0, NCHUNK) as c:
                split_hi(act, N_Z + 1, adv=c)
                act.wait_ge(turned2, c + 1)
                act.activation(tok16[:, :, :], work[:, 2, P:P + 32], ACT.Copy).then_inc(tok_ready, 1)
                act.activation(b_tok[:, :], work[:, 2, 0:P], ACT.Copy).then_inc(b_ready, 1)
                act.wait_ge(bc_loaded[1], 32 * c + 32)
                act.activation(e_acs[:, :, :], acs_n[:, :, :], ACT.Exp).then_inc(e_acs_done, 1)
                act.wait_ge(end_arg, c + 1)
                act.activation(to_end[:, 1, :], to_end[:, 0, :], ACT.Exp).then_inc(end_exp, 1)
                act.wait_ge(masked2, c + 1)
                act.activation(decay[:, :, :], decay[:, :, :], ACT.Exp).then_inc(decay_done, 1)
                for i in range(2):
                    act.wait_ge(stash_saved[i], 16 * c + 16)
                    for half in range(2):
                        read_half(act, N_Z + i, half, 2 * c + i, stash[:, i, :], adv=c)
                    act.drain().then_inc(stash_ready[i], 1)
                    if i == 0:
                        split_hi(act, N_Z + 2, adv=c)
            for a in range(2):
                act.drain().then_inc(acc_free[a], NCHUNK)
            end_stage(act, 2)

        def dve_2(dve):
            begin_stage(dve, 2)
            dve.memset(state[:, :, :], 0.0)
            dve.drain().then_inc(chunk_done, 1)
            with dve.Fori(0, NCHUNK) as c:
                dve.wait_ge(tok_ready, c + 1)
                dve.wait_ge(bc_loaded[0], 16 * c + 16)
                dve.tensor_tensor(decay[:, :, :], acs_bc[:, :, :],
                                  tok16[:, 1, :].unsqueeze(2).to_broadcast([P, SSM_HEADS, CHUNK]),
                                  ALU.subtract).then_inc(seg_done, 1)
                dve.tensor_tensor(to_end[:, 0, :], acs_bc[:, :, CHUNK - 1], tok16[:, 1, :],
                                  ALU.subtract).then_inc(end_arg, 1)
                dve.tensor_tensor(xdt[:, :, :], work[:, 0:2, :].rearrange("p b (h d) -> p (b h) d", d=SSM_P),
                                  tok16[:, 0, :].unsqueeze(2).to_broadcast([P, SSM_HEADS, SSM_P]), ALU.mult)
                dve.drain()
                dve.wait_ge(end_exp, c + 1)
                dve.tensor_tensor(xdec[:, :, :], xdt[:, :, :],
                                  to_end[:, 1, :].unsqueeze(2).to_broadcast([P, SSM_HEADS, SSM_P]),
                                  ALU.mult).then_inc(xdec_done, 1)
                dve.wait_ge(e_acs_done, c + 1)
                dve.tensor_tensor(c_dec[:, :, :], e_acs[:, :, :],
                                  bc_st[:, 1, :].unsqueeze(1).to_broadcast([P, HPG, CHUNK]), ALU.mult).then_inc(cdec_done, 1)
                dve.wait_ge(decay_done, c + 1)
                dve.wait_ge(cb_done, c + 1)
                for g in range(SSM_G):
                    m = dve.tensor_tensor(decay[:, g * HPG:(g + 1) * HPG, :], decay[:, g * HPG:(g + 1) * HPG, :],
                                          cbpsum[:, g * CHUNK:(g + 1) * CHUNK].unsqueeze(1).to_broadcast([P, HPG, CHUNK]),
                                          ALU.mult)
                m.then_inc(m_done, 1)
                split_lo(dve, N_Z + 1, adv=c)
                dve.wait_ge(xskip_done, c + 1)
                dve.wait_ge(y_done, c + 1)
                dve.tensor_tensor(chunk_of(xbc[:, 0:8, :], c), ypsum.rearrange("p (i l) -> p i l", l=CHUNK),
                                  xskip[:, :, :], ALU.add)
                dve.wait_ge(kv_done, c + 1)
                dve.tensor_tensor(state[:, :, :], state[:, :, :],
                                  e_acs[:, :, CHUNK - 1].unsqueeze(2).to_broadcast([P, HPG, SSM_P]), ALU.mult)
                dve.drain()
                dve.tensor_tensor(state[:, :, :], state[:, :, :], kvpsum.rearrange("p (r d) -> p r d", d=SSM_P), ALU.add)
                dve.drain().then_inc(chunk_done, 1)
                split_lo(dve, N_Z + 2, adv=c)
            end_stage(dve, 2)

        silu_z = Region(at_arena + XBC_TILES * T * 4, arena_end)("silu_z", [P, 2, T])
        yw = Region(at_arena + 8 * T * 4, arena_end)("yw", [P, 2, T])
        z_loaded, z_silued = [sem("z_loaded0"), sem("z_loaded1")], sem("z_silued")
        yz_done, yw_done = sem("yz_done"), sem("yw_done")

        ga_half = Region(at_arena + XBC_TILES * T * 4 + 2 * T * 4, arena_end)("ga_half", [P, HALF])
        ga_ready, ga_saved = sem("ga_ready"), sem("ga_saved")

        def sp_3(sp):
            def save(m, dst):
                for half in range(2):
                    wait_here(sp, ga_ready, 2 * m + half + 1)
                    sp.dma_start(dst[:, half * HALF:(half + 1) * HALF], ga_half[:, :]).then_inc(ga_saved, 16)

            with sp.Fori(0, 3) as j:
                for b in range(2):
                    load_w(sp, N_GATT + 2 + b, cols(w_in, G_OFF + D + (2 + b) * P + 2 * P * j), adv=j)
                    save(2 * j + b, row(ga_scr, 2 * j + b))
            for b in range(2):
                load_w(sp, N_MIX1 + b, cols(io["w_proj_ssm"], b * P))
                for half in range(2):
                    sp.wait_ge(ga_ready, 2 * (6 + b) + half + 1)
                    sp.dma_start(ga_scr[:, 6 + b, half * HALF:(half + 1) * HALF], ga_half[:, :]).then_inc(ga_saved, 16)

        def pool_3(pool):
            begin_stage(pool, 3)
            for i in range(2):
                pool.wait_ge(stash_saved[i], 16 * (NCHUNK + 1))
            with pool.Fori(0, 4) as j:
                for b in range(2):
                    wait_here(pool, yz_done, 2 * j + b + 1)
                    pool.dma_start(silu_z[:, b, :], row(z_scr, 2 * j + b)).then_inc(z_loaded[b], 16)
            end_stage(pool, 3)

        def pe_3(pe):
            begin_stage(pe, 3)
            with pe.Fori(0, 4) as j:
                for b in range(2):
                    project(pe, N_GATT + b, ha_hi, ha_lo, adv=j)
            end_stage(pe, 3)

        def act_3(act):
            begin_stage(act, 3)
            act.drain().then_inc(ga_saved, 16)
            with act.Fori(0, 4) as j:
                for b in range(2):
                    n = N_GATT + b
                    split_hi(act, n + 1, adv=j)
                    act.wait_ge(z_loaded[b], 16 * j + 16)
                    act.activation(silu_z[:, b, :], silu_z[:, b, :], ACT.Silu).then_inc(z_silued, 1)
                    act.wait_ge(yw_done, 2 * j + b + 1)
                    act.activation(row(ya_hi, 2 * j + b), yw[:, b, :], ACT.Copy).then_inc(x_hi_done, 1)
                    act.activation(row(xbc, 2 * j + b), row(xbc, 2 * j + b), ACT.Square).then_inc(Norm.squared, 1)
                    projected(act, n, adv=j)
                    for half in range(2):
                        act.wait_ge(ga_saved, 64 * j + 32 * b + 16 * half + 16)
                        e = act.activation(ga_half[:, :], acc[:, n % 2, half * HALF:(half + 1) * HALF], ACT.Copy)
                        if half:
                            e.then_inc(acc_free[n % 2], 1)
                        act.drain().then_inc(ga_ready, 1)
            end_stage(act, 3)

        def dve_3(dve):
            begin_stage(dve, 3)
            dve.drain().then_inc(yz_done, 2)
            with dve.Fori(0, 4) as j:
                for b in range(2):
                    split_lo(dve, N_GATT + b + 1, adv=j)
                    dve.wait_ge(z_silued, 2 * j + b + 1)
                    dve.tensor_tensor(row(xbc, 2 * j + b), row(xbc, 2 * j + b), silu_z[:, b, :], ALU.mult)
                    dve.drain().then_inc(yz_done, 1)
                    dve.tensor_scalar(yw[:, b, :], row(xbc, 2 * j + b), dcol(vec1, VEC1, "ssm_norm_w", 2 * j + b), None,
                                      ALU.mult).then_inc(yw_done, 1)
                    dve.wait_ge(x_hi_done, SPLITS[3] + 2 * j + b + 1)
                    dve.tensor_tensor(row(ya_lo, 2 * j + b), yw[:, b, :], row(ya_hi, 2 * j + b).bitcast(F32), ALU.subtract)
            end_stage(dve, 3)

        ar = Region(at_arena + 8 * T * 4, arena_end)
        root4 = ar("root4", [P, T])
        rstd4 = ar("rstd4", [P, T])
        ar = arena()
        gate4 = ar("gate4", [P, 2, T])
        mix4 = ar("mix4", [P, 2, T])
        norm4 = Norm(1)
        g_loaded4, g_sigmoid = [sem("g_loaded4_0"), sem("g_loaded4_1")], sem("g_sigmoid")
        mix4_done, mix4_saved, mix4_free = sem("mix4_done"), sem("mix4_saved"), sem("mix4_free")

        def sp_4(sp):
            with sp.Fori(0, 3) as j:
                for b in range(2):
                    load_w(sp, N_MIX1 + 2 + b, cols(io["w_proj_ssm"], (2 + b) * P + 2 * P * j), adv=j)

        def pe_4(pe):
            begin_stage(pe, 4)
            for f in range(KT):
                for h in range(2):
                    mm = pe.matmul(work[:, h, :], ones[:, :], xbc[:, f, h * HALF:(h + 1) * HALF],
                                   start=(f == 0), stop=(f == KT - 1))
                mm.then_inc(norm4.summed, 1)
            with pe.Fori(0, 4) as j:
                for b in range(2):
                    project(pe, N_MIX1 + b, ya_hi, ya_lo, adv=j)
            end_stage(pe, 4)

        def act_4(act):
            begin_stage(act, 4)
            norm4.act_root(act, root4)
            with act.Fori(0, 4) as j:
                for b in range(2):
                    split_hi(act, N_MIX1 + b + 1, adv=j)
                    act.wait_ge(g_loaded4[b], 16 * j + 16)
                    act.activation(gate4[:, b, :], gate4[:, b, :], ACT.Sigmoid,
                                   bias=dcol(vec1, VEC1, "b_gate", 2 * j + b)).then_inc(g_sigmoid, 1)
            end_stage(act, 4)

        def dve_4(dve):
            begin_stage(dve, 4)
            dve.drain().then_inc(mix4_done, 2)
            dve.drain().then_inc(mix4_free, 2)
            norm4.dve(dve, root4, rstd4)
            dve.drain()
            with dve.Fori(0, 4) as j:
                for b in range(2):
                    n = N_MIX1 + b
                    split_lo(dve, n + 1, adv=j)
                    dve.wait_ge(g_sigmoid, 2 * j + b + 1)
                    dve.tensor_tensor(gate4[:, b, :], gate4[:, b, :], rstd4[:, :], ALU.mult)
                    dve.drain()
                    projected(dve, n, adv=j)
                    dve.wait_ge(mix4_free, 2 * j + b + 1)
                    dve.tensor_tensor(mix4[:, b, :], acc[:, n % 2, :], gate4[:, b, :],
                                      ALU.mult).then_inc(acc_free[n % 2], 1)
                    dve.drain().then_inc(mix4_done, 1)
            end_stage(dve, 4)

        def pool_4(pool):
            begin_stage(pool, 4)
            pool.wait_ge(norm4.summed, norm4.tiles + KT)
            pool.wait_ge(ga_saved, 16 * 17)
            with pool.Fori(0, 4) as j:
                for b in range(2):
                    wait_here(pool, mix4_done, 2 * j + b + 1)
                    pool.dma_start(gate4[:, b, :], row(g_scr, 2 * j + b)).then_inc(g_loaded4[b], 16)
                for b in range(2):
                    wait_here(pool, mix4_done, 2 * j + b + 3)
                    pool.dma_start(row(merged_scr, 2 * j + b), mix4[:, b, :]).then_inc(mix4_saved, 16)
                    wait_here(pool, mix4_saved, 32 * j + 16 * b + 16)
                    pool.drain().then_inc(mix4_free, 1)
            end_stage(pool, 4)

        ar = arena()
        q_t = ar("q_t", [P, T])
        k_t = ar("k_t", [P, T])
        v_tok = ar("v_tok", [P, NT, FOX_D])
        silu_za = ar("silu_za", [P, T])
        f_bc = ar("f_bc", [P, T])
        prob = ar("prob", [P, 2, T])
        prob_t = ar("prob_t", [P, 2, NT, P])
        y_head = ar("y_head", [P, T])
        neg_max = ar("neg_max", [P, 2])
        row_sum = ar("row_sum", [P, 2])
        row_inv = ar("row_inv", [P, 2])
        last = (FOX_HEADS - 1) * T * 4
        next_tiles = [Region(at_ya + last, at_ya + big)("next_q", [P, T]), Region(at_ya + big + last, at_ya + 2 * big)("next_k", [P, T]),
                      ar("next_v", [P, T]), ar("next_z", [P, T])]
        nxt_ready = sem("nxt_ready")
        taken = sem("taken")
        fbc_loaded, fbc_used = sem("fbc_loaded"), sem("fbc_used")
        v_turned, v_ready = sem("v_turned"), sem("v_ready")
        qk_done, logits_done, diag_done, max_done = sem("qk_done"), sem("logits_done"), sem("diag_done"), sem("max_done")
        exp_done, prob_done, p_turned, p_copied = sem("exp_done"), sem("prob_done"), sem("p_turned"), sem("p_copied")
        pv_done, y_gated, za_ready = sem("pv_done"), sem("y_gated"), sem("za_ready")
        FOX_SCALE = float(FOX_D) ** -0.5
        FILLS2 = 2 * NCHUNK
        BANK_TILES = HALF // P

        def fox_chunks(t):
            first = sum((v + BANK_TILES) // BANK_TILES for v in range(t))
            return [(first + i, a, min(a + BANK_TILES, t + 1)) for i, a in enumerate(range(0, t + 1, BANK_TILES))]

        FC = fox_chunks(NT)[0][0]

        def sp_5(sp):
            with sp.Fori(0, FOX_HEADS) as h:
                for i, off in enumerate((Q_OFF, K_OFF, V_OFF, ZA_OFF)):
                    load_w(sp, N_FOX + i, cols(w_in, off + P * h), adv=2 * h)

        def pool_5(pool):
            begin_stage(pool, 5)
            pool.drain().then_inc(fbc_used, 1)
            masked_fill = pool.to_reg(MASKED)
            with pool.Fori(0, FOX_HEADS) as h:
                wait_here(pool, nxt_ready, 4 * h + 2)
                pool.tensor_copy(q_t[:, :], next_tiles[0][:, :])
                pool.tensor_copy(k_t[:, :], next_tiles[1][:, :])
                pool.drain().then_inc(taken, 1)
                wait_here(pool, fbc_used, h + 1)
                pool.dma_start(f_bc[:, :], fcum_scr[bass.ds(h, 1), :].rearrange("a t -> (a t)").partition_broadcast(P)
                               ).then_inc(fbc_loaded, 16)
                for t in range(NT):
                    wait_here(pool, logits_done, FC * h + fox_chunks(t)[-1][0] + 1)
                    pool.affine_select(out=prob[:, t % 2, t * P:(t + 1) * P], in_=prob[:, t % 2, t * P:(t + 1) * P],
                                       compare_op=ALU.is_ge, fill=masked_fill, base=0, pattern=[[-1, P]],
                                       channel_multiplier=1).then_inc(diag_done, 1)
            end_stage(pool, 5)

        def pe_5(pe):
            begin_stage(pe, 5)
            for i in range(4):
                project(pe, N_FOX + i, ha_hi, ha_lo)
            for a in range(2):
                pe.wait_ge(acc_free[(N_FOX + 2 + a) % 2], (N_FOX + 2 + a) // 2 + 1)

            def head(h, ahead=True):
                def fill(part):
                    if ahead:
                        project_part(pe, N_FOX + 4 + part // 4, part % 4, FILLS2 + 4 * h + part // 4, adv=2 * h)

                def scores(t):
                    for c, a, b in fox_chunks(t):
                        if c >= 2:
                            pe.wait_ge(logits_done, FC * h + c - 1)
                        pe.matmul(work[:, c % 2, 0:(b - a) * P], q_t[:, t * P:(t + 1) * P], k_t[:, a * P:b * P],
                                  start=True, stop=True).then_inc(qk_done, 1)

                def turn_probs(t):
                    pe.wait_ge(prob_done, NT * h + t + 1)
                    for c, a, b in fox_chunks(t):
                        if c >= 2:
                            pe.wait_ge(p_copied, FC * h + c - 1)
                        for k in range(a, b):
                            mm = pe.transpose(work[:, 2 + c % 2, (k - a) * P:(k - a + 1) * P], prob[:, t % 2, k * P:(k + 1) * P],
                                              ident[:, :])
                        mm.then_inc(p_turned, 1)

                def weigh_values(t):
                    for c, a, b in fox_chunks(t):
                        pe.wait_ge(p_copied, FC * h + c + 1)
                        for k in range(a, b):
                            mm = pe.matmul(acc[:, 1, t * P:(t + 1) * P], v_tok[:, k, :], prob_t[:, t % 2, k, :],
                                           start=(k == 0), stop=(k == t))
                    mm.then_inc(pv_done, 1)

                pe.wait_ge(nxt_ready, 4 * h + 3)
                for b in range(NT):
                    mm = pe.transpose(work[:, 2 + b // 4, (b % 4) * P:(b % 4 + 1) * P], next_tiles[2][:, b * P:(b + 1) * P], ident[:, :])
                mm.then_inc(v_turned, 1)
                pe.wait_ge(taken, h + 1)
                scores(0)
                scores(1)
                for t in range(NT):
                    fill(2 * t)
                    if t + 1 < NT:
                        fill(2 * t + 1)
                    if t == 0:
                        pe.wait_ge(v_ready, h + 1)
                        pe.wait_ge(y_gated, 2 * h + 2)
                    turn_probs(t)
                    if t + 2 < NT:
                        scores(t + 2)
                    weigh_values(t)
                fill(2 * NT - 1)

            with pe.Fori(0, FOX_HEADS - 1) as h:
                head(h)
            head(FOX_HEADS - 1, ahead=False)
            end_stage(pe, 5)

        def act_5(act):
            begin_stage(act, 5)
            for i in range(4):
                n = N_FOX + i
                split_hi(act, n + 1)
                projected(act, n)
                act.activation(next_tiles[i][:, :], acc[:, n % 2, :], ACT.Copy).then_inc(acc_free[n % 2], 1)
            act.drain().then_inc(nxt_ready, 4)

            def head(h, ahead=True):
                def exps(t):
                    act.wait_ge(max_done, NT * h + t + 1)
                    w = (t + 1) * P
                    act.activation(prob[:, t % 2, 0:w], prob[:, t % 2, 0:w], ACT.Exp, bias=neg_max[:, t % 2:t % 2 + 1],
                                   accum_out=row_sum[:, t % 2:t % 2 + 1]).then_inc(exp_done, 1)

                def read_next(t):
                    i, half = divmod(t, 2)
                    read_half(act, N_FOX + 4 + i, half, FILLS2 + 4 * h + i, next_tiles[i], adv=2 * h)
                    if half:
                        act.drain().then_inc(nxt_ready, 1)

                act.wait_ge(v_turned, h + 1)
                act.activation(v_tok[:, :, :], work[:, 2:4, :], ACT.Copy).then_inc(v_ready, 1)
                act.activation(silu_za[:, :], next_tiles[3][:, :], ACT.Silu)
                act.drain().then_inc(za_ready, 1)
                act.wait_ge(taken, h + 1)
                exps(0)
                for t in range(NT):
                    if t + 1 < NT:
                        exps(t + 1)
                    if ahead and t % 2 == 0:
                        split_hi(act, N_FOX + 5 + t // 2, adv=2 * h)
                    for c, a, b in fox_chunks(t):
                        act.wait_ge(p_turned, FC * h + c + 1)
                        act.activation(prob_t[:, t % 2, a:b, :], work[:, 2 + c % 2, 0:(b - a) * P], ACT.Copy).then_inc(p_copied, 1)
                    if ahead:
                        read_next(t)
                act.wait_ge(y_gated, 2 * h + 4)
                act.activation(row(ya_hi, h), y_head[:, :], ACT.Copy).then_inc(x_hi_done, 1)

            with act.Fori(0, FOX_HEADS - 1) as h:
                head(h)
            head(FOX_HEADS - 1, ahead=False)
            for a in range(2):
                act.drain().then_inc(acc_free[a], 2 * (FOX_HEADS - 1))
            end_stage(act, 5)

        def dve_5(dve):
            begin_stage(dve, 5)
            dve.drain().then_inc(y_gated, 2)
            for i in range(4):
                split_lo(dve, N_FOX + i + 1)

            def head(h, ahead=True):
                def logits(t):
                    if t >= 2:
                        dve.wait_ge(p_turned, FC * h + fox_chunks(t - 1)[0][0])
                    for c, a, b in fox_chunks(t):
                        dve.wait_ge(qk_done, FC * h + c + 1)
                        dve.scalar_tensor_tensor(prob[:, t % 2, a * P:b * P], work[:, c % 2, 0:(b - a) * P], FOX_SCALE,
                                                 f_bc[:, a * P:b * P], ALU.mult, ALU.add).then_inc(logits_done, 1)
                    dve.drain()
                    dve.wait_ge(diag_done, NT * h + t + 1)
                    dve.tensor_reduce(neg_max[:, t % 2:t % 2 + 1], prob[:, t % 2, 0:(t + 1) * P], AX.X, ALU.max,
                                      negate=True).then_inc(max_done, 1)

                def normalise(t):
                    dve.wait_ge(exp_done, NT * h + t + 1)
                    dve.reciprocal(row_inv[:, t % 2:t % 2 + 1], row_sum[:, t % 2:t % 2 + 1])
                    dve.drain()
                    w = (t + 1) * P
                    dve.tensor_scalar(prob[:, t % 2, 0:w], prob[:, t % 2, 0:w], row_inv[:, t % 2:t % 2 + 1], None,
                                      ALU.mult).then_inc(prob_done, 1)

                def gate(half):
                    dve.wait_ge(pv_done, NT * h + 4 * half + 4)
                    s = slice(half * HALF, (half + 1) * HALF)
                    dve.tensor_tensor(y_head[:, s], acc[:, 1, s], silu_za[:, s], ALU.mult).then_inc(y_gated, 1)

                dve.wait_ge(fbc_loaded, 16 * h + 16)
                logits(0)
                for t in range(NT):
                    normalise(t)
                    if t + 1 < NT:
                        logits(t + 1)
                    if t == NT - 2:
                        dve.drain().then_inc(fbc_used, 1)
                    if ahead and t % 2 == 1:
                        split_lo(dve, N_FOX + 5 + t // 2, adv=2 * h)
                    if t == 5:
                        dve.wait_ge(za_ready, h + 1)
                        gate(0)
                gate(1)
                dve.wait_ge(x_hi_done, SPLITS[5] + h + 1)
                dve.tensor_tensor(row(ya_lo, h), y_head[:, :], row(ya_hi, h).bitcast(F32), ALU.subtract)

            with dve.Fori(0, FOX_HEADS - 1) as h:
                head(h)
            head(FOX_HEADS - 1, ahead=False)
            end_stage(dve, 5)

        ar = arena()
        merged = ar("merged", [P, KT, T])
        gate6 = ar("gate6", [P, 2, T])
        mix_before = ar("mix_before", [P, 2, T])
        gate6_used, gate6_done = sem("gate6_used"), sem("gate6_done")
        g_loaded6, mix_loaded = [sem("g_loaded6_0"), sem("g_loaded6_1")], [sem("mix_loaded0"), sem("mix_loaded1")]

        def sp_6(sp):
            with sp.Fori(0, 4) as j:
                for b in range(2):
                    load_w(sp, N_MIX2 + b, cols(io["w_proj_att"], b * P + 2 * P * j), adv=j)

        def pe_6(pe):
            begin_stage(pe, 6)
            with pe.Fori(0, 4) as j:
                for b in range(2):
                    project(pe, N_MIX2 + b, ya_hi, ya_lo, adv=j)
            end_stage(pe, 6)

        def act_6(act):
            begin_stage(act, 6)
            with act.Fori(0, 4) as j:
                for b in range(2):
                    split_hi(act, N_MIX2 + b + 1, adv=j)
                    act.wait_ge(g_loaded6[b], 16 * j + 16)
                    act.activation(gate6[:, b, :], gate6[:, b, :], ACT.Sigmoid,
                                   bias=vec1[:, VEC1["b_gate"][0] + 8:VEC1["b_gate"][1]][:, bass.ds(2 * j + b, 1)]
                                   ).then_inc(gate6_done, 1)
            end_stage(act, 6)

        def dve_6(dve):
            begin_stage(dve, 6)
            dve.drain().then_inc(gate6_used, 2)
            with dve.Fori(0, 4) as j:
                for b in range(2):
                    n = N_MIX2 + b
                    split_lo(dve, n + 1, adv=j)
                    dve.wait_ge(gate6_done, 2 * j + b + 1)
                    projected(dve, n, adv=j)
                    dve.tensor_tensor(gate6[:, b, :], acc[:, n % 2, :], gate6[:, b, :], ALU.mult).then_inc(acc_free[n % 2], 1)
                    dve.drain()
                    dve.wait_ge(mix_loaded[b], 16 * j + 16)
                    dve.tensor_tensor(row(merged, 2 * j + b), gate6[:, b, :], mix_before[:, b, :], ALU.add)
                    dve.drain().then_inc(gate6_used, 1)
            end_stage(dve, 6)

        def pool_6(pool):
            begin_stage(pool, 6)
            with pool.Fori(0, 4) as j:
                for b in range(2):
                    wait_here(pool, gate6_used, 2 * j + b + 1)
                    pool.dma_start(gate6[:, b, :], row(ga_scr, 2 * j + b)).then_inc(g_loaded6[b], 16)
                    pool.dma_start(mix_before[:, b, :], row(merged_scr, 2 * j + b)).then_inc(mix_loaded[b], 16)
            end_stage(pool, 6)

        x1 = Region(at_ya, at_ya + big)("x1", [P, KT, T])
        ar = Region(at_arena + big, arena_end)
        xt_tile = ar("xt_tile", [P, 2, T])
        xt_loaded, res_done = [sem("xt_loaded0"), sem("xt_loaded1")], sem("res_done")

        def sp_7(sp):
            with sp.Fori(0, 4) as j:
                for b in range(2):
                    load_w(sp, N_OUT1 + b, cols(io["w_out"], b * P + 2 * P * j), adv=j)

        def pe_7(pe):
            begin_stage(pe, 7)
            pe.wait_ge(x_lo_done, LO_SPLITS[7] + KT)
            with pe.Fori(0, 4) as j:
                for b in range(2):
                    project(pe, N_OUT1 + b, ha_hi, ha_lo, adv=j)
            end_stage(pe, 7)

        def act_7(act):
            begin_stage(act, 7)
            for k in range(KT):
                act.activation(ha_hi[:, k, :], merged[:, k, :], ACT.Copy).then_inc(x_hi_done, 1)
            with act.Fori(0, 3) as j:
                for b in range(2):
                    split_hi(act, N_OUT1 + b + 1, adv=j)
            split_hi(act, N_SMALL2 - 1)
            act.wait_ge(w_part, 3 * 16)
            split_hi(act, N_SMALL2)
            end_stage(act, 7)

        def dve_7(dve):
            begin_stage(dve, 7)
            dve.drain().then_inc(res_done, 2)
            for k in range(KT):
                dve.wait_ge(x_hi_done, SPLITS[7] + k + 1)
                dve.tensor_tensor(ha_lo[:, k, :], merged[:, k, :], ha_hi[:, k, :].bitcast(F32),
                                  ALU.subtract).then_inc(x_lo_done, 1)
            with dve.Fori(0, 4) as j:
                for b in range(2):
                    n = N_OUT1 + b
                    split_lo(dve, n + 1, adv=j)
                    projected(dve, n, adv=j)
                    dve.wait_ge(xt_loaded[b], 16 * j + 16)
                    dve.scalar_tensor_tensor(row(x1, 2 * j + b), acc[:, n % 2, :], ada[:, 16:24][:, bass.ds(2 * j + b, 1)],
                                             xt_tile[:, b, :], ALU.mult, ALU.add).then_inc(acc_free[n % 2], 1)
                    dve.drain().then_inc(res_done, 1)
            end_stage(dve, 7)

        def pool_7(pool):
            begin_stage(pool, 7)
            with pool.Fori(0, 4) as j:
                for b in range(2):
                    wait_here(pool, res_done, 2 * j + b + 1)
                    pool.dma_start(xt_tile[:, b, :], row(xt_scr, 2 * j + b)).then_inc(xt_loaded[b], 16)
            end_stage(pool, 7)

        ar = arena()
        sq8 = ar("sq8", [P, 2, T])
        root8 = ar("root8", [P, T])
        rstd8 = ar("rstd8", [P, T])
        root9 = ar("root9", [P, T])
        rstd9 = ar("rstd9", [P, T])
        v8 = ar("v8", [P, 2, T])
        norm8, norm9 = Norm(2), Norm(3)
        x1_done, v8_done, x1_saved = sem("x1_done"), sem("v8_done"), sem("x1_saved")

        def sp_8(sp):
            wait_here(sp, lo_done, N_SMALL2 - 1)
            sp.dma_start(w_raw[:, N_SMALL2 % 2, :, 0:32], cols(w_in2f, MI, 32)).then_inc(w_loaded[N_SMALL2 % 2], 16)
            sp.dma_start(w_raw[:, N_SMALL2 % 2, :, 32:64], cols(w_in2f, MF, 32)).then_inc(w_part, 16)
            sp.dma_start(w_raw[:, N_SMALL2 % 2, :, 64:P], cols(w_in2f, GA, 64)).then_inc(w_part, 16)
            load_w(sp, N_MG, cols(w_in2f, MG))
            sp.wait_ge(x1_done, KT)
            sp.dma_start(x1_scr, x1[:, :, :]).then_inc(x1_saved, 16)

        w_in2f = w_in2.rearrange("a d c -> (a d) c")

        def pe_8(pe):
            begin_stage(pe, 8)
            norm8.pe(pe, lambda f: sq8[:, f % 2, :])
            pe.wait_ge(norm8.rooted, norm8.use + 1)
            norm9.pe(pe, lambda f: sq8[:, f % 2, :])
            end_stage(pe, 8)

        def act_8(act):
            begin_stage(act, 8)
            norm8.act(act, x1, sq8, root8)
            for f in range(KT):
                act.wait_ge(x1_done, f + 1)
                if f >= 2:
                    act.wait_ge(norm9.summed, norm9.tiles + f - 1)
                act.activation(sq8[:, f % 2, :], x1[:, f, :], ACT.Square).then_inc(norm9.squared, 1)
            norm9.act_root(act, root9)
            for f in range(KT):
                act.wait_ge(v8_done, f + 1)
                act.activation(ha_hi[:, f, :], v8[:, f % 2, :], ACT.Copy).then_inc(x_hi_done, 1)
            end_stage(act, 8)

        def dve_8(dve):
            begin_stage(dve, 8)
            norm8.dve(dve, root8, rstd8)
            dve.drain()
            for f in range(KT):
                dve.scalar_tensor_tensor(x1[:, f, :], x1[:, f, :], col1("final_norm_w", f), rstd8[:, :],
                                         ALU.mult, ALU.mult).then_inc(x1_done, 1)
            norm9.dve(dve, root9, rstd9)
            dve.drain()
            for f in range(KT):
                dve.scalar_tensor_tensor(v8[:, f % 2, :], x1[:, f, :], vec2[:, VEC2["norm_g_2"][0] + f:][:, 0:1],
                                         rstd9[:, :], ALU.mult, ALU.mult).then_inc(v8_done, 1)
                dve.wait_ge(x_hi_done, SPLITS[8] + f + 1)
                dve.tensor_tensor(ha_lo[:, f, :], v8[:, f % 2, :], ha_hi[:, f, :].bitcast(F32), ALU.subtract)
                dve.drain()
            end_stage(dve, 8)

        ar = Region(v8_end := ar.at, arena_end)
        bias_rows = ar("bias_rows", [P, 3 * P])
        bias_tile = ar("bias_tile", [P, BANDW])
        bias_moved = sem("bias_moved")
        rel_rev = io["rel_bias_2"].rearrange("a h r -> (a h) r")

        def pool_8(pool):
            begin_stage(pool, 8)
            with pool.Fori(0, ML_HEADS) as h:
                pool.dma_start(bias_rows[:, P - 1:3 * P - 1],
                               rel_rev[bass.ds(h, 1), 0:2 * P].rearrange("a r -> (a r)").partition_broadcast(P)
                               ).then_inc(bias_moved, 16)
                wait_here(pool, bias_moved, 64 * h + 16)
                pool.tensor_copy(bias_rows[:, 0:P - 1], bias_rows[:, P - 1:P].to_broadcast([P, P - 1]))
                pool.tensor_copy(bias_rows[:, 3 * P - 1:3 * P], bias_rows[:, P - 1:P])
                pool.tensor_copy(bias_tile[:, 0:3 * P], bias_rows[:, P - 1:P].to_broadcast([P, 3 * P]))
                pool.drain()
                pool.dma_start(skew_scr.rearrange("(q w) -> q w", w=3 * P), bias_rows[:, :]).then_inc(bias_moved, 16)
                wait_here(pool, bias_moved, 64 * h + 32)
                pool.dma_start(bias_tile[:, 3 * P:BANDW],
                               skew_scr[P - 1:P - 1 + P * (3 * P - 1)].rearrange("(q w) -> q w", w=3 * P - 1)[:, 0:2 * P]
                               ).then_inc(bias_moved, 16)
                wait_here(pool, bias_moved, 64 * h + 48)
                pool.memset(bias_tile[0:HD, BANDW - HD:BANDW], MASKED)
                pool.memset(bias_tile[HD:P, 0:HD], MASKED)
                pool.drain()
                pool.dma_start(bias_scr[bass.ds(h, 1), :, :].rearrange("a q w -> q (a w)"), bias_tile[:, :]
                               ).then_inc(bias_moved, 16)
                wait_here(pool, bias_moved, 64 * h + 64)
            end_stage(pool, 8)

        b_gla = Region(at_arena, arena_end)("b_gla", [P, NCHUNK, 1 + CHUNK])
        keep = Region(at_arena + (NCHUNK * (1 + CHUNK) * 4 + 31) // 32 * 32, arena_end)
        B_tok = keep("B_tok", [P, NT, 8])
        em_tok = keep("em_tok", [P, NT, 8])
        PAD = 3
        nxt = keep("nxt", [P, 4, T + 8])
        nxt_t = nxt[:, :, PAD:PAD + T]
        at_arena2 = keep.at
        y2 = Region(at_ya + big, at_ya + 2 * big)("y2", [P, KT, T])
        ar = Region(at_arena2, arena_end)
        spa = {k: ar(f"spa_{k}", [P, T]) for k in ("u", "e", "relu", "s", "s2", "p")}
        ga_t = ar("ga_t", [P, T])
        ar = Region(at_ya, at_ya + big)
        spm = {k: ar(f"spm_{k}", [32, T]) for k in ("u", "e", "relu", "s", "s2", "p")}
        ig9 = ar("ig9", [32, T])
        f9 = ar("f9", [32, T])
        m9, em9 = spm["relu"], spm["s2"]
        softplus_ml, softplus_al = Softplus(1), Softplus(2)
        gates_read, alpha_mul, m_ready, em_ready = sem("gates_read"), sem("alpha_mul"), sem("m_ready"), sem("em_ready")
        ab_ready, turned9 = sem("ab_ready"), sem("turned9")

        def sp_9(sp):
            for j in range(1, PAIRS):
                load_w(sp, N_MG + j, cols(w_in2f, MG + P * j))
            for j in range(2):
                load_w(sp, N_GG + j, cols(w_in2f, GG + P * j))

        def act_9(act):
            begin_stage(act, 9)

            def silu_gate(n, i):
                split_hi(act, n + 1)
                projected(act, n)
                act.activation(y2[:, i, :], acc[:, n % 2, :], ACT.Silu).then_inc(acc_free[n % 2], 1)

            split_hi(act, N_MG)
            projected(act, N_SMALL2)
            act.wait_ge(x1_saved, 16)
            act.activation(ig9[:, :], acc[0:32, N_SMALL2 % 2, :], ACT.Identity, bias=gate_bias2[0:32, :])
            act.activation(ga_t[64:64 + GLA_RANK, :], acc[64:64 + GLA_RANK, N_SMALL2 % 2, :], ACT.Copy)
            act.drain().then_inc(gates_read, 1)
            softplus_ml.act(act, spm["u"][:, :], spm["e"][:, :], spm["relu"][:, :])
            softplus_al.act(act, spa["u"][:, :], spa["e"][:, :], spa["relu"][:, :])
            for j in range(PAIRS):
                silu_gate(N_MG + j, 3 + j)
            split_hi(act, N_GG + 1)
            act.wait_ge(m_ready, 1)
            act.activation(em9[:, :], m9[:, :], ACT.Exp, scale=-1.0).then_inc(em_ready, 1)
            projected(act, N_GG)
            act.activation(y2[:, 6, :], acc[:, N_GG % 2, :], ACT.Silu).then_inc(acc_free[N_GG % 2], 1)
            act.wait_ge(turned9, 1)
            for dst, bank in ((B_tok, 2), (em_tok, 3)):
                act.activation(dst[:, :, :], work[:, bank, 0:NT * 32].rearrange("p (t h) -> p t h", h=32)[:, :, 0:8], ACT.Copy)
            silu_gate(N_GG + 1, 7)
            for i in range(4):
                n = N_BAND + i
                split_hi(act, n + 1)
                projected(act, n)
                act.activation(nxt_t[:, i, :], acc[:, n % 2, :], ACT.Copy).then_inc(acc_free[n % 2], 1)
            act.drain().then_inc(nxt_ready, 4)
            end_stage(act, 9)

        def pe_9(pe):
            begin_stage(pe, 9)
            project(pe, N_SMALL2, ha_hi, ha_lo)
            pe.wait_ge(gates_read, 1)
            for h in range(2):
                mm = pe.matmul(work[:, h, :], w_alpha[64:64 + GLA_RANK, :],
                               ga_t[64:64 + GLA_RANK, h * HALF:(h + 1) * HALF], start=True, stop=True)
            mm.then_inc(alpha_mul, 1)
            for j in range(PAIRS):
                project(pe, N_MG + j, ha_hi, ha_lo)
            project(pe, N_GG, ha_hi, ha_lo)
            pe.wait_ge(ab_ready, 1)
            pe.wait_ge(em_ready, 1)
            for src, bank in ((spm["u"], 2), (em9, 3)):
                for i in range(NT):
                    mm = pe.transpose(work[:, bank, i * 32:(i + 1) * 32], src[:, i * P:(i + 1) * P], ident[0:32, 0:32])
            mm.then_inc(turned9, 1)
            project(pe, N_GG + 1, ha_hi, ha_lo)
            for i in range(4):
                project(pe, N_BAND + i, ha_hi, ha_lo)
            end_stage(pe, 9)

        def dve_9(dve):
            begin_stage(dve, 9)
            split_lo(dve, N_MG)
            projected(dve, N_SMALL2)
            dve.wait_ge(gates_read, 1)
            dve.tensor_scalar(spm["u"][:, :], acc[32:64, N_SMALL2 % 2, :], gate_bias2[32:64, :], -1.0, ALU.add,
                              ALU.mult).then_inc(acc_free[N_SMALL2 % 2], 1)
            dve.drain().then_inc(softplus_ml.ready, 1)
            dve.wait_ge(alpha_mul, 1)
            dve.tensor_scalar(spa["u"][:, :], work[:, 0:2, :].rearrange("p a b -> p (a b)"),
                              vec2[:, VEC2["b_alpha_2"][0]:VEC2["b_alpha_2"][1]], -1.0, ALU.add, ALU.mult)
            dve.drain().then_inc(softplus_al.ready, 1)
            softplus_ml.dve_ratio(dve, *(spm[k][:, :] for k in ("e", "s", "s2")))
            split_lo(dve, N_MG + 1)
            softplus_ml.dve_series(dve, *(spm[k][:, :] for k in ("relu", "s", "s2", "p")))
            split_lo(dve, N_MG + 2)
            dve.drain()
            lf = spm["e"]
            dve.tensor_scalar(lf[:, :], spm["p"][:, :], -1.0, None, ALU.mult)
            dve.drain()
            dve.tensor_tensor_scan(f9[:, :], lf[:, :], zero_col[0:32, :].to_broadcast([32, T]), 0.0, ALU.add, ALU.add)
            dve.tensor_tensor_scan(m9[:, :], lf[:, :], ig9[:, :], 0.0, ALU.add, ALU.max).then_inc(m_ready, 1)
            dve.drain()
            split_lo(dve, N_GG)
            dve.tensor_tensor(spm["u"][:, :], ig9[:, :], f9[:, :], ALU.subtract)
            dve.tensor_tensor(spm["s"][:, :], f9[:, :], m9[:, :], ALU.subtract)
            dve.drain().then_inc(ab_ready, 1)
            softplus_al.dve_ratio(dve, *(spa[k][:, :] for k in ("e", "s", "s2")))
            split_lo(dve, N_GG + 1)
            softplus_al.dve_series(dve, *(spa[k][:, :] for k in ("relu", "s", "s2", "p")))
            split_lo(dve, N_BAND)
            dve.drain()
            la = spa["u"]
            dve.tensor_scalar(la[:, :], spa["p"][:, :], -1.0 / GLA_TAU, None, ALU.mult)
            dve.drain()
            for c in range(NCHUNK):
                dve.tensor_tensor_scan(b_gla[:, c, 1:1 + CHUNK], la[:, c * CHUNK:(c + 1) * CHUNK],
                                       zero_col[:, :].to_broadcast([P, CHUNK]), 0.0, ALU.add, ALU.add)
            for i in range(4):
                split_lo(dve, N_BAND + i + 1)
            end_stage(dve, 9)

        def pool_9(pool):
            begin_stage(pool, 9)
            pool.memset(b_gla[:, :, 0:1], 0.0)
            pool.memset(nxt[:, :, 0:PAD], 0.0)
            pool.wait_ge(ab_ready, 1)
            pool.dma_start(ml_a_scr, spm["s"][0:8, :]).then_inc(sums_saved, 16)
            pool.wait_ge(sums_saved, 48)
            end_stage(pool, 9)

        ar = Region(at_arena2, arena_end)
        bq = ar("bq", [P, T])
        bk = ar("bk", [P, T])
        bv_tok = ar("bv_tok", [P, NT, P])
        band_max = ar("band_max", [P, 2 * NT])
        band_sum = ar("band_sum", [P, 2 * NT])
        band_inv = ar("band_inv", [P, 2 * NT])
        ar = Region(at_ya, at_ya + big)
        band_bias = ar("band_bias", [P, 2, BANDW])
        band_p = ar("band_p", [P, 2, BANDW])
        band_pt = ar("band_pt", [P, 2, BAND_TILES, P])
        att_tok = ar("att_tok", [P, 2 * NT, HD])
        BU = 2 * NT
        FILLS = FILLS2 + 4 * (FOX_HEADS - 1)
        bias_loaded, band_gated = sem("bias_loaded"), sem("band_gated")
        V5, U5 = FOX_HEADS, FOX_HEADS * NT
        C5 = FOX_HEADS * FC
        N5 = 4 * FOX_HEADS
        tok_done, feat_turned = sem("tok_done"), sem("feat_turned")
        HD_SCALE = float(HD) ** -0.5

        def band_tiles(u):
            return min(u // 2, BAND_TILES - 1) + 1

        def band_chunks(u):
            first = sum(1 if band_tiles(v) <= 4 else 2 for v in range(u))
            n = band_tiles(u)
            return [(first, 0, n)] if n <= 4 else [(first, 0, 3), (first + 1, 3, n)]

        BC = band_chunks(BU)[0][0]

        def sp_10(sp):
            for i, off in enumerate((AQ, AK, AV, AG)):
                load_w(sp, N_BAND + i, cols(w_in2f, off))
            with sp.Fori(0, PAIRS - 1) as p:
                for i, off in enumerate((AQ, AK, AV, AG)):
                    load_w(sp, N_BAND + 4 + i, cols(w_in2f, off + P + P * p), adv=2 * p)

        def pool_10(pool):
            begin_stage(pool, 10)
            with pool.Fori(0, PAIRS) as p:
                wait_here(pool, band_gated, p + 1)
                pool.dma_start(band_bias[:, :, :], bias_scr[bass.ds(2 * p, 2), :, :].rearrange("h q w -> q h w")
                               ).then_inc(bias_loaded, 16)
            end_stage(pool, 10)

        def pe_10(pe):
            begin_stage(pe, 10)
            with pe.Fori(0, PAIRS) as p:

                def fill(q):
                    project_part(pe, N_BAND + 4 + q // 4, q % 4, FILLS + 4 * p + q // 4, adv=2 * p)

                def scores(u):
                    m, r = divmod(u, 2)
                    k0 = m + 1 - band_tiles(u)
                    for c, a, b in band_chunks(u):
                        if c >= 2:
                            pe.wait_ge(logits_done, C5 + BC * p + c - 1)
                        pe.matmul(work[:, c % 2, 0:(b - a) * P], bq[r * HD:(r + 1) * HD, m * P:(m + 1) * P],
                                  bk[r * HD:(r + 1) * HD, (k0 + a) * P:(k0 + b) * P], start=True, stop=True).then_inc(qk_done, 1)

                def turn_probs(u):
                    pe.wait_ge(exp_done, U5 + BU * p + u + 1)
                    for c, a, b in band_chunks(u):
                        if c >= 2:
                            pe.wait_ge(p_copied, C5 + BC * p + c - 1)
                        for t in range(a, b):
                            mm = pe.transpose(work[:, 2 + c % 2, (t - a) * P:(t - a + 1) * P], band_p[:, u % 2, t * P:(t + 1) * P],
                                              ident[:, :])
                        mm.then_inc(p_turned, 1)

                def weigh_values(u):
                    m, r = divmod(u, 2)
                    n = band_tiles(u)
                    for c, a, b in band_chunks(u):
                        pe.wait_ge(p_copied, C5 + BC * p + c + 1)
                        for t in range(a, b):
                            mm = pe.matmul(acc[:, 1, u * HD:(u + 1) * HD], band_pt[:, u % 2, t, :],
                                           bv_tok[:, m + 1 - n + t, r * HD:(r + 1) * HD], start=(t == 0), stop=(t == n - 1))
                    mm.then_inc(pv_done, 1)

                pe.wait_ge(band_gated, p + 1)
                pe.wait_ge(nxt_ready, N5 + 4 * p + 4)
                for b in range(NT):
                    mm = pe.transpose(work[:, 2 + b // 4, (b % 4) * P:(b % 4 + 1) * P], nxt_t[:, 2, b * P:(b + 1) * P], ident[:, :])
                mm.then_inc(v_turned, 1)
                pe.wait_ge(taken, V5 + p + 1)
                scores(0)
                scores(1)
                fill(0)
                pe.wait_ge(v_ready, V5 + p + 1)
                for u in range(BU):
                    if 0 < u < BU - 1:
                        fill(u)
                    turn_probs(u)
                    if u + 2 < BU:
                        scores(u + 2)
                    weigh_values(u)
                fill(BU - 1)
                pe.wait_ge(tok_done, p + 1)
                for b in range(NT):
                    mm = pe.transpose(work[:, 2 + b // 4, (b % 4) * P:(b % 4 + 1) * P], att_tok[:, 2 * b:2 * b + 2, :], ident[:, :])
                mm.then_inc(feat_turned, 1)
            end_stage(pe, 10)

        def act_10(act):
            begin_stage(act, 10)
            with act.Fori(0, PAIRS) as p:

                def exps(u):
                    act.wait_ge(max_done, U5 + BU * p + u + 1)
                    w = band_tiles(u) * P
                    act.activation(band_p[:, u % 2, 0:w], band_p[:, u % 2, 0:w], ACT.Exp, bias=band_max[:, u:u + 1],
                                   accum_out=band_sum[:, u:u + 1]).then_inc(exp_done, 1)

                def read_next(h):
                    i, half = divmod(h, 2)
                    read_half(act, N_BAND + 4 + i, half, FILLS + 4 * p + i, nxt_t[:, i, :], adv=2 * p)

                act.activation(row(y2, p), nxt_t[:, 3, :], ACT.Silu)
                act.wait_ge(v_turned, V5 + p + 1)
                act.activation(bv_tok[:, :, :], work[:, 2:4, :], ACT.Copy).then_inc(v_ready, 1)
                act.wait_ge(taken, V5 + p + 1)
                exps(0)
                for u in range(BU):
                    if u % 4 == 1:
                        split_hi(act, N_BAND + 5 + u // 4, adv=2 * p)
                    if u + 1 < BU:
                        exps(u + 1)
                    for c, a, b in band_chunks(u):
                        act.wait_ge(p_turned, C5 + BC * p + c + 1)
                        act.activation(band_pt[:, u % 2, a:b, :], work[:, 2 + c % 2, 0:(b - a) * P], ACT.Copy).then_inc(p_copied, 1)
                    if u % 2 == 1:
                        read_next(u // 2)
                act.drain().then_inc(nxt_ready, 4)
            end_stage(act, 10)

        def dve_10(dve):
            begin_stage(dve, 10)
            dve.drain().then_inc(band_gated, 1)
            with dve.Fori(0, PAIRS) as p:
                dve.wait_ge(nxt_ready, N5 + 4 * p + 4)
                dve.tensor_copy(bq[:, :], nxt_t[:, 0, :])
                dve.tensor_copy(bk[:, :], nxt_t[:, 1, :])
                dve.drain().then_inc(taken, 1)
                dve.wait_ge(bias_loaded, 16 * p + 16)
                for u in range(BU):
                    if u >= 2:
                        dve.wait_ge(p_turned, C5 + BC * p + band_chunks(u - 1)[0][0])
                    w = band_tiles(u) * P
                    for c, a, b in band_chunks(u):
                        dve.wait_ge(qk_done, C5 + BC * p + c + 1)
                        dve.scalar_tensor_tensor(band_p[:, u % 2, a * P:b * P], work[:, c % 2, 0:(b - a) * P], HD_SCALE,
                                                 band_bias[:, u % 2, BANDW - w + a * P:BANDW - w + b * P],
                                                 ALU.mult, ALU.add).then_inc(logits_done, 1)
                    dve.drain()
                    dve.tensor_reduce(band_max[:, u:u + 1], band_p[:, u % 2, 0:w], AX.X, ALU.max,
                                      negate=True).then_inc(max_done, 1)
                    if u % 4 == 2:
                        split_lo(dve, N_BAND + 5 + u // 4, adv=2 * p)
                dve.wait_ge(pv_done, U5 + BU * p + BU)
                dve.reciprocal(band_inv[:, :], band_sum[:, :])
                dve.drain()
                dve.tensor_tensor(att_tok[:, :, :], acc[:, 1, :].rearrange("p (u d) -> p u d", d=HD),
                                  band_inv[:, :].unsqueeze(2).to_broadcast([P, BU, HD]), ALU.mult).then_inc(tok_done, 1)
                dve.wait_ge(feat_turned, p + 1)
                dve.tensor_tensor(row(y2, p), work[:, 2:4, :].rearrange("p a b -> p (a b)"), row(y2, p), ALU.mult)
                dve.drain().then_inc(band_gated, 1)
            end_stage(dve, 10)

        ar = Region(at_arena2, arena_end)
        ml_conv = ar("ml_conv", [P, 2, T])
        mq_t = ar("mq_t", [P, T])
        mk_t = ar("mk_t", [P, T])
        mv_tok = ar("mv_tok", [P, 2 * NT, HD + 1])
        den = ar("den", [P, 2 * NT])
        den_abs = ar("den_abs", [P, 2 * NT])
        ss11 = ar("ss11", [P, 2 * NT])
        root11 = ar("root11", [P, 2 * NT])
        ar = Region(at_ya, at_ya + big)
        BLOCKS = NT * (NT + 1) // 2
        at_pt = ar.at
        ml_pt = ar("ml_pt", [P, BLOCKS, P])
        h_sq = Region(at_pt, ar.at)("h_sq", [P, 2 * NT, HD])
        so = ar("so", [P, T])
        h_tok = ar("h_tok", [P, 2 * NT, HD])
        ar = Region(at_arena2 + 20 * T + 512, arena_end)
        a_bc = ar("a_bc", [P, 2, T])
        abc_loaded, ml_gated = sem("abc_loaded"), sem("ml_gated")
        ml_conved, mqk_ready, so_ready = sem("ml_conved"), sem("mqk_ready"), sem("so_ready")
        d_done, pt_done, pt_masked = sem("d_done"), sem("pt_done"), sem("pt_masked")
        V10, U10, C10, FILLS10 = V5 + PAIRS, U5 + PAIRS * BU, C5 + PAIRS * BC, FILLS + PAIRS * 4
        ss_ready, root_ready = sem("ss_ready"), sem("root_ready")
        SLOTS = HALF // (HD + 1)
        out_banks = [acc[:, 1, 0:HALF], acc[:, 1, HALF:2 * HALF], work[:, 2, :]]
        FILL_UNITS = [1, 2, 3, 5, 6, 7, 9, 10, 11, 13, 14, 15]

        def pt_row(jb):
            at = jb * NT - jb * (jb - 1) // 2
            return ml_pt[:, at:at + NT - jb, :].rearrange("p a b -> p (a b)")

        def ml_chunks(u):
            widths = [(NT - v % NT) * P for v in range(u + 1)]
            first = sum((w + HALF - 1) // HALF for w in widths[:-1])
            return [(first + i, a, min(a + HALF, widths[-1])) for i, a in enumerate(range(0, widths[-1], HALF))]

        MC = 2 * sum(((NT - jb) * P + HALF - 1) // HALF for jb in range(NT))

        def slot_groups():
            for g in range(0, 2 * NT, SLOTS):
                n = min(SLOTS, 2 * NT - g)
                yield slice(g, g + n), n, out_banks[g // SLOTS][:, 0:n * (HD + 1)].rearrange("p (u e) -> p u e", e=HD + 1)

        def sp_11(sp):
            for i, off in enumerate((MQ, MK, MV, MO)):
                load_w(sp, N_ML + i, cols(w_in2f, off))
            with sp.Fori(0, PAIRS - 1) as p:
                for i, off in enumerate((MQ, MK, MV, MO)):
                    load_w(sp, N_ML + 4 + i, cols(w_in2f, off + P + P * p), adv=2 * p)

        def pool_11(pool):
            begin_stage(pool, 11)
            pool.memset(mv_tok[:, :, HD:HD + 1], 1.0)
            zero_fill = pool.to_reg(0.0)
            with pool.Fori(0, PAIRS) as p:
                wait_here(pool, ml_gated, p + 1)
                for r in range(2):
                    pool.dma_start(a_bc[:, r, :], ml_a_scr[bass.ds(2 * p + r, 1), :].rearrange("a t -> (a t)").partition_broadcast(P)
                                   ).then_inc(abc_loaded, 16)
                wait_here(pool, so_ready, p + 1)
                pool.tensor_tensor(row(y2, 3 + p), row(y2, 3 + p), so[:, :], ALU.mult)
                for u in range(BU):
                    wait_here(pool, pt_done, MC * p + ml_chunks(u)[0][0] + 1)
                    diag = pt_row(u % NT)[:, 0:P]
                    pool.affine_select(out=diag, in_=diag, compare_op=ALU.is_ge, fill=zero_fill, base=0,
                                       pattern=[[1, P]], channel_multiplier=-1).then_inc(pt_masked, 1)
            end_stage(pool, 11)

        def pe_11(pe):
            begin_stage(pe, 11)
            with pe.Fori(0, PAIRS) as p:

                def fill(q):
                    project_part(pe, N_ML + 4 + q // 4, q % 4, FILLS10 + 4 * p + q // 4, adv=2 * p)

                def scores(u):
                    r, jb = divmod(u, NT)
                    for c, a, b in ml_chunks(u):
                        if c >= 2:
                            pe.wait_ge(pt_done, MC * p + c - 1)
                        pe.matmul(work[:, c % 2, 0:b - a], mk_t[r * HD:(r + 1) * HD, jb * P:(jb + 1) * P],
                                  mq_t[r * HD:(r + 1) * HD, jb * P + a:jb * P + b], start=True, stop=True).then_inc(qk_done, 1)

                def weigh_values(u):
                    r, tb = divmod(u, NT)
                    s = 2 * tb + r
                    o = out_banks[s // SLOTS][:, s % SLOTS * (HD + 1):(s % SLOTS + 1) * (HD + 1)]
                    for jb in range(tb + 1):
                        mm = pe.matmul(o, pt_row(jb)[:, (tb - jb) * P:(tb - jb + 1) * P], mv_tok[:, 2 * jb + r, :],
                                       start=(jb == 0), stop=(jb == tb))
                    mm.then_inc(pv_done, 1)

                pe.wait_ge(ml_gated, p + 1)
                pe.wait_ge(nxt_ready, N5 + 4 * (PAIRS + 1) + 4 * p)
                for b in range(NT):
                    mm = pe.transpose(work[:, 2 + b // 4, (b % 4) * P:(b % 4 + 1) * P], nxt_t[:, 2, b * P:(b + 1) * P], ident[:, :])
                mm.then_inc(v_turned, 1)
                for q in range(4):
                    fill(q)
                pe.wait_ge(mqk_ready, 2 * p + 2)
                scores(0)
                scores(1)
                pe.wait_ge(v_ready, V10 + p + 1)
                for u in range(BU):
                    if u in FILL_UNITS[:-1]:
                        fill(4 + FILL_UNITS.index(u))
                    pe.wait_ge(pt_masked, BU * p + u + 1)
                    pe.wait_ge(pt_done, MC * p + ml_chunks(u)[-1][0] + 1)
                    if u == NT - 1:
                        weigh_values(u)
                    if u + 2 < BU:
                        scores(u + 2)
                    if u != NT - 1:
                        weigh_values(u)
                fill(4 + len(FILL_UNITS) - 1)
                pe.wait_ge(tok_done, PAIRS + p + 1)
                for b in range(NT):
                    mm = pe.transpose(acc[:, 1, b * P:(b + 1) * P], h_tok[:, 2 * b:2 * b + 2, :], ident[:, :])
                mm.then_inc(feat_turned, 1)
            end_stage(pe, 11)

        def act_11(act):
            begin_stage(act, 11)
            with act.Fori(0, PAIRS) as p:

                def read_next(h):
                    i, half = divmod(h, 2)
                    read_half(act, N_ML + 4 + i, half, FILLS10 + 4 * p + i, nxt_t[:, i, :], adv=2 * p)

                def exps(u):
                    r, jb = divmod(u, NT)
                    if u == NT:
                        act.wait_ge(pv_done, U10 + BU * p + NT)
                    act.activation(pt_row(jb), a_bc[:, r, jb * P:], ACT.Exp, bias=B_tok[:, jb, :][:, bass.ds(2 * p + r, 1)]
                                   ).then_inc(d_done, 1)

                split_hi(act, N_ML + 5, adv=2 * p)
                act.activation(so[:, :], nxt_t[:, 3, :], ACT.Sigmoid).then_inc(so_ready, 1)
                act.wait_ge(v_turned, V10 + p + 1)
                act.activation(mv_tok[:, :, 0:HD], work[:, 2:4, :].rearrange("p a (b d) -> p (a b) d", d=HD),
                               ACT.Copy).then_inc(v_ready, 1)
                for i, dst in enumerate((mq_t, mk_t)):
                    act.wait_ge(ml_conved, 2 * p + i + 1)
                    act.activation(dst[:, :], ml_conv[:, i, :], ACT.Silu).then_inc(mqk_ready, 1)
                for half in range(2):
                    read_next(half)
                act.wait_ge(abc_loaded, 32 * p + 32)
                exps(0)
                exps(1)
                for u in range(BU):
                    if u + 2 < BU:
                        exps(u + 2)
                    if u in (1, 6, 11):
                        split_hi(act, N_ML + 6 + u // 5, adv=2 * p)
                    if u in FILL_UNITS[1::2]:
                        read_next(2 + FILL_UNITS.index(u) // 2)
                act.drain().then_inc(nxt_ready, 4)
                act.wait_ge(ss_ready, p + 1)
                act.activation(root11[:, :], ss11[:, :], ACT.Sqrt, bias=eps_col[:, :], scale=1.0 / HD).then_inc(root_ready, 1)
            for a in range(2):
                act.drain().then_inc(acc_free[a], 4 * PAIRS)
            end_stage(act, 11)

        def dve_11(dve):
            begin_stage(dve, 11)
            dve.drain().then_inc(ml_gated, 1)
            with dve.Fori(0, PAIRS) as p:
                dve.wait_ge(nxt_ready, N5 + 4 * (PAIRS + 1) + 4 * p)
                for i in range(2):
                    conv_taps(dve, ml_conv[:, i, :], lambda k: nxt[:, i, k:k + T],
                              lambda k: vec2[:, VEC2["conv_w_2"][0] + 2 * PAIRS * k + PAIRS * i:][:, bass.ds(p, 1)]
                              ).then_inc(ml_conved, 1)
                    if i == 0:
                        split_lo(dve, N_ML + 5, adv=2 * p)
                for u in range(BU):
                    dve.wait_ge(d_done, BU * p + u + 1)
                    for c, a, b in ml_chunks(u):
                        dve.wait_ge(qk_done, C10 + MC * p + c + 1)
                        pt = pt_row(u % NT)[:, a:b]
                        dve.scalar_tensor_tensor(pt, work[:, c % 2, 0:b - a], HD_SCALE, pt, ALU.mult, ALU.mult
                                                 ).then_inc(pt_done, 1)
                    if u in (2, 7, 12):
                        split_lo(dve, N_ML + 6 + u // 5, adv=2 * p)
                dve.wait_ge(pv_done, U10 + BU * p + BU)
                for us, n, out11 in slot_groups():
                    dve.tensor_copy(den[:, us], out11[:, :, HD])
                dve.drain()
                dve.scalar_tensor_tensor(den_abs[:, :], den[:, :], -1.0, den[:, :], ALU.mult, ALU.max)
                dve.drain()
                dve.tensor_tensor(den[:, :].rearrange("p (t r) -> p t r", r=2), den_abs[:, :].rearrange("p (t r) -> p t r", r=2),
                                  em_tok[:, :, bass.ds(2 * p, 2)], ALU.max)
                dve.drain()
                dve.reciprocal(den_abs[:, :], den[:, :])
                dve.drain()
                for us, n, out11 in slot_groups():
                    dve.tensor_tensor(h_tok[:, us, :], out11[:, :, 0:HD],
                                      den_abs[:, us].unsqueeze(2).to_broadcast([P, n, HD]), ALU.mult)
                dve.drain()
                dve.tensor_tensor(h_sq[:, :, :], h_tok[:, :, :], h_tok[:, :, :], ALU.mult)
                dve.drain()
                dve.tensor_reduce(ss11[:, :], h_sq[:, :, :], AX.X, ALU.add).then_inc(ss_ready, 1)
                dve.wait_ge(root_ready, p + 1)
                dve.reciprocal(den[:, :], root11[:, :])
                dve.drain()
                dve.tensor_tensor(h_tok[:, :, :], h_tok[:, :, :], den[:, :].unsqueeze(2).to_broadcast([P, 2 * NT, HD]),
                                  ALU.mult).then_inc(tok_done, 1)
                dve.wait_ge(feat_turned, PAIRS + p + 1)
                dve.wait_ge(pt_masked, BU * p + BU)
                dve.scalar_tensor_tensor(row(y2, 3 + p), acc[:, 1, :], dcol(vec2, VEC2, "ml_norm_g_2", p), row(y2, 3 + p),
                                         ALU.mult, ALU.mult)
                dve.drain().then_inc(ml_gated, 1)
            end_stage(dve, 11)

        ar = Region(at_arena2, arena_end)
        gq_t = ar("gq_t", [P, T])
        gv_tok = ar("gv_tok", [P, NCHUNK, GLA_HEADS * GLA_DV])
        in_ha = Region(at_ha, at_ya)
        e_b = in_ha("e_b", [P, T])
        e_q = in_ha("e_q", [P, T])
        e_end = in_ha("e_end", [P, T])
        e_k = in_ha("e_k", [P, 2, NSUB, CHUNK])
        k_ref = in_ha("k_ref", [P, 2, NSUB, CHUNK])
        q_own = in_ha("q_own", [P, 2, NSUB, GLA_HEADS, SUB])
        q_dec = ar("q_dec", [P, 2, CHUNK])
        k_dec = ar("k_dec", [P, 2, CHUNK])
        k_tok = ar("k_tok", [P, 2, P])
        att_gla = ar("att_gla", [P, 2, GLA_HEADS, CHUNK])
        s_gla = ar("s_gla", [P, GLA_HEADS * GLA_DV])
        kv_own = ar("kv_own", [P, GLA_HEADS * GLA_DV])
        own = ar("own", [P, GLA_HEADS * GLA_DV])
        ss12 = ar("ss12", [P, NCHUNK * GLA_HEADS])
        root12 = ar("root12", [P, NCHUNK * GLA_HEADS])
        inv12 = ar("inv12", [P, NCHUNK * GLA_HEADS])
        o_tok = in_ha("o_tok", [P, NCHUNK, GLA_HEADS * GLA_DV])
        o_sq = in_ha("o_sq", [P, NCHUNK, GLA_HEADS * GLA_DV])
        gk_t, gv_t = nxt_t[:, 1, :], nxt_t[:, 2:4, :]
        own_ready, decay_args, decays_ready = sem("own_ready"), sem("decay_args"), sem("decays_ready")
        karg_done, kexp_done, chunk_ready, kdec_ready = sem("karg_done"), sem("kexp_done"), sem("chunk_ready"), sem("kdec_ready")
        kdec_turned, ktok_ready, gkv_done = sem("kdec_turned"), sem("ktok_ready"), sem("gkv_done")
        qdec_ready = sem("qdec_ready")
        gatt_done, gatt_masked, go_done, gstate_done, go_copied = (sem("gatt_done"), sem("gatt_masked"), sem("go_done"),
                                                                   sem("gstate_done"), sem("go_copied"))
        osq_done = sem("osq_done")
        V11 = V10 + PAIRS
        b_now = b_gla[:, :, 1:1 + CHUNK]
        b_ref = b_gla[:, :, 0:CHUNK].rearrange("p c (s t) -> p c s t", t=SUB)[:, :, :, 0:1]
        NXT_READY = N5 + 4 * (2 * PAIRS + 1)
        x1_back = sem("x1_back")

        w_out2 = io["w_out_2"].rearrange("a e d -> (a e) d")

        def at_chunk(x, c):
            return x[:, bass.ds(c * CHUNK, CHUNK)]

        def sp_12(sp):
            for i, off in enumerate((GQ, GK, GV, GV + P)):
                load_w(sp, N_GLA + i, cols(w_in2f, off))
            for i in range(2):
                load_w(sp, N_OUT2 + i, cols(w_out2, i * P))
            sp.wait_ge(stage_done, 4 * 12)
            sp.dma_start(x1[:, :, :], x1_scr).then_inc(x1_back, 16)

        def pool_12(pool):
            begin_stage(pool, 12)
            pool.memset(own[:, :], 0.0)
            pool.memset(s_gla[:, :], 0.0)
            pool.drain()
            for h in range(GLA_HEADS):
                pool.memset(own[h * GLA_DK:(h + 1) * GLA_DK, h * GLA_DV:(h + 1) * GLA_DV], 1.0)
                pool.drain()
            pool.drain().then_inc(own_ready, 1)
            pool.wait_ge(decays_ready, 1)

            def decay_ends(c, b):
                pool.tensor_tensor(k_dec[:, b, :], at_chunk(gk_t, c), at_chunk(e_end, c), ALU.mult).then_inc(kdec_ready, 1)
                pool.tensor_tensor(q_dec[:, b, :], at_chunk(gq_t, c), at_chunk(e_b, c), ALU.mult).then_inc(qdec_ready, 1)

            decay_ends(0, 0)
            decay_ends(1, 1)
            with pool.Fori(0, NCHUNK // 2 - 1) as i:
                for b in range(2):
                    wait_here(pool, go_done, 2 * i + b + 1)
                    decay_ends(2 * i + b + 2, b)
            end_stage(pool, 12)

        def pe_12(pe):
            begin_stage(pe, 12)
            pe.wait_ge(nxt_ready, NXT_READY)
            for c in range(NCHUNK):
                for i in range(2):
                    at = c * 2 + i
                    mm = pe.transpose(work[:, at // 4, at % 4 * P:(at % 4 + 1) * P], gv_t[:, i, c * P:(c + 1) * P], ident[:, :])
            mm.then_inc(v_turned, 1)
            pe.wait_ge(v_ready, V11 + 1)

            def turn_keys(c, b):
                pe.wait_ge(kdec_ready, c + 1)
                if not (isinstance(c, int) and c == 0):
                    pe.wait_ge(ktok_ready, c)
                pe.transpose(work[:, 3, 0:P], k_dec[:, b, :], ident[:, :]).then_inc(kdec_turned, 1)

            def attend(c, b):
                pe.wait_ge(chunk_ready, c + 1)
                for s in range(NSUB):
                    mm = pe.matmul(accf[:, b * HALF + s * GLA_HEADS * SUB:b * HALF + (s + 1) * GLA_HEADS * SUB], k_ref[:, b, s, :],
                                   q_own[:, b, s, :, :], start=True, stop=True)
                mm.then_inc(gatt_done, 1)

            def sum_keys(c, b):
                pe.wait_ge(ktok_ready, c + 1)
                pe.wait_ge(gstate_done, c + 1)
                pe.matmul(work[:, 2, 0:GLA_HEADS * GLA_DV], k_tok[:, b, :], row(gv_tok, c), start=True, stop=True
                          ).then_inc(gkv_done, 1)

            def outputs(c, b):
                pe.wait_ge(gatt_masked, c + 1)
                pe.wait_ge(qdec_ready, c + 1)
                pe.wait_ge(go_copied, c + 1)
                o = work[:, b, 0:GLA_HEADS * GLA_DV]
                for h in range(GLA_HEADS):
                    v = slice(h * GLA_DV, (h + 1) * GLA_DV)
                    pe.matmul(o[:, v], q_dec[:, b, :], s_gla[:, v], start=True, stop=False)
                    mm = pe.matmul(o[:, v], att_gla[:, b, h, :], row(gv_tok, c)[:, v], start=False, stop=True)
                mm.then_inc(go_done, 1)

            def chunk(c, b, ahead=True):
                if ahead:
                    turn_keys(c + 1, 1 - b)
                sum_keys(c, b)
                if ahead:
                    attend(c + 1, 1 - b)
                outputs(c, b)

            turn_keys(0, 0)
            attend(0, 0)
            with pe.Fori(0, NCHUNK // 2 - 1) as i:
                for b in range(2):
                    chunk(2 * i + b, b)
            chunk(NCHUNK - 2, 0)
            chunk(NCHUNK - 1, 1, ahead=False)
            pe.wait_ge(tok_done, 2 * PAIRS + 1)
            for i in range(2):
                for c in range(NCHUNK):
                    mm = pe.transpose(work[:, 2 * i + c // 4, c % 4 * P:(c % 4 + 1) * P], o_tok[:, c, i * P:(i + 1) * P], ident[:, :])
            mm.then_inc(feat_turned, 1)
            end_stage(pe, 12)

        def act_12(act):
            begin_stage(act, 12)
            act.drain().then_inc(go_copied, 2)
            act.activation(gq_t[:, :], nxt_t[:, 0, :], ACT.Copy, scale=float(GLA_DK) ** -0.5)
            act.wait_ge(v_turned, V11 + 1)
            act.activation(gv_tok[:, :, :], work[:, :, :], ACT.Copy).then_inc(v_ready, 1)
            act.activation(e_b[:, :].rearrange("p (c t) -> p c t", t=CHUNK), b_now, ACT.Exp)
            act.wait_ge(decay_args, 2)
            act.activation(e_q[:, :], e_q[:, :], ACT.Exp)
            act.activation(e_end[:, :], e_end[:, :], ACT.Exp)
            act.drain().then_inc(decays_ready, 1)

            def exp_keys(c, b):
                act.wait_ge(karg_done, c + 1)
                act.activation(e_k[:, b, :, :], e_k[:, b, :, :], ACT.Exp).then_inc(kexp_done, 1)

            def copy_keys(c, b):
                act.wait_ge(kdec_turned, c + 1)
                act.activation(k_tok[:, b, :], work[:, 3, 0:P], ACT.Copy).then_inc(ktok_ready, 1)

            def copy_outputs(c, b):
                act.wait_ge(go_done, c + 1)
                act.activation(row(o_tok, c), work[:, b, 0:GLA_HEADS * GLA_DV], ACT.Copy).then_inc(go_copied, 1)

            exp_keys(0, 0)
            exp_keys(1, 1)
            copy_keys(0, 0)
            with act.Fori(0, NCHUNK // 2 - 1) as i:
                for b in range(2):
                    copy_keys(2 * i + b + 1, 1 - b)
                    exp_keys(2 * i + b + 2, b)
                    copy_outputs(2 * i + b, b)
            copy_keys(NCHUNK - 1, 1)
            copy_outputs(NCHUNK - 2, 0)
            copy_outputs(NCHUNK - 1, 1)
            act.drain()
            act.activation(o_sq[:, :, :], o_tok[:, :, :], ACT.Square).then_inc(osq_done, 1)
            act.wait_ge(ss_ready, PAIRS + 1)
            act.activation(root12[:, :], ss12[:, :], ACT.Sqrt, bias=eps_col[:, :], scale=1.0 / GLA_DV).then_inc(root_ready, 1)
            end_stage(act, 12)

        def dve_12(dve):
            begin_stage(dve, 12)
            dve.drain().then_inc(gstate_done, 1)
            sub = dict(t=SUB)
            dve.tensor_tensor(e_q[:, :].rearrange("p (c s t) -> p c s t", s=NSUB, **sub), b_now.rearrange("p c (s t) -> p c s t", **sub),
                              b_ref.to_broadcast([P, NCHUNK, NSUB, SUB]), ALU.subtract).then_inc(decay_args, 1)
            dve.tensor_tensor(e_end[:, :].rearrange("p (c t) -> p c t", t=CHUNK), b_gla[:, :, CHUNK:CHUNK + 1].to_broadcast([P, NCHUNK, CHUNK]),
                              b_now, ALU.subtract).then_inc(decay_args, 1)
            dve.wait_ge(own_ready, 1)
            dve.wait_ge(decays_ready, 1)
            dve.tensor_tensor(e_q[:, :], e_q[:, :], gq_t[:, :], ALU.mult)
            dve.drain()
            own_rows = own[:, :].rearrange("p (h v) -> p h v", v=GLA_DV)[:, :, 0:1]

            def key_args(c, b):
                b_c = b_gla[:, bass.ds(c, 1), :].rearrange("p a t -> p (a t)")
                r_c = b_c[:, 0:CHUNK].rearrange("p (s t) -> p s t", t=SUB)[:, :, 0:1]
                dve.tensor_tensor(e_k[:, b, :, :], r_c.to_broadcast([P, NSUB, CHUNK]),
                                  b_c[:, 1:1 + CHUNK].unsqueeze(1).to_broadcast([P, NSUB, CHUNK]), ALU.subtract).then_inc(karg_done, 1)

            def operands(c, b):
                dve.wait_ge(kexp_done, c + 1)
                dve.scalar_tensor_tensor(k_ref[:, b, :, :], e_k[:, b, :, :], KEY_CAP,
                                         at_chunk(gk_t, c).unsqueeze(1).to_broadcast([P, NSUB, CHUNK]), ALU.min, ALU.mult)
                dve.tensor_tensor(q_own[:, b, :, :, :],
                                  at_chunk(e_q, c).rearrange("p (s t) -> p s t", t=SUB).unsqueeze(2).to_broadcast([P, NSUB, GLA_HEADS, SUB]),
                                  own_rows.unsqueeze(1).to_broadcast([P, NSUB, GLA_HEADS, SUB]), ALU.mult)
                dve.drain().then_inc(chunk_ready, 1)

            def mask_weights(c, b):
                dve.wait_ge(gatt_done, c + 1)
                dve.tensor_tensor(att_gla[:, b, :, :].rearrange("p h (s t) -> p s h t", t=SUB),
                                  accf[:, b * HALF:(b + 1) * HALF].rearrange("p (s h t) -> p s h t", s=NSUB, h=GLA_HEADS),
                                  causal01[:, :].rearrange("p (s t) -> p s t", t=SUB).unsqueeze(2).to_broadcast([P, NSUB, GLA_HEADS, SUB]),
                                  ALU.mult).then_inc(gatt_masked, 1)

            def update_state(c, b):
                dve.wait_ge(gkv_done, c + 1)
                dve.tensor_tensor(kv_own[:, :], work[:, 2, 0:GLA_HEADS * GLA_DV], own[:, :], ALU.mult)
                dve.drain()
                dve.wait_ge(go_done, c + 1)
                dve.scalar_tensor_tensor(s_gla[:, :], s_gla[:, :], at_chunk(e_b, c)[:, CHUNK - 1:CHUNK], kv_own[:, :],
                                         ALU.mult, ALU.add)
                dve.drain().then_inc(gstate_done, 1)

            key_args(0, 0)
            key_args(1, 1)
            operands(0, 0)
            with dve.Fori(0, NCHUNK // 2 - 1) as i:
                for b in range(2):
                    c = 2 * i + b
                    mask_weights(c, b)
                    operands(c + 1, 1 - b)
                    key_args(c + 2, b)
                    update_state(c, b)
            mask_weights(NCHUNK - 2, 0)
            operands(NCHUNK - 1, 1)
            update_state(NCHUNK - 2, 0)
            mask_weights(NCHUNK - 1, 1)
            update_state(NCHUNK - 1, 1)
            dve.wait_ge(osq_done, 1)
            heads = dict(d=GLA_DV)
            dve.tensor_reduce(ss12[:, :], o_sq[:, :, :].rearrange("p c (h d) -> p (c h) d", **heads), AX.X, ALU.add).then_inc(ss_ready, 1)
            dve.wait_ge(root_ready, PAIRS + 1)
            dve.reciprocal(inv12[:, :], root12[:, :])
            dve.drain()
            o_h = o_tok[:, :, :].rearrange("p c (h d) -> p (c h) d", **heads)
            dve.tensor_tensor(o_h, o_h, inv12[:, :].unsqueeze(2).to_broadcast([P, NCHUNK * GLA_HEADS, GLA_DV]), ALU.mult
                              ).then_inc(tok_done, 1)
            dve.wait_ge(feat_turned, 2 * PAIRS + 1)
            for i in range(2):
                g_col = vec2[:, VEC2["gla_norm_g_2"][0] + i:][:, 0:1]
                dve.scalar_tensor_tensor(y2[:, 6 + i, :], work[:, 2 * i:2 * i + 2, :].rearrange("p a b -> p (a b)"), g_col,
                                         y2[:, 6 + i, :], ALU.mult, ALU.mult)
            end_stage(dve, 12)


        def sp_13(sp):
            with sp.Fori(0, 3) as j:
                for b in range(2):
                    load_w(sp, N_OUT2 + 2 + b, cols(w_out2, (2 + b) * P + 2 * P * j), adv=j)

        def pool_13(pool):
            begin_stage(pool, 13)
            pool.dma_start(final_g[:, :], io["final_g_2"].partition_broadcast(P)).then_inc(g_loaded, 16)
            end_stage(pool, 13)

        def pe_13(pe):
            begin_stage(pe, 13)
            pe.wait_ge(x_lo_done, LO_SPLITS[13] + KT)
            with pe.Fori(0, 4) as j:
                for b in range(2):
                    project(pe, N_OUT2 + b, ha_hi, ha_lo, adv=j)
            end_stage(pe, 13)

        def act_13(act):
            begin_stage(act, 13)
            for k in range(KT):
                act.activation(ha_hi[:, k, :], y2[:, k, :], ACT.Copy).then_inc(x_hi_done, 1)
            with act.Fori(0, 3) as j:
                for b in range(2):
                    split_hi(act, N_OUT2 + b + 1, adv=j)
            split_hi(act, N_TILES - 1)
            end_stage(act, 13)

        def dve_13(dve):
            begin_stage(dve, 13)
            for k in range(KT):
                dve.wait_ge(x_hi_done, SPLITS[13] + k + 1)
                dve.tensor_tensor(ha_lo[:, k, :], y2[:, k, :], ha_hi[:, k, :].bitcast(F32), ALU.subtract).then_inc(x_lo_done, 1)

            def add_residual(n, x, adv=0):
                projected(dve, n, adv=adv)
                dve.tensor_tensor(x, acc[:, n % 2, :], x, ALU.add).then_inc(acc_free[n % 2], 1)

            dve.wait_ge(x1_back, 16)
            with dve.Fori(0, 3) as j:
                for b in range(2):
                    split_lo(dve, N_OUT2 + b + 1, adv=j)
                    add_residual(N_OUT2 + b, row(x1, 2 * j + b), adv=j)
            split_lo(dve, N_TILES - 1)
            add_residual(N_TILES - 2, x1[:, KT - 2, :])
            add_residual(N_TILES - 1, x1[:, KT - 1, :])
            end_stage(dve, 13)

        ar = Region(at_arena, arena_end)
        final_g = ar("final_g", [P, D])
        x2_sq = ar("x2_sq", [P, 2, D])
        ss14 = ar("ss14", [P, NT])
        root14 = ar("root14", [P, NT])
        inv14 = ar("inv14", [P, NT])
        out_tok = Region(at_ya + big, at_ya + 2 * big)("out_tok", [P, NT, D])
        g_loaded, x2_turned, x2_rooted, out_ready, stored = (sem("g_loaded"), sem("x2_turned"),
                                                                        sem("x2_rooted"), sem("out_ready"), sem("stored"))
        banks14 = [acc[:, 0, :], acc[:, 1, :], work[:, 0:2, :].rearrange("p a b -> p (a b)"),
                   work[:, 2:4, :].rearrange("p a b -> p (a b)")]

        def sp_14(sp):
            dst = out.rearrange("a (t p) d -> p (a t) d", p=P)
            for i in range(NT):
                sp.wait_ge(out_ready, i + 1)
                sp.dma_start(dst[:, i, :], out_tok[:, i, :]).then_inc(stored, 16)
            sp.wait_ge(stored, 16 * NT)

        def pool_14(pool):
            begin_stage(pool, 14)
            end_stage(pool, 14)

        def pe_14(pe):
            begin_stage(pe, 14)
            for i in range(NT):
                if i >= 4:
                    pe.wait_ge(out_ready, i - 3)
                for f in range(KT):
                    mm = pe.transpose(banks14[i % 4][:, f * P:(f + 1) * P], x1[:, f, i * P:(i + 1) * P], ident[:, :])
                mm.then_inc(x2_turned, 1)
            end_stage(pe, 14)

        def act_14(act):
            begin_stage(act, 14)
            for i in range(NT):
                act.wait_ge(x2_turned, i + 1)
                act.activation(x2_sq[:, i % 2, :], banks14[i % 4], ACT.Square, accum_out=ss14[:, i:i + 1])
                act.drain()
                act.activation(root14[:, i:i + 1], ss14[:, i:i + 1], ACT.Sqrt, bias=eps_col[:, :], scale=1.0 / D).then_inc(x2_rooted, 1)
            end_stage(act, 14)

        def dve_14(dve):
            begin_stage(dve, 14)
            dve.wait_ge(g_loaded, 16)
            for i in range(NT):
                dve.wait_ge(x2_rooted, i + 1)
                dve.reciprocal(inv14[:, i:i + 1], root14[:, i:i + 1])
                dve.drain()
                dve.scalar_tensor_tensor(out_tok[:, i, :], banks14[i % 4], inv14[:, i:i + 1], final_g[:, :],
                                         ALU.mult, ALU.mult).then_inc(out_ready, 1)
            end_stage(dve, 14)

        block = ctx.enter_context(nc.Block())

        @block.sync
        def _(sp):
            sp_0(sp)
            sp_1(sp)
            sp_2(sp)
            sp_3(sp)
            sp_4(sp)
            sp_5(sp)
            sp_6(sp)
            sp_7(sp)
            sp_8(sp)
            sp_9(sp)
            sp_10(sp)
            sp_11(sp)
            sp_12(sp)
            sp_13(sp)
            sp_14(sp)

        @block.scalar
        def _(act):
            act_0(act)
            act_1(act)
            act_2(act)
            act_3(act)
            act_4(act)
            act_5(act)
            act_6(act)
            act_7(act)
            act_8(act)
            act_9(act)
            act_10(act)
            act_11(act)
            act_12(act)
            act_13(act)
            act_14(act)

        @block.tensor
        def _(pe):
            pe_0(pe)
            pe_1(pe)
            pe_2(pe)
            pe_3(pe)
            pe_4(pe)
            pe_5(pe)
            pe_6(pe)
            pe_7(pe)
            pe_8(pe)
            pe_9(pe)
            pe_10(pe)
            pe_11(pe)
            pe_12(pe)
            pe_13(pe)
            pe_14(pe)

        @block.vector
        def _(dve):
            dve_0(dve)
            dve_1(dve)
            dve_2(dve)
            dve_3(dve)
            dve_4(dve)
            dve_5(dve)
            dve_6(dve)
            dve_7(dve)
            dve_8(dve)
            dve_9(dve)
            dve_10(dve)
            dve_11(dve)
            dve_12(dve)
            dve_13(dve)
            dve_14(dve)

        @block.gpsimd
        def _(pool):
            pool_0(pool)
            pool_1(pool)
            pool_2(pool)
            pool_3(pool)
            pool_4(pool)
            pool_5(pool)
            pool_6(pool)
            pool_7(pool)
            pool_8(pool)
            pool_9(pool)
            pool_10(pool)
            pool_11(pool)
            pool_12(pool)
            pool_13(pool)
            pool_14(pool)


_INS = ["x", "c", "w_ada", "b_ada", "norm_w", "w_in", "conv_w", "conv_b", "dt_bias", "a_log", "d_skip",
        "ssm_norm_w", "b_f", "b_gate", "w_proj_ssm", "w_proj_att", "w_out", "final_norm_w", "norm_g_2",
        "w_in_2", "b_gates_2", "conv_w_2", "w_alpha_2", "b_alpha_2", "rel_bias_2", "ml_norm_g_2",
        "gla_norm_g_2", "w_out_2", "final_g_2"]


def kernel(**inputs):
    import numpy as np
    import concourse.bacc as bacc
    from concourse.bass_utils import run_bass_kernel_spmd

    arrays = {name: np.ascontiguousarray(inputs[name]) for name in _INS}
    arrays["rel_bias_2"] = np.ascontiguousarray(arrays["rel_bias_2"][:, :, ::-1])
    nc = bacc.Bacc("TRN2", target_bir_lowering=False, num_devices=1)
    io = {name: nc.dram_tensor(f"in_{name}", a.shape, F32, kind="ExternalInput").ap() for name, a in arrays.items()}
    out = nc.dram_tensor("out", [1, T, D], F32, kind="ExternalOutput").ap()
    build(nc, io, out)
    r = run_bass_kernel_spmd(nc, [{f"in_{name}": a for name, a in arrays.items()}], core_ids=[0])
    return r.results[0]["out"]
```

```python
from contextlib import ExitStack

import concourse.bass as bass
from concourse import mybir

F32 = mybir.dt.float32
F32R = mybir.dt.float32r
ALU = mybir.AluOpType
ACT = mybir.ActivationFunctionType
AX = mybir.AxisListType

P = 128
T = 1024
D = 1024
KT = D // P
NT = T // P
HALF = 512
EPS = 1e-6
MASKED = -1e30

SSM_HEADS, SSM_P, SSM_N, SSM_G = 16, 64, 64, 2
HPG = SSM_HEADS // SSM_G
CHUNK = 128
NCHUNK = T // CHUNK
CONV_K = 4
XBC_TILES = (SSM_HEADS * SSM_P + 2 * SSM_G * SSM_N) // P
FOX_HEADS, FOX_D = 8, 128
Z_OFF = 0
XBC_OFF = D
DT_OFF = XBC_OFF + XBC_TILES * P
Q_OFF = DT_OFF + SSM_HEADS
K_OFF, V_OFF, ZA_OFF = Q_OFF + D, Q_OFF + 2 * D, Q_OFF + 3 * D
F_OFF = Q_OFF + 4 * D
G_OFF = F_OFF + FOX_HEADS

PAIRS = 3
HD = 64
W2 = PAIRS * P
AQ, AK, AV, AG = 0, W2, 2 * W2, 3 * W2
MQ, MK, MV, MO = 4 * W2, 5 * W2, 6 * W2, 7 * W2
ML_HEADS = 6
MI, MF = 8 * W2, 8 * W2 + ML_HEADS
MG = MF + ML_HEADS
GLA_HEADS, GLA_DK, GLA_DV, GLA_RANK = 4, 32, 64, 16
GQ = MG + W2
GK, GV = GQ + P, GQ + 2 * P
GA = GV + 2 * P
GG = GA + GLA_RANK
GLA_TAU = 16.0
SUB = 16
NSUB = CHUNK // SUB
KEY_CAP = 1e30
BAND_TILES = 5
BANDW = BAND_TILES * P

VEC1 = {}
VEC2 = {}


def _count(table, sizes):
    at = 0
    for name, rows in sizes:
        table[name] = (at, at + rows)
        at += rows
    return at


NVEC1 = _count(VEC1, [("b_ada", 24), ("norm_w", 8), ("conv_w", CONV_K * XBC_TILES), ("conv_b", XBC_TILES),
                      ("ssm_norm_w", 8), ("b_gate", 16), ("final_norm_w", 8), ("c", 8)])
NVEC2 = _count(VEC2, [("norm_g_2", 8), ("conv_w_2", CONV_K * 2 * PAIRS), ("b_alpha_2", 1), ("final_g_2", 8),
                      ("ml_norm_g_2", PAIRS), ("gla_norm_g_2", 2)])

N_SMALL1 = 0
N_XBC = 1
N_Z = N_XBC + XBC_TILES
N_GATT = N_Z + 16
N_MIX1 = N_GATT + KT // 2
N_FOX = N_MIX1 + 8
N_MIX2 = N_FOX + 4 * FOX_HEADS + KT // 2
N_OUT1 = N_MIX2 + 8
N_SMALL2 = N_OUT1 + 8
N_MG = N_SMALL2 + 1
N_GG = N_MG + PAIRS
N_BAND = N_GG + 2
N_ML = N_BAND + 4 * PAIRS
N_GLA = N_ML + 4 * PAIRS
N_OUT2 = N_GLA + 4
N_TILES = N_OUT2 + 8


def build(nc, io, out):
    ctx = ExitStack()
    with ctx:
        def psum(name, shape):
            return ctx.enter_context(nc.psum_tensor(name, shape, F32))

        def sem(name):
            return ctx.enter_context(nc.semaphore(name))

        def scratch(name, shape):
            return nc.dram_tensor(name, shape, F32, kind="Internal").ap()

        base = (nc.sbuf_base + 63) // 64 * 64
        big = KT * T * 4
        at_ha, at_ya = base, base + 2 * big
        at_ring = at_ya + 2 * big
        tile_bytes = KT * P * 4
        at_const = at_ring + 6 * tile_bytes
        at_arena = at_const + 5312
        arena_end = nc.sbuf_usable_end

        class Region:

            def __init__(self, at, end):
                self.at, self.end = at, end

            def __call__(self, name, shape, dt=F32):
                size = 4
                for s in shape[1:]:
                    size *= s
                t = nc.alloc_sbuf_tensor_at(name, shape, dt, offset=self.at)
                self.at += (size + 31) // 32 * 32
                assert self.at <= self.end, (name, self.at, self.end)
                return t

        def arena():
            return Region(at_arena, arena_end)

        def ya_region():
            return Region(at_ya, at_ya + 2 * big)

        ha = Region(at_ha, at_ya)
        ha_hi = ha("ha_hi", [P, KT, T], F32R)
        ha_lo = ha("ha_lo", [P, KT, T], F32R)
        ya = ya_region()
        ya_hi = ya("ya_hi", [P, KT, T], F32R)
        ya_lo = ya("ya_lo", [P, KT, T], F32R)
        rg = Region(at_ring, at_const)
        w_raw = rg("w_raw", [P, 2, KT, P])
        w_hi = rg("w_hi", [P, 2, KT, P], F32R)
        w_lo = rg("w_lo", [P, 2, KT, P], F32R)

        cst = Region(at_const, at_arena)
        ident = cst("ident", [P, P])
        ones = cst("ones", [P, P])
        causal01 = cst("causal01", [P, P])
        vec1 = cst("vec1", [P, NVEC1])
        vec2 = cst("vec2", [P, NVEC2])
        ada = cst("ada", [P, 24])
        a1 = cst("a1", [P, 8])
        silu_c = cst("silu_c", [P, 8])
        dskip = cst("dskip", [P, 8])
        zero_col = cst("zero_col", [P, 1])
        eps_col = cst("eps_col", [P, 1])
        eps2_col = cst("eps2_col", [P, 1])
        sp_bias = cst("sp_bias", [64, 1])
        sp_sign = cst("sp_sign", [64, 1])
        neg_a = cst("neg_a", [SSM_HEADS, 1])
        gate_bias2 = cst("gate_bias2", [64, 1])
        w_alpha = cst("w_alpha", [P, P])

        def row(x, i):
            return x[:, bass.ds(i, 1), :].rearrange("p a t -> p (a t)")

        def dcol(vec, table, name, i):
            return vec[:, table[name][0]:table[name][1]][:, bass.ds(i, 1)]

        acc = psum("acc", [P, 2, 2 * HALF])
        work = psum("work", [P, 4, HALF])
        accf = acc[:, :, :].rearrange("p a b -> p (a b)")

        xt_scr = scratch("xt_scr", [P, KT, T])
        res_scr = scratch("res_scr", [P, KT, T])
        root8_scr = scratch("root8_scr", [P, T])
        merged_scr = scratch("merged_scr", [P, KT, T])
        z_scr = scratch("z_scr", [P, KT, T])
        g_scr = scratch("g_scr", [P, KT, T])
        ga_scr = scratch("ga_scr", [P, KT, T])
        acs_scr = scratch("acs_scr", [SSM_HEADS, T])
        fcum_scr = scratch("fcum_scr", [FOX_HEADS, T])
        ml_a_scr = scratch("ml_a_scr", [8, T])
        skew_scr = scratch("skew_scr", [P * 3 * P])
        bias_scr = scratch("bias_scr", [ML_HEADS, P, BANDW])

        w_loaded = [sem("w_loaded0"), sem("w_loaded1")]
        w_part = sem("w_part")
        hi_done = sem("hi_done")
        lo_done = sem("lo_done")
        mm_done = sem("mm_done")
        acc_free = [sem("acc_free0"), sem("acc_free1")]
        SPLITS = {0: 0, 3: KT, 5: 2 * KT, 6: 3 * KT, 8: 4 * KT, 13: 5 * KT}
        x_hi_done = sem("x_hi_done")
        LO_SPLITS = {0: 0, 3: KT, 5: 2 * KT, 6: 3 * KT, 8: 4 * KT, 13: 5 * KT}
        x_lo_done = sem("x_lo_done")
        half_done = sem("half_done")
        fill_free = sem("fill_free")
        stage_done = sem("stage_done")

        def end_stage(eng, i):
            eng.drain().then_inc(stage_done, 1)

        def begin_stage(eng, i):
            eng.wait_ge(stage_done, 4 * i)

        ticks = {}

        def wait_here(eng, s, value):
            eng.wait_ge(s, value)
            if eng not in ticks:
                ticks[eng] = sem(f"tick{len(ticks)}")
            eng.sem_inc(ticks[eng], 1)

        def load_w(sp, n, src, adv=0):
            if n >= 2:
                wait_here(sp, lo_done, n - 1 + 2 * adv)
            sp.dma_start(w_raw[:, n % 2, :, :], src).then_inc(w_loaded[n % 2], 16)

        def split_hi(act, n, adv=0):
            act.wait_ge(w_loaded[n % 2], 16 * (n // 2 + 1) + 16 * adv)
            if n >= 2:
                act.wait_ge(mm_done, n - 1 + 2 * adv)
            act.activation(w_hi[:, n % 2, :, :], w_raw[:, n % 2, :, :], ACT.Copy).then_inc(hi_done, 1)

        def split_lo(dve, n, adv=0):
            dve.wait_ge(hi_done, n + 1 + 2 * adv)
            dve.tensor_tensor(w_lo[:, n % 2, :, :], w_raw[:, n % 2, :, :],
                              w_hi[:, n % 2, :, :].bitcast(F32), ALU.subtract).then_inc(lo_done, 1)

        def project(pe, n, x_hi, x_lo, adv=0, after=None):
            pe.wait_ge(lo_done, n + 1 + 2 * adv)
            if n >= 2:
                pe.wait_ge(acc_free[n % 2], n // 2 + adv)
            for k in range(KT):
                if after is not None:
                    pe.wait_ge(x_lo_done, after + k + 1)
                passes = [(w_hi, x_hi), (w_hi, x_lo), (w_lo, x_hi)]
                for i, (w, x) in enumerate(passes):
                    for h in range(2):
                        mm = pe.matmul(acc[:, n % 2, h * HALF:(h + 1) * HALF], w[:, n % 2, k, :],
                                       x[:, k, h * HALF:(h + 1) * HALF],
                                       start=(k == 0 and i == 0), stop=(k == KT - 1 and i == 2))
            mm.then_inc(mm_done, 1)

        def project_part(pe, n, part, m, adv=0):
            half, kpart = divmod(part, 2)
            if part == 0:
                pe.wait_ge(lo_done, n + 1 + 2 * adv)
            if kpart == 0:
                pe.wait_ge(fill_free, 2 * m + half + 1)
            for k in range(kpart * KT // 2, (kpart + 1) * KT // 2):
                passes = [(w_hi, ha_hi), (w_hi, ha_lo), (w_lo, ha_hi)]
                for i, (w, x) in enumerate(passes):
                    mm = pe.matmul(acc[:, 0, half * HALF:(half + 1) * HALF], w[:, n % 2, k, :],
                                   x[:, k, half * HALF:(half + 1) * HALF],
                                   start=(k == 0 and i == 0), stop=(k == KT - 1 and i == 2))
            if kpart:
                mm.then_inc(mm_done if half else half_done, 1)

        def read_half(act, n, half, m, dst, adv=0):
            if half:
                projected(act, n, adv=adv)
            else:
                act.wait_ge(half_done, m + 1)
            s = slice(half * HALF, (half + 1) * HALF)
            return act.activation(dst[:, s], acc[:, 0, s], ACT.Copy).then_inc(fill_free, 1)

        def projected(eng, n, adv=0):
            eng.wait_ge(mm_done, n + 1 + 2 * adv)

        def cols(w, off, width=P):
            return w.rearrange("(k p) c -> p k c", p=P)[:, :, bass.ds(off, width)]

        w_in, w_in2 = io["w_in"], io["w_in_2"]

        class Norm:
            squared = sem("norm_squared")
            summed = sem("norm_summed")
            rooted = sem("norm_rooted")

            def __init__(self, use):
                self.use = use
                self.tiles = use * KT

            def act(self, act, x, sq, root, beside=lambda f: None):
                for f in range(KT):
                    beside(f)
                    if f >= 2:
                        act.wait_ge(self.summed, self.tiles + f - 1)
                    act.activation(sq[:, f % 2, :], x[:, f, :], ACT.Square).then_inc(self.squared, 1)
                self.act_root(act, root)

            def act_root(self, act, root):
                act.wait_ge(self.summed, self.tiles + KT)
                act.activation(root[:, :], work[:, 0:2, :], ACT.Sqrt,
                               bias=eps_col[:, :], scale=1.0 / D).then_inc(self.rooted, 1)

            def pe(self, pe, sq_of):
                for f in range(KT):
                    pe.wait_ge(self.squared, self.tiles + f + 1)
                    for h in range(2):
                        mm = pe.matmul(work[:, h, :], ones[:, :], sq_of(f)[:, h * HALF:(h + 1) * HALF],
                                       start=(f == 0), stop=(f == KT - 1))
                    mm.then_inc(self.summed, 1)

            def dve(self, dve, root, rstd):
                dve.wait_ge(self.rooted, self.use + 1)
                dve.reciprocal(rstd[:, :], root[:, :])

        class Softplus:
            ready = sem("softplus_u_ready")
            exped = sem("softplus_exped")

            def __init__(self, use):
                self.use = use

            def act(self, act, u, e, relu):
                act.wait_ge(self.ready, self.use + 1)
                act.activation(e, u, ACT.Abs)
                act.activation(relu, u, ACT.Relu)
                act.drain()
                act.activation(e, e, ACT.Exp, scale=-1.0).then_inc(self.exped, 1)

            def dve_ratio(self, dve, e, s, s2):
                dve.wait_ge(self.exped, self.use + 1)
                dve.tensor_scalar(s, e, 2.0, None, ALU.add)
                dve.drain()
                dve.reciprocal(s2, s)
                dve.drain()
                dve.tensor_tensor(s, e, s2, ALU.mult)
                dve.drain()
                dve.tensor_tensor(s2, s, s, ALU.mult)
                dve.drain()

            def dve_series(self, dve, relu, s, s2, p):
                dve.tensor_scalar(p, s2, 1.0 / 15, None, ALU.mult)
                for c in (13, 11, 9, 7, 5, 3):
                    dve.drain()
                    dve.scalar_tensor_tensor(p, p, 1.0 / c, s2, ALU.add, ALU.mult)
                dve.drain()
                dve.scalar_tensor_tensor(p, p, 1.0, s, ALU.add, ALU.mult)
                dve.drain()
                dve.scalar_tensor_tensor(p, p, 2.0, relu, ALU.mult, ALU.add)

        ar = arena()
        x_tok = ar("x_tok", [P, NT, D])
        sq0 = ar("sq0", [P, 2, T])
        rstd0 = ar("rstd0", [P, T])
        rows1 = ar("rows1", [P, P])
        rows2 = ar("rows2", [P, P])
        xn = arena()("xn", [P, KT, T])
        root0 = Region(at_arena + big, arena_end)("root0", [P, T])
        h_tile = Region(at_arena + big, arena_end)("h_tile", [P, 2, T])
        xt = Region(at_ya, at_ya + big)("xt", [P, KT, T])
        w_ada = Region(at_ha, at_ya)("w_ada", [P, KT, 2 * D])
        w_ada_g = Region(at_ya + big, at_ya + 2 * big)("w_ada_g", [P, KT, D])
        shift_sum, scale_sum, gate_sum = w_ada[:, 0, 0:D], w_ada[:, 0, D:2 * D], w_ada_g[:, 0, :]

        pair_loaded = [sem(f"pair_loaded{i}") for i in range(4)]
        vec_loaded, col_loaded = sem("vec_loaded"), sem("col_loaded")
        consts = sem("consts")
        vec_turned, vec_ready = sem("vec_turned"), sem("vec_ready")
        xt_turned = sem("xt_turned")
        xt_act, xt_dve = sem("xt_act"), sem("xt_dve")
        silu_c_done, ada_mul = sem("silu_c_done"), sem("ada_mul")
        slice_scaled = sem("slice_scaled")
        pool_steps = sem("pool_steps")
        dve_steps = sem("dve_steps")
        XN_DVE = 5
        xt_saved = sem("xt_saved")
        norm0 = Norm(0)

        def vec_sources():
            v1 = [("b_ada", io["b_ada"]), ("norm_w", io["norm_w"]),
                  ("conv_w", io["conv_w"].rearrange("j c -> (j c)")), ("conv_b", io["conv_b"]),
                  ("ssm_norm_w", io["ssm_norm_w"]), ("b_gate", io["b_gate"]),
                  ("final_norm_w", io["final_norm_w"]), ("c", io["c"].rearrange("a d -> (a d)"))]
            v2 = [("norm_g_2", io["norm_g_2"].rearrange("a d -> (a d)")),
                  ("conv_w_2", io["conv_w_2"].rearrange("a j c -> (a j c)")),
                  ("b_alpha_2", io["b_alpha_2"].rearrange("a d -> (a d)")), ("final_g_2", io["final_g_2"]),
                  ("ml_norm_g_2", io["ml_norm_g_2"].rearrange("a d -> (a d)")),
                  ("gla_norm_g_2", io["gla_norm_g_2"].rearrange("a d -> (a d)"))]
            for rows, table, vs in ((rows1, VEC1, v1), (rows2, VEC2, v2)):
                for name, src in vs:
                    a, b = table[name]
                    yield rows[a:b, :], src.rearrange("(r p) -> r p", p=P)

        VECS = len(VEC1) + len(VEC2)

        def sp_0(sp):
            x = io["x"].rearrange("a (t p) d -> p (a t) d", p=P)
            for i in range(NT):
                sp.dma_start(x_tok[:, i, :], x[:, i, :]).then_inc(pair_loaded[i // 2], 16)
            sp.wait_ge(vec_loaded, 16 * VECS)
            wa = io["w_ada"].rearrange("(k p) c -> p k c", p=P)
            for k in range(KT):
                if k % 2 == 0:
                    sp.wait_ge(pair_loaded[k // 2], 32)
                sp.dma_start(w_ada[:, k, :], wa[:, k, 0:2 * D]).then_inc(pair_loaded[k // 2], 16)
            sp.dma_start(w_raw[:, 0, :, 0:32], cols(w_in, DT_OFF, 32)).then_inc(w_loaded[0], 16)
            sp.dma_start(w_raw[:, 0, :, 32:P], cols(w_in, F_OFF, P - 32)).then_inc(w_part, 16)
            load_w(sp, N_XBC, cols(w_in, XBC_OFF))
            for k in range(KT):
                if k % 2 == 0:
                    sp.wait_ge(pair_loaded[k // 2], 64)
                sp.dma_start(w_ada_g[:, k, :], wa[:, k, 2 * D:3 * D]).then_inc(pair_loaded[k // 2], 16)
            sp.wait_ge(xt_act, NT)
            sp.wait_ge(xt_dve, NT)
            sp.dma_start(xt_scr, xt[:, :, :]).then_inc(xt_saved, 16)

        def act_0(act):
            for dst, src in vec_sources():
                act.dma_start(dst, src).then_inc(vec_loaded, 16)
            act.wait_ge(consts, 1)
            act.dma_start(sp_bias[0:SSM_HEADS, :], io["dt_bias"].rearrange("(h a) -> h a", a=1)).then_inc(col_loaded, 16)
            act.dma_start(sp_bias[32:32 + FOX_HEADS, :], io["b_f"].rearrange("(h a) -> h a", a=1)).then_inc(col_loaded, 16)
            act.dma_start(neg_a[:, :], io["a_log"].rearrange("(h a) -> h a", a=1)).then_inc(col_loaded, 16)
            bg = io["b_gates_2"].rearrange("a (h b) -> (a h) b", b=1)
            act.dma_start(gate_bias2[0:ML_HEADS, :], bg[0:ML_HEADS, :]).then_inc(col_loaded, 16)
            act.dma_start(gate_bias2[32:32 + ML_HEADS, :], bg[ML_HEADS:2 * ML_HEADS, :]).then_inc(col_loaded, 16)
            act.dma_start(w_alpha[64:64 + GLA_RANK, :], io["w_alpha_2"].rearrange("a r k -> (a r) k")).then_inc(col_loaded, 16)
            for w in range(2):
                ds = io["d_skip"].rearrange("(t w) -> w t", w=2)[w, :]
                act.dma_start(dskip[64 * w:64 * w + 64, :], ds.partition_broadcast(64),
                              allow_slow_non_contiguous=True).then_inc(col_loaded, 16)
            def copy_xt(i):
                act.wait_ge(xt_turned, 2 * i + 1)
                act.activation(xt[:, 0:4, i * P:(i + 1) * P], acc[:, i % 2, 0:HALF], ACT.Copy).then_inc(xt_act, 1)

            for i in range(NT // 2):
                copy_xt(i)
            act.wait_ge(vec_turned, 1)
            act.activation(vec1[:, :], work[:, 0, 0:NVEC1], ACT.Copy)
            act.activation(vec2[:, :], work[:, 1, 0:NVEC2], ACT.Copy).then_inc(vec_ready, 1)
            act.drain()
            act.activation(silu_c[:, :], vec1[:, VEC1["c"][0]:VEC1["c"][1]], ACT.Silu).then_inc(silu_c_done, 1)
            for i in range(NT // 2, NT):
                copy_xt(i)
            act.drain()
            act.wait_ge(xt_dve, NT)

            def scale_slice(k, w, count):
                act.wait_ge(pair_loaded[k // 2], count)
                act.activation(w[:, k, 0:D], w[:, k, 0:D], ACT.Copy, scale=silu_c[:, k:k + 1]).then_inc(slice_scaled, 1)

            norm0.act(act, xt, sq0, root0, beside=lambda f: f >= 2 and scale_slice(f - 2, w_ada, 64))
            for k in range(KT - 2, KT):
                scale_slice(k, w_ada, 64)
            act.wait_ge(col_loaded, 16 * 8)
            act.activation(neg_a[:, :], neg_a[:, :], ACT.Exp)
            act.drain()
            act.activation(neg_a[:, :], neg_a[:, :], ACT.Copy, scale=-1.0)
            act.wait_ge(w_part, 16)
            split_hi(act, N_SMALL1)
            for k in range(KT // 2):
                scale_slice(k, w_ada_g, 96)
            act.wait_ge(dve_steps, 3)
            for f in range(KT):
                if f == XN_DVE:
                    act.wait_ge(pool_steps, 2)
                act.activation(ha_hi[:, f, :], xn[:, f, :], ACT.Identity, scale=a1[:, f:f + 1],
                               bias=ada[:, f:f + 1]).then_inc(x_hi_done, 1)
            split_hi(act, N_XBC)
            for k in range(KT // 2, KT):
                scale_slice(k, w_ada_g, 96)
            end_stage(act, 0)

        def pe_0(pe):
            pe.wait_ge(consts, 1)
            for i in range(NT):
                if i == NT // 2:
                    pe.wait_ge(vec_loaded, 16 * VECS)
                    pe.transpose(work[:, 0, 0:NVEC1], rows1[0:NVEC1, :], ident[0:NVEC1, 0:NVEC1])
                    pe.transpose(work[:, 1, 0:NVEC2], rows2[0:NVEC2, :], ident[0:NVEC2, 0:NVEC2]).then_inc(vec_turned, 1)
                if i % 2 == 0:
                    pe.wait_ge(pair_loaded[i // 2], 32)
                for g in range(2):
                    if i >= 2:
                        pe.wait_ge(xt_dve if g else xt_act, i - 1)
                    for f in range(4):
                        mm = pe.transpose(acc[:, i % 2, g * HALF + f * P:g * HALF + (f + 1) * P],
                                          x_tok[:, i, (4 * g + f) * P:(4 * g + f + 1) * P], ident[:, :])
                    mm.then_inc(xt_turned, 1)
            pe.wait_ge(vec_ready, 1)
            norm0.pe(pe, lambda f: sq0[:, f % 2, :])
            pe.wait_ge(dve_steps, 1)
            sum_columns(pe, scale_sum, KT)
            pe.wait_ge(pool_steps, 1)
            sum_columns(pe, shift_sum, 0).then_inc(ada_mul, 1)
            project(pe, N_SMALL1, ha_hi, ha_lo, after=LO_SPLITS[0])
            end_stage(pe, 0)

        def sum_columns(pe, x, m0):
            for m in range(KT):
                mm = pe.matmul(work[:, 2, m0 + m:m0 + m + 1], x[:, m * P:(m + 1) * P], ones[:, 0:1], start=True, stop=True)
            return mm

        def dve_0(dve):
            for i in range(NT):
                dve.wait_ge(xt_turned, 2 * i + 2)
                dve.tensor_copy(xt[:, 4:8, i * P:(i + 1) * P],
                                acc[:, i % 2, HALF:2 * HALF].rearrange("p (f t) -> p f t", f=4)).then_inc(xt_dve, 1)
            dve.wait_ge(silu_c_done, 1)
            for k in range(KT):
                if k % 2 == 0:
                    dve.wait_ge(pair_loaded[k // 2], 64)
                w, c = w_ada[:, k, D:2 * D], silu_c[:, k:k + 1]
                if k == 0:
                    dve.tensor_scalar(scale_sum, w, c, None, ALU.mult)
                else:
                    dve.drain()
                    e = dve.scalar_tensor_tensor(scale_sum, w, c, scale_sum, ALU.mult, ALU.add)
            e.then_inc(dve_steps, 1)
            norm0.dve(dve, root0, rstd0)
            dve.drain().then_inc(dve_steps, 1)
            dve.wait_ge(xt_act, NT)
            for f in range(XN_DVE):
                dve.tensor_tensor(xn[:, f, :], xt[:, f, :], rstd0[:, :], ALU.mult)
            split_lo(dve, N_SMALL1)
            dve.wait_ge(ada_mul, 1)
            dve.wait_ge(vec_ready, 1)
            dve.tensor_tensor(ada[:, 0:16], work[:, 2, 0:16], vec1[:, VEC1["b_ada"][0]:VEC1["b_ada"][0] + 16], ALU.add)
            dve.drain()
            dve.scalar_tensor_tensor(a1[:, :], ada[:, 8:16], 1.0, vec1[:, VEC1["norm_w"][0]:VEC1["norm_w"][1]],
                                     ALU.add, ALU.mult)
            dve.drain().then_inc(dve_steps, 1)
            for f in range(KT):
                if f == XN_DVE:
                    dve.wait_ge(pool_steps, 2)
                dve.tensor_scalar(h_tile[:, f % 2, :], xn[:, f, :], a1[:, f:f + 1], ada[:, f:f + 1], ALU.mult, ALU.add)
                dve.wait_ge(x_hi_done, SPLITS[0] + f + 1)
                dve.drain()
                dve.tensor_tensor(ha_lo[:, f, :], h_tile[:, f % 2, :], ha_hi[:, f, :].bitcast(F32),
                                  ALU.subtract).then_inc(x_lo_done, 1)
            split_lo(dve, N_XBC)
            end_stage(dve, 0)

        def pool_0(pool):
            pool.memset(sp_bias[:, :], 0.0)
            pool.memset(gate_bias2[:, :], 0.0)
            pool.memset(ident[:, :], 0.0)
            pool.memset(ones[:, :], 1.0)
            pool.memset(causal01[:, :], 1.0)
            pool.memset(zero_col[:, :], 0.0)
            pool.memset(eps_col[:, :], EPS)
            pool.memset(eps2_col[:, :], EPS * EPS)
            pool.memset(sp_sign[:, :], -1.0)
            pool.drain()
            pool.memset(sp_sign[0:32, :], 1.0)
            pool.affine_select(out=ident[:, :], in_=ident[:, :], compare_op=ALU.not_equal, fill=1.0,
                               base=0, pattern=[[-1, P]], channel_multiplier=1)
            pool.affine_select(out=causal01[:, :], in_=causal01[:, :], compare_op=ALU.is_ge, fill=0.0,
                               base=0, pattern=[[1, P]], channel_multiplier=-1)
            pool.drain().then_inc(consts, 1)
            sum_slices(pool, shift_sum, w_ada, 0)
            pool.drain().then_inc(pool_steps, 1)
            pool.wait_ge(xt_act, NT)
            pool.wait_ge(xt_dve, NT)
            pool.wait_ge(dve_steps, 2)
            for f in range(XN_DVE, KT):
                pool.tensor_tensor(xn[:, f, :], xt[:, f, :], rstd0[:, :], ALU.mult)
            pool.drain().then_inc(pool_steps, 1)
            sum_slices(pool, gate_sum, w_ada_g, KT)
            pool.drain().then_inc(pool_steps, 1)
            end_stage(pool, 0)

        def sum_slices(pool, total, w, before):
            for k in range(1, KT):
                pool.wait_ge(slice_scaled, before + k + 1)
                pool.drain()
                pool.tensor_tensor(total, total, w[:, k, 0:D], ALU.add)

        ar = arena()
        xbc = ar("xbc", [P, XBC_TILES, T])
        spt = ar("spt", [64, T])
        acs = ar("acs", [SSM_HEADS, T])
        ya = Region(at_ya + big + T * 4, at_ya + 2 * big)
        sp1 = {k: ya(f"sp1_{k}", [64, T]) for k in ("u", "e", "relu", "s", "s2", "p")}
        ya = Region(at_ya, at_ya + big)
        conv_in = ya("conv_in", [P, 2, T + 8])
        conv_out = ya("conv_out", [P, 2, T])
        fcum = ya("fcum", [64, T])
        softplus1 = Softplus(0)
        pad_zeroed = sem("pad_zeroed")
        conved, conv_silued = sem("conved"), sem("conv_silued")
        sums_ready, sums_saved = sem("sums_ready"), sem("sums_saved")
        series = ya("series", [64, KT])

        def sp_1(sp):
            with sp.Fori(0, XBC_TILES // 2 - 1) as j:
                load_w(sp, N_XBC + 1, cols(w_in, XBC_OFF + P + 2 * P * j), adv=j)
                load_w(sp, N_XBC + 2, cols(w_in, XBC_OFF + 2 * P + 2 * P * j), adv=j)
            load_w(sp, N_Z - 1, cols(w_in, XBC_OFF + (XBC_TILES - 1) * P))

        def act_1(act):
            begin_stage(act, 1)
            act.drain().then_inc(conv_silued, 2)
            softplus1.act(act, sp1["u"][:, :], sp1["e"][:, :], sp1["relu"][:, :])
            act.wait_ge(pad_zeroed, 1)
            with act.Fori(0, XBC_TILES // 2) as j:
                for b in range(2):
                    n = N_XBC + b
                    split_hi(act, n + 1, adv=j)
                    projected(act, n, adv=j)
                    act.wait_ge(conved, 2 * j + b + 1)
                    act.activation(conv_in[:, b, 3:3 + T], acc[:, n % 2, :], ACT.Copy).then_inc(acc_free[n % 2], 1)
                    act.wait_ge(conved, 2 * j + b + 3)
                    act.activation(row(xbc, 2 * j + b), conv_out[:, b, :], ACT.Silu,
                                   bias=dcol(vec1, VEC1, "conv_b", 2 * j + b)).then_inc(conv_silued, 1)
            end_stage(act, 1)

        def pe_1(pe):
            begin_stage(pe, 1)
            with pe.Fori(0, XBC_TILES // 2) as j:
                for b in range(2):
                    project(pe, N_XBC + b, ha_hi, ha_lo, adv=j)
            pe.wait_ge(pool_steps, 3)
            sum_columns(pe, gate_sum, 2 * KT).then_inc(ada_mul, 1)
            end_stage(pe, 1)

        def conv_taps(dve, dst, src, tap):
            dve.tensor_scalar(dst, src(0), tap(0), None, ALU.mult)
            for j in range(1, CONV_K):
                dve.drain()
                last = dve.scalar_tensor_tensor(dst, src(j), tap(j), dst, ALU.mult, ALU.add)
            return last

        def dve_1(dve):
            begin_stage(dve, 1)
            dve.drain().then_inc(conved, 2)
            projected(dve, N_SMALL1)
            dve.wait_ge(col_loaded, 16 * 8)
            dve.tensor_scalar(sp1["u"][:, :], acc[0:64, 0, :], sp_bias[:, :], sp_sign[:, :], ALU.add,
                              ALU.mult).then_inc(acc_free[0], 1)
            dve.drain().then_inc(softplus1.ready, 1)
            softplus1.dve_ratio(dve, *(sp1[k][:, :] for k in ("e", "s", "s2")))
            dve.drain().then_inc(dve_steps, 1)

            def tiles(j):
                for b in range(2):
                    n = N_XBC + b
                    split_lo(dve, n + 1, adv=j)
                    dve.wait_ge(acc_free[n % 2], n // 2 + 1 + j)
                    dve.wait_ge(conv_silued, 2 * j + b + 1)
                    conv_taps(dve, conv_out[:, b, :], lambda k: conv_in[:, b, k:k + T],
                              lambda k: vec1[:, VEC1["conv_w"][0] + k * XBC_TILES:][:, bass.ds(2 * j + b, 1)]
                              ).then_inc(conved, 1)

            with dve.Fori(0, 3) as j:
                tiles(j)
            dve.wait_ge(pool_steps, 4)
            a = sp1["u"][0:SSM_HEADS, :]
            dve.tensor_scalar(a, spt[0:SSM_HEADS, :], neg_a[:, :], None, ALU.mult)
            dve.drain()
            for c in range(NCHUNK):
                t = slice(c * CHUNK, (c + 1) * CHUNK)
                dve.tensor_tensor_scan(acs[:, t], a[:, t], zero_col[0:SSM_HEADS, :].to_broadcast([SSM_HEADS, CHUNK]),
                                       0.0, ALU.add, ALU.add)
            f = slice(32, 32 + FOX_HEADS)
            dve.tensor_tensor_scan(fcum[f, :], spt[f, :], zero_col[f, :].to_broadcast([FOX_HEADS, T]),
                                   0.0, ALU.add, ALU.add)
            dve.drain().then_inc(sums_ready, 1)
            with dve.Fori(3, XBC_TILES // 2) as j:
                tiles(j)
            dve.wait_ge(ada_mul, 2)
            dve.tensor_tensor(ada[:, 16:24], work[:, 2, 16:24], vec1[:, VEC1["b_ada"][0] + 16:VEC1["b_ada"][1]], ALU.add)
            end_stage(dve, 1)

        def pool_1(pool):
            begin_stage(pool, 1)
            pool.wait_ge(xt_saved, 16)
            pool.memset(conv_in[:, :, 0:3], 0.0).then_inc(pad_zeroed, 1)
            for i in range(KT):
                pool.memset(series[:, i:i + 1], 1.0 / (2 * i + 1))
            pool.drain()
            pool.wait_ge(dve_steps, 4)
            relu, s, s2, p = (sp1[k][:, :] for k in ("relu", "s", "s2", "p"))
            term = [series[:, i:i + 1].to_broadcast([64, T]) for i in range(KT)]
            pool.tensor_tensor(p, s2, term[KT - 1], ALU.mult)
            for i in range(KT - 2, -1, -1):
                pool.drain()
                pool.tensor_tensor(p, p, term[i], ALU.add)
                pool.drain()
                pool.tensor_tensor(p, p, s2 if i else s, ALU.mult)
            pool.drain()
            pool.tensor_tensor(p, p, p, ALU.add)
            pool.drain()
            pool.tensor_tensor(spt[:, :], p, relu, ALU.add)
            pool.drain().then_inc(pool_steps, 1)
            pool.wait_ge(sums_ready, 1)
            pool.dma_start(acs_scr, acs[:, :]).then_inc(sums_saved, 16)
            pool.dma_start(fcum_scr, fcum[32:32 + FOX_HEADS, :]).then_inc(sums_saved, 16)
            pool.wait_ge(sums_saved, 32)
            end_stage(pool, 1)


        ya = ya_region()
        x_st = ya("x_st", [P, 8, CHUNK])
        bc_st = ya("bc_st", [P, 2, CHUNK])
        dtacs_st = ya("dtacs_st", [SSM_HEADS, 2, CHUNK])
        acs_bc = ya("acs_bc", [P, SSM_HEADS, CHUNK])
        acs_n = ya("acs_n", [P, HPG, CHUNK])
        decay = ya("decay", [P, SSM_HEADS, CHUNK])
        tok16 = ya("tok16", [P, 2, SSM_HEADS])
        b_tok = ya("b_tok", [P, P])
        e_acs = ya("e_acs", [P, HPG, CHUNK])
        c_dec = ya("c_dec", [P, HPG, CHUNK])
        xdt = ya("xdt", [P, SSM_HEADS, SSM_P])
        xdec = ya("xdec", [P, SSM_HEADS, SSM_P])
        state = ya("state", [P, HPG, SSM_P])
        xskip = ya("xskip", [P, 8, CHUNK])
        to_end = ya("to_end", [P, 2, SSM_HEADS])
        staged, bc_loaded = sem("staged"), [sem("bc_loaded0"), sem("bc_loaded1")]
        turned2, tok_ready, b_ready = sem("turned2"), sem("tok_ready"), sem("b_ready")
        cb_done, seg_done, masked2, decay_done = sem("cb_done"), sem("seg_done"), sem("masked2"), sem("decay_done")
        end_arg, end_exp, e_acs_done = sem("end_arg"), sem("end_exp"), sem("e_acs_done")
        cdec_done, xdec_done, m_done = sem("cdec_done"), sem("xdec_done"), sem("m_done")
        xskip_done, y_done, kv_done = sem("xskip_done"), sem("y_done"), sem("kv_done")
        chunk_done = sem("chunk_done")
        b_own = ya("b_own", [P, SSM_G, CHUNK])
        stash = ya("stash", [P, 2, T])
        stash_ready, stash_saved = [sem("z_ready"), sem("g_ready")], [sem("z_saved"), sem("g_saved")]
        ypsum = acc[:, 1, :]
        cbpsum = work[:, 2, 256:256 + SSM_G * CHUNK]
        kvpsum = work[:, 3, :]

        def chunk_of(x, c):
            return x[:, :, bass.ds(c * CHUNK, CHUNK)]

        def sp_2(sp):
            load_w(sp, N_Z, cols(w_in, Z_OFF))
            load_w(sp, N_Z + 1, cols(w_in, G_OFF))

            def save(i, c, scr):
                wait_here(sp, stash_ready[i], c + 1)
                sp.dma_start(row(scr, c), stash[:, i, :]).then_inc(stash_saved[i], 16)

            with sp.Fori(0, NCHUNK - 1) as c:
                load_w(sp, N_Z + 2, cols(w_in, Z_OFF + P + P * c), adv=c)
                save(0, c, z_scr)
                load_w(sp, N_Z + 3, cols(w_in, G_OFF + P + P * c), adv=c)
                save(1, c, g_scr)
            for i, scr in ((0, z_scr), (1, g_scr)):
                load_w(sp, N_GATT + i, cols(w_in, G_OFF + D + i * P))
                sp.wait_ge(stash_ready[i], NCHUNK)
                sp.dma_start(scr[:, NCHUNK - 1, :], stash[:, i, :]).then_inc(stash_saved[i], 16)

        def pool_2(pool):
            begin_stage(pool, 2)
            masked_fill = pool.to_reg(MASKED)
            pool.memset(b_own[:, :, :], 0.0)
            pool.drain()

            def stage(c):
                pool.tensor_copy(bc_st[:, :, :], chunk_of(xbc[:, 8:10, :], c))
                for g in range(SSM_G):
                    gp = slice(g * 64, g * 64 + 64)
                    pool.drain()
                    pool.tensor_copy(b_own[gp, g, :], xbc[gp, 8, bass.ds(c * CHUNK, CHUNK)])
                pool.drain()
                pool.tensor_copy(dtacs_st[:, 0, :], spt[0:SSM_HEADS, bass.ds(c * CHUNK, CHUNK)])
                pool.tensor_copy(dtacs_st[:, 1, :], acs[:, bass.ds(c * CHUNK, CHUNK)])
                pool.drain().then_inc(staged, 1)

            def chunk(c, ahead=True):
                pool.wait_ge(chunk_done, c + 1)
                pool.dma_start(acs_bc[:, :, :], acs_scr[:, bass.ds(c * CHUNK, CHUNK)].partition_broadcast(P)
                               ).then_inc(bc_loaded[0], 16)
                for g in range(SSM_G):
                    pool.dma_start(acs_n[g * 64:g * 64 + 64, :, :],
                                   acs_scr[g * HPG:(g + 1) * HPG, bass.ds(c * CHUNK, CHUNK)].partition_broadcast(64)
                                   ).then_inc(bc_loaded[1], 16)
                pool.tensor_tensor(xskip[:, :, :], x_st[:, :, :],
                                   dskip[:, :].unsqueeze(2).to_broadcast([P, 8, CHUNK]), ALU.mult).then_inc(xskip_done, 1)
                if ahead:
                    pool.drain()
                    wait_here(pool, turned2, c + 1)
                    pool.tensor_copy(x_st[:, :, :], chunk_of(xbc[:, 0:8, :], c + 1))
                wait_here(pool, seg_done, c + 1)
                pool.affine_select(out=decay[:, :, :], in_=decay[:, :, :], compare_op=ALU.is_ge, fill=masked_fill,
                                   base=0, pattern=[[0, SSM_HEADS], [1, CHUNK]], channel_multiplier=-1
                                   ).then_inc(masked2, 1)
                if ahead:
                    wait_here(pool, cb_done, c + 1)
                    wait_here(pool, cdec_done, c + 1)
                    stage(c + 1)

            pool.tensor_copy(x_st[:, :, :], chunk_of(xbc[:, 0:8, :], 0))
            stage(0)
            with pool.Fori(0, NCHUNK - 1) as c:
                chunk(c)
            chunk(NCHUNK - 1, ahead=False)
            end_stage(pool, 2)

        def pe_2(pe):
            begin_stage(pe, 2)
            with pe.Fori(0, NCHUNK) as c:
                for part in range(4):
                    project_part(pe, N_Z, part, 2 * c, adv=c)
                pe.wait_ge(staged, c + 1)
                for i in range(8):
                    pe.transpose(work[:, i // 4, (i % 4) * P:(i % 4 + 1) * P], x_st[:, i, :], ident[:, :])
                pe.transpose(work[:, 2, 0:P], bc_st[:, 0, :], ident[:, :])
                for i in range(2):
                    mm = pe.transpose(work[:, 2, P + i * 16:P + i * 16 + 16], dtacs_st[:, i, :], ident[0:16, 0:16])
                mm.then_inc(turned2, 1)
                for part in range(2):
                    project_part(pe, N_Z + 1, part, 2 * c + 1, adv=c)
                pe.wait_ge(b_ready, c + 1)
                for g in range(SSM_G):
                    mm = pe.matmul(cbpsum[:, g * CHUNK:(g + 1) * CHUNK], b_own[:, g, :], bc_st[:, 1, :], start=True, stop=True)
                mm.then_inc(cb_done, 1)
                for part in range(2, 4):
                    project_part(pe, N_Z + 1, part, 2 * c + 1, adv=c)
                pe.wait_ge(xdec_done, c + 1)
                for g in range(SSM_G):
                    mm = pe.matmul(kvpsum[g * 64:g * 64 + 64, :], b_tok[:, g * 64:g * 64 + 64],
                                   xdec[:, g * HPG:(g + 1) * HPG, :], start=True, stop=True)
                mm.then_inc(kv_done, 1)
                pe.wait_ge(m_done, c + 1)
                pe.wait_ge(cdec_done, c + 1)
                for h in range(SSM_HEADS):
                    g, r = divmod(h, HPG)
                    y = ypsum[(h % 2) * 64:(h % 2) * 64 + 64, (h // 2) * CHUNK:(h // 2 + 1) * CHUNK]
                    pe.matmul(y, xdt[:, h, :], decay[:, h, :], start=True, stop=False)
                    mm = pe.matmul(y, state[g * 64:g * 64 + 64, r, :], c_dec[g * 64:g * 64 + 64, r, :],
                                   start=False, stop=True)
                mm.then_inc(y_done, 1)
            end_stage(pe, 2)

        def act_2(act):
            begin_stage(act, 2)
            act.drain().then_inc(fill_free, 2)
            for i in range(2):
                act.drain().then_inc(stash_saved[i], 16)
            with act.Fori(0, NCHUNK) as c:

                def read_tile(i):
                    act.wait_ge(stash_saved[i], 16 * c + 16)
                    for half in range(2):
                        read_half(act, N_Z + i, half, 2 * c + i, stash[:, i, :], adv=c)
                    act.drain().then_inc(stash_ready[i], 1)

                split_hi(act, N_Z + 1, adv=c)
                read_tile(0)
                split_hi(act, N_Z + 2, adv=c)
                act.wait_ge(turned2, c + 1)
                act.activation(tok16[:, :, :], work[:, 2, P:P + 32], ACT.Copy).then_inc(tok_ready, 1)
                act.activation(b_tok[:, :], work[:, 2, 0:P], ACT.Copy).then_inc(b_ready, 1)
                act.wait_ge(bc_loaded[1], 32 * c + 32)
                act.activation(e_acs[:, :, :], acs_n[:, :, :], ACT.Exp).then_inc(e_acs_done, 1)
                act.wait_ge(end_arg, c + 1)
                act.activation(to_end[:, 1, :], to_end[:, 0, :], ACT.Exp).then_inc(end_exp, 1)
                act.wait_ge(masked2, c + 1)
                act.activation(decay[:, :, :], decay[:, :, :], ACT.Exp).then_inc(decay_done, 1)
                read_tile(1)
            for a in range(2):
                act.drain().then_inc(acc_free[a], NCHUNK)
            end_stage(act, 2)

        def dve_2(dve):
            begin_stage(dve, 2)
            dve.memset(state[:, :, :], 0.0)
            dve.drain().then_inc(chunk_done, 1)
            with dve.Fori(0, NCHUNK) as c:
                split_lo(dve, N_Z + 1, adv=c)
                dve.wait_ge(tok_ready, c + 1)
                dve.wait_ge(bc_loaded[0], 16 * c + 16)
                dve.tensor_tensor(decay[:, :, :], acs_bc[:, :, :],
                                  tok16[:, 1, :].unsqueeze(2).to_broadcast([P, SSM_HEADS, CHUNK]),
                                  ALU.subtract).then_inc(seg_done, 1)
                dve.tensor_tensor(to_end[:, 0, :], acs_bc[:, :, CHUNK - 1], tok16[:, 1, :],
                                  ALU.subtract).then_inc(end_arg, 1)
                dve.tensor_tensor(xdt[:, :, :], work[:, 0:2, :].rearrange("p b (h d) -> p (b h) d", d=SSM_P),
                                  tok16[:, 0, :].unsqueeze(2).to_broadcast([P, SSM_HEADS, SSM_P]), ALU.mult)
                dve.drain()
                dve.wait_ge(end_exp, c + 1)
                dve.tensor_tensor(xdec[:, :, :], xdt[:, :, :],
                                  to_end[:, 1, :].unsqueeze(2).to_broadcast([P, SSM_HEADS, SSM_P]),
                                  ALU.mult).then_inc(xdec_done, 1)
                dve.wait_ge(e_acs_done, c + 1)
                dve.tensor_tensor(c_dec[:, :, :], e_acs[:, :, :],
                                  bc_st[:, 1, :].unsqueeze(1).to_broadcast([P, HPG, CHUNK]), ALU.mult).then_inc(cdec_done, 1)
                dve.wait_ge(decay_done, c + 1)
                dve.wait_ge(cb_done, c + 1)
                for g in range(SSM_G):
                    m = dve.tensor_tensor(decay[:, g * HPG:(g + 1) * HPG, :], decay[:, g * HPG:(g + 1) * HPG, :],
                                          cbpsum[:, g * CHUNK:(g + 1) * CHUNK].unsqueeze(1).to_broadcast([P, HPG, CHUNK]),
                                          ALU.mult)
                m.then_inc(m_done, 1)
                split_lo(dve, N_Z + 2, adv=c)
                dve.wait_ge(xskip_done, c + 1)
                dve.wait_ge(y_done, c + 1)
                dve.tensor_tensor(chunk_of(xbc[:, 0:8, :], c), ypsum.rearrange("p (i l) -> p i l", l=CHUNK),
                                  xskip[:, :, :], ALU.add)
                dve.wait_ge(kv_done, c + 1)
                dve.tensor_tensor(state[:, :, :], state[:, :, :],
                                  e_acs[:, :, CHUNK - 1].unsqueeze(2).to_broadcast([P, HPG, SSM_P]), ALU.mult)
                dve.drain()
                dve.tensor_tensor(state[:, :, :], state[:, :, :], kvpsum.rearrange("p (r d) -> p r d", d=SSM_P), ALU.add)
                dve.drain().then_inc(chunk_done, 1)
            end_stage(dve, 2)

        silu_z = Region(at_arena + XBC_TILES * T * 4, arena_end)("silu_z", [P, 2, T])
        yw = Region(at_arena + 8 * T * 4, arena_end)("yw", [P, 2, T])
        z_loaded, z_silued = [sem("z_loaded0"), sem("z_loaded1")], sem("z_silued")
        yz_done = sem("yz_done")

        ga_half = Region(at_arena + XBC_TILES * T * 4 + 2 * T * 4, arena_end)("ga_half", [P, HALF])
        ga_ready, ga_saved = sem("ga_ready"), sem("ga_saved")

        def sp_3(sp):
            for m in range(KT // 2):
                if m < 2:
                    load_w(sp, N_GATT + 2 + m, cols(w_in, G_OFF + D + (2 + m) * P))
                elif m == 2:
                    for i in range(2):
                        load_w(sp, N_MIX1 + i, cols(io["w_proj_ssm"], i * P))
                for half in range(2):
                    sp.wait_ge(ga_ready, 2 * m + half + 1)
                    sp.dma_start(ga_scr[:, m, half * HALF:(half + 1) * HALF], ga_half[:, :]).then_inc(ga_saved, 16)

        def pool_3(pool):
            begin_stage(pool, 3)
            for i in range(2):
                pool.wait_ge(stash_saved[i], 16 * (NCHUNK + 1))
            with pool.Fori(0, 4) as j:
                for b in range(2):
                    wait_here(pool, yz_done, 2 * j + b + 1)
                    pool.dma_start(silu_z[:, b, :], row(z_scr, 2 * j + b)).then_inc(z_loaded[b], 16)
            end_stage(pool, 3)

        def pe_3(pe):
            begin_stage(pe, 3)
            with pe.Fori(0, 2) as j:
                for b in range(2):
                    project(pe, N_GATT + b, ha_hi, ha_lo, adv=j)
            project(pe, N_MIX1, ya_hi, ya_lo, after=LO_SPLITS[3])
            end_stage(pe, 3)

        def act_3(act):
            begin_stage(act, 3)
            act.drain().then_inc(ga_saved, 16)
            with act.Fori(0, 2) as j:

                def silu(b):
                    act.wait_ge(z_loaded[b % 2], 32 * j + 16 * (b // 2) + 16)
                    act.activation(silu_z[:, b % 2, :], silu_z[:, b % 2, :], ACT.Silu).then_inc(z_silued, 1)

                def tile(b):
                    act.wait_ge(yz_done, 4 * j + b + 3)
                    act.activation(row(xbc, 4 * j + b), row(xbc, 4 * j + b), ACT.Square).then_inc(Norm.squared, 1)
                    act.activation(row(ya_hi, 4 * j + b), yw[:, b % 2, :], ACT.Copy).then_inc(x_hi_done, 1)

                def gate(i, half):
                    n = N_GATT + i
                    projected(act, n, adv=j)
                    act.wait_ge(ga_saved, 64 * j + 32 * i + 16 * half + 16)
                    e = act.activation(ga_half[:, :], acc[:, n % 2, half * HALF:(half + 1) * HALF], ACT.Copy)
                    if half:
                        e.then_inc(acc_free[n % 2], 1)
                    act.drain().then_inc(ga_ready, 1)

                split_hi(act, N_GATT + 1, adv=j)
                silu(0)
                silu(1)
                tile(0)
                silu(2)
                tile(1)
                gate(0, 0)
                split_hi(act, N_GATT + 2, adv=j)
                silu(3)
                tile(2)
                gate(0, 1)
                tile(3)
                gate(1, 0)
                gate(1, 1)
            split_hi(act, N_MIX1 + 1)
            end_stage(act, 3)

        def dve_3(dve):
            begin_stage(dve, 3)
            dve.drain().then_inc(yz_done, 2)
            with dve.Fori(0, 2) as j:
                for b in range(4):
                    f = 4 * j + b
                    if b % 2 == 0:
                        split_lo(dve, N_GATT + b // 2 + 1, adv=j)
                    dve.wait_ge(z_silued, f + 1)
                    dve.scalar_tensor_tensor(yw[:, b % 2, :], row(xbc, f), dcol(vec1, VEC1, "ssm_norm_w", f),
                                             silu_z[:, b % 2, :], ALU.mult, ALU.mult)
                    dve.tensor_tensor(row(xbc, f), row(xbc, f), silu_z[:, b % 2, :], ALU.mult)
                    dve.drain().then_inc(yz_done, 1)
                    dve.wait_ge(x_hi_done, SPLITS[3] + f + 1)
                    dve.tensor_tensor(row(ya_lo, f), yw[:, b % 2, :], row(ya_hi, f).bitcast(F32), ALU.subtract
                                      ).then_inc(x_lo_done, 1)
                    if b % 2:
                        dve.wait_ge(Norm.squared, KT + f + 1)
                        dve.tensor_tensor(row(xbc, f - 1), row(xbc, f - 1), row(xbc, f), ALU.add)
            split_lo(dve, N_MIX1 + 1)
            end_stage(dve, 3)

        ar = Region(at_arena + 8 * T * 4, arena_end)
        root4 = ar("root4", [P, T])
        rstd4 = ar("rstd4", [P, T])
        ar = arena()
        gate4 = ar("gate4", [P, 2, T])
        mix4 = ar("mix4", [P, 2, T])
        norm4 = Norm(1)
        g_loaded4, g_sigmoid = [sem("g_loaded4_0"), sem("g_loaded4_1")], sem("g_sigmoid")
        mix4_done, mix4_saved, mix4_free = sem("mix4_done"), sem("mix4_saved"), sem("mix4_free")

        def sp_4(sp):
            with sp.Fori(0, 3) as j:
                for b in range(2):
                    load_w(sp, N_MIX1 + 2 + b, cols(io["w_proj_ssm"], (2 + b) * P + 2 * P * j), adv=j)

        def pe_4(pe):
            begin_stage(pe, 4)
            for f in range(0, KT, 2):
                for h in range(2):
                    mm = pe.matmul(work[:, h, :], ones[:, :], xbc[:, f, h * HALF:(h + 1) * HALF],
                                   start=(f == 0), stop=(f == KT - 2))
                mm.then_inc(norm4.summed, 2)
            with pe.Fori(0, 3) as j:
                for b in range(2):
                    project(pe, N_MIX1 + 1 + b, ya_hi, ya_lo, adv=j)
            project(pe, N_FOX - 1, ya_hi, ya_lo)
            end_stage(pe, 4)

        def act_4(act):
            begin_stage(act, 4)
            norm4.act_root(act, root4)

            def sigmoid(j, b):
                act.wait_ge(g_loaded4[b], 16 * j + 16)
                act.activation(gate4[:, b, :], gate4[:, b, :], ACT.Sigmoid,
                               bias=dcol(vec1, VEC1, "b_gate", 2 * j + b)).then_inc(g_sigmoid, 1)

            with act.Fori(0, 3) as j:
                for b in range(2):
                    sigmoid(j, b)
                    split_hi(act, N_MIX1 + b + 2, adv=j)
            sigmoid(3, 0)
            split_hi(act, N_FOX)
            sigmoid(3, 1)
            end_stage(act, 4)

        def dve_4(dve):
            begin_stage(dve, 4)
            dve.drain().then_inc(mix4_done, 2)
            dve.drain().then_inc(mix4_free, 2)
            norm4.dve(dve, root4, rstd4)
            dve.drain()

            def mix(j, b):
                n = N_MIX1 + b
                dve.wait_ge(g_sigmoid, 2 * j + b + 1)
                dve.tensor_tensor(gate4[:, b, :], gate4[:, b, :], rstd4[:, :], ALU.mult)
                dve.drain()
                projected(dve, n, adv=j)
                dve.wait_ge(mix4_free, 2 * j + b + 1)
                dve.tensor_tensor(mix4[:, b, :], acc[:, n % 2, :], gate4[:, b, :], ALU.mult).then_inc(acc_free[n % 2], 1)
                dve.drain().then_inc(mix4_done, 1)

            with dve.Fori(0, 3) as j:
                for b in range(2):
                    mix(j, b)
                    split_lo(dve, N_MIX1 + b + 2, adv=j)
            mix(3, 0)
            split_lo(dve, N_FOX)
            mix(3, 1)
            end_stage(dve, 4)

        def pool_4(pool):
            begin_stage(pool, 4)
            pool.wait_ge(norm4.summed, norm4.tiles + KT)
            pool.wait_ge(ga_saved, 16 * (KT + 1))
            with pool.Fori(0, 4) as j:
                for b in range(2):
                    wait_here(pool, mix4_done, 2 * j + b + 1)
                    pool.dma_start(gate4[:, b, :], row(g_scr, 2 * j + b)).then_inc(g_loaded4[b], 16)
                for b in range(2):
                    wait_here(pool, mix4_done, 2 * j + b + 3)
                    pool.dma_start(row(merged_scr, 2 * j + b), mix4[:, b, :]).then_inc(mix4_saved, 16)
                    wait_here(pool, mix4_saved, 32 * j + 16 * b + 16)
                    pool.drain().then_inc(mix4_free, 1)
            end_stage(pool, 4)

        ar = arena()
        q_t = ar("q_t", [P, T])
        k_t = ar("k_t", [P, T])
        v_tok = ar("v_tok", [P, NT, FOX_D])
        silu_za = ar("silu_za", [P, T])
        f_bc = ar("f_bc", [P, T])
        prob = ar("prob", [P, 2, T])
        prob_t = ar("prob_t", [P, 2, NT, P])
        y_head = ar("y_head", [P, T])
        neg_max = ar("neg_max", [P, 2])
        row_sum = ar("row_sum", [P, 2])
        row_inv = ar("row_inv", [P, 2])
        last = (FOX_HEADS - 1) * T * 4
        next_tiles = [Region(at_ya + last, at_ya + big)("next_q", [P, T]), Region(at_ya + big + last, at_ya + 2 * big)("next_k", [P, T]),
                      ar("next_v", [P, T]), ar("next_z", [P, T])]
        nxt_ready = sem("nxt_ready")
        taken = sem("taken")
        fbc_loaded, fbc_used = sem("fbc_loaded"), sem("fbc_used")
        v_turned, v_ready = sem("v_turned"), sem("v_ready")
        qk_done, logits_done, diag_done, max_done = sem("qk_done"), sem("logits_done"), sem("diag_done"), sem("max_done")
        exp_done, prob_done, p_turned, p_copied = sem("exp_done"), sem("prob_done"), sem("p_turned"), sem("p_copied")
        pv_done, y_gated, za_ready = sem("pv_done"), sem("y_gated"), sem("za_ready")
        N_LATE = N_FOX + 4 * FOX_HEADS
        late_saved = stash_saved
        LATE_SAVED = 16 * (NCHUNK + 1) + 32
        FOX_SCALE = float(FOX_D) ** -0.5
        FILLS2 = 2 * NCHUNK
        BANK_TILES = HALF // P

        def fox_chunks(t):
            first = sum((v + BANK_TILES) // BANK_TILES for v in range(t))
            return [(first + i, a, min(a + BANK_TILES, t + 1)) for i, a in enumerate(range(0, t + 1, BANK_TILES))]

        def fox_fills(t):
            return range(3) if t == 0 else range(2 * t + 2, 2 * t + 4) if t < 5 else [t + 7]

        FC = fox_chunks(NT)[0][0]

        def sp_5(sp):
            with sp.Fori(0, FOX_HEADS) as h:
                for i, off in enumerate((Q_OFF, K_OFF, V_OFF, ZA_OFF)):
                    load_w(sp, N_FOX + i, cols(w_in, off + P * h), adv=2 * h)
            for i in range(2):
                load_w(sp, N_LATE + i, cols(w_in, G_OFF + D + (KT // 2 + i) * P))
            for i in range(4):
                if i < 2:
                    load_w(sp, N_LATE + 2 + i, cols(w_in, G_OFF + D + (KT // 2 + 2 + i) * P))
                else:
                    load_w(sp, N_MIX2 + i - 2, cols(io["w_proj_att"], (i - 2) * P))
                sp.wait_ge(nxt_ready, 4 * FOX_HEADS + i + 1)
                sp.dma_start(ga_scr[:, KT // 2 + i, :], next_tiles[i][:, :]).then_inc(late_saved[i // 2], 16)

        def pool_5(pool):
            begin_stage(pool, 5)
            pool.drain().then_inc(fbc_used, 1)
            masked_fill = pool.to_reg(MASKED)
            with pool.Fori(0, FOX_HEADS) as h:
                wait_here(pool, nxt_ready, 4 * h + 2)
                pool.tensor_copy(q_t[:, :], next_tiles[0][:, :])
                pool.tensor_copy(k_t[:, :], next_tiles[1][:, :])
                pool.drain().then_inc(taken, 1)
                wait_here(pool, fbc_used, h + 1)
                pool.dma_start(f_bc[:, :], fcum_scr[bass.ds(h, 1), :].rearrange("a t -> (a t)").partition_broadcast(P)
                               ).then_inc(fbc_loaded, 16)
                for t in range(NT):
                    wait_here(pool, logits_done, FC * h + fox_chunks(t)[-1][0] + 1)
                    pool.affine_select(out=prob[:, t % 2, t * P:(t + 1) * P], in_=prob[:, t % 2, t * P:(t + 1) * P],
                                       compare_op=ALU.is_ge, fill=masked_fill, base=0, pattern=[[-1, P]],
                                       channel_multiplier=1).then_inc(diag_done, 1)
            end_stage(pool, 5)

        def pe_5(pe):
            for i in range(4):
                project(pe, N_FOX + i, ha_hi, ha_lo)
            begin_stage(pe, 5)
            for a in range(2):
                pe.wait_ge(acc_free[(N_FOX + 2 + a) % 2], (N_FOX + 2 + a) // 2 + 1)

            def head(h):
                def fill(part):
                    project_part(pe, N_FOX + 4 + part // 4, part % 4, FILLS2 + 4 * h + part // 4, adv=2 * h)

                def scores(t):
                    for c, a, b in fox_chunks(t):
                        if c >= 2:
                            pe.wait_ge(logits_done, FC * h + c - 1)
                        pe.matmul(work[:, c % 2, 0:(b - a) * P], q_t[:, t * P:(t + 1) * P], k_t[:, a * P:b * P],
                                  start=True, stop=True).then_inc(qk_done, 1)

                def turn_probs(t):
                    pe.wait_ge(prob_done, NT * h + t + 1)
                    for c, a, b in fox_chunks(t):
                        if c >= 2:
                            pe.wait_ge(p_copied, FC * h + c - 1)
                        for k in range(a, b):
                            mm = pe.transpose(work[:, 2 + c % 2, (k - a) * P:(k - a + 1) * P], prob[:, t % 2, k * P:(k + 1) * P],
                                              ident[:, :])
                        mm.then_inc(p_turned, 1)

                def weigh_values(t):
                    for c, a, b in fox_chunks(t):
                        pe.wait_ge(p_copied, FC * h + c + 1)
                        for k in range(a, b):
                            mm = pe.matmul(acc[:, 1, t * P:(t + 1) * P], v_tok[:, k, :], prob_t[:, t % 2, k, :],
                                           start=(k == 0), stop=(k == t))
                    mm.then_inc(pv_done, 1)

                pe.wait_ge(nxt_ready, 4 * h + 3)
                for b in range(NT):
                    mm = pe.transpose(work[:, 2 + b // 4, (b % 4) * P:(b % 4 + 1) * P], next_tiles[2][:, b * P:(b + 1) * P], ident[:, :])
                mm.then_inc(v_turned, 1)
                pe.wait_ge(taken, h + 1)
                scores(0)
                scores(1)
                for t in range(NT):
                    for part in fox_fills(t):
                        fill(part)
                    if t == 0:
                        pe.wait_ge(v_ready, h + 1)
                        pe.wait_ge(y_gated, 2 * h + 2)
                    turn_probs(t)
                    if t + 2 < NT:
                        scores(t + 2)
                    if t == 0:
                        fill(3)
                    weigh_values(t)
                fill(2 * NT - 1)

            with pe.Fori(0, FOX_HEADS) as h:
                head(h)
            end_stage(pe, 5)

        def act_5(act):
            begin_stage(act, 5)
            for i in range(4):
                n = N_FOX + i
                split_hi(act, n + 1)
                projected(act, n)
                act.activation(next_tiles[i][:, :], acc[:, n % 2, :], ACT.Copy).then_inc(acc_free[n % 2], 1)
                act.drain().then_inc(nxt_ready, 1)

            def head(h, last=False):
                def exps(t):
                    act.wait_ge(max_done, NT * h + t + 1)
                    w = (t + 1) * P
                    act.activation(prob[:, t % 2, 0:w], prob[:, t % 2, 0:w], ACT.Exp, bias=neg_max[:, t % 2:t % 2 + 1],
                                   accum_out=row_sum[:, t % 2:t % 2 + 1]).then_inc(exp_done, 1)

                def read_next(t):
                    i, half = divmod(t, 2)
                    read_half(act, N_FOX + 4 + i, half, FILLS2 + 4 * h + i, next_tiles[i], adv=2 * h)
                    if half:
                        act.drain().then_inc(nxt_ready, 1)

                act.wait_ge(v_turned, h + 1)
                act.activation(v_tok[:, :, :], work[:, 2:4, :], ACT.Copy).then_inc(v_ready, 1)
                act.activation(silu_za[:, :], next_tiles[3][:, :], ACT.Silu)
                act.drain().then_inc(za_ready, 1)
                act.wait_ge(taken, h + 1)
                exps(0)
                for t in range(NT):
                    if t + 1 < NT:
                        exps(t + 1)
                    if t % 2 == 0:
                        split_hi(act, N_FOX + 5 + t // 2, adv=2 * h)
                    for c, a, b in fox_chunks(t):
                        act.wait_ge(p_turned, FC * h + c + 1)
                        act.activation(prob_t[:, t % 2, a:b, :], work[:, 2 + c % 2, 0:(b - a) * P], ACT.Copy).then_inc(p_copied, 1)
                    read_next(t)
                act.wait_ge(y_gated, 2 * h + 4)
                if last:
                    act.wait_ge(late_saved[0], LATE_SAVED)
                act.activation(row(ya_hi, h), y_head[:, :], ACT.Copy).then_inc(x_hi_done, 1)

            with act.Fori(0, FOX_HEADS - 1) as h:
                head(h)
            head(FOX_HEADS - 1, last=True)
            for a in range(2):
                act.drain().then_inc(acc_free[a], 2 * FOX_HEADS)
            end_stage(act, 5)

        def dve_5(dve):
            begin_stage(dve, 5)
            dve.drain().then_inc(y_gated, 2)
            for i in range(4):
                split_lo(dve, N_FOX + i + 1)

            def head(h):
                def logits(t):
                    if t >= 2:
                        dve.wait_ge(p_turned, FC * h + fox_chunks(t - 1)[0][0])
                    for c, a, b in fox_chunks(t):
                        dve.wait_ge(qk_done, FC * h + c + 1)
                        dve.scalar_tensor_tensor(prob[:, t % 2, a * P:b * P], work[:, c % 2, 0:(b - a) * P], FOX_SCALE,
                                                 f_bc[:, a * P:b * P], ALU.mult, ALU.add).then_inc(logits_done, 1)
                    dve.drain()
                    dve.wait_ge(diag_done, NT * h + t + 1)
                    dve.tensor_reduce(neg_max[:, t % 2:t % 2 + 1], prob[:, t % 2, 0:(t + 1) * P], AX.X, ALU.max,
                                      negate=True).then_inc(max_done, 1)

                def normalise(t):
                    dve.wait_ge(exp_done, NT * h + t + 1)
                    dve.reciprocal(row_inv[:, t % 2:t % 2 + 1], row_sum[:, t % 2:t % 2 + 1])
                    dve.drain()
                    w = (t + 1) * P
                    dve.tensor_scalar(prob[:, t % 2, 0:w], prob[:, t % 2, 0:w], row_inv[:, t % 2:t % 2 + 1], None,
                                      ALU.mult).then_inc(prob_done, 1)

                def gate(half):
                    dve.wait_ge(pv_done, NT * h + 4 * half + 4)
                    s = slice(half * HALF, (half + 1) * HALF)
                    dve.tensor_tensor(y_head[:, s], acc[:, 1, s], silu_za[:, s], ALU.mult).then_inc(y_gated, 1)

                dve.wait_ge(fbc_loaded, 16 * h + 16)
                logits(0)
                for t in range(NT):
                    normalise(t)
                    if t + 1 < NT:
                        logits(t + 1)
                    if t == NT - 2:
                        dve.drain().then_inc(fbc_used, 1)
                    if t % 2 == 0:
                        split_lo(dve, N_FOX + 5 + t // 2, adv=2 * h)
                    if t == 5:
                        dve.wait_ge(za_ready, h + 1)
                        gate(0)
                gate(1)
                dve.wait_ge(x_hi_done, SPLITS[5] + h + 1)
                dve.tensor_tensor(row(ya_lo, h), y_head[:, :], row(ya_hi, h).bitcast(F32), ALU.subtract
                                  ).then_inc(x_lo_done, 1)

            with dve.Fori(0, FOX_HEADS) as h:
                head(h)
            end_stage(dve, 5)

        ar = arena()
        merged = ar("merged", [P, KT, T])
        gate6 = ar("gate6", [P, 2, T])
        mix_before = ar("mix_before", [P, 2, T])
        gate6_used, gate6_done = sem("gate6_used"), sem("gate6_done")
        g_loaded6, mix_loaded = [sem("g_loaded6_0"), sem("g_loaded6_1")], [sem("mix_loaded0"), sem("mix_loaded1")]

        def sp_6(sp):
            with sp.Fori(0, 3) as j:
                for b in range(2):
                    load_w(sp, N_MIX2 + 2 + b, cols(io["w_proj_att"], (2 + b) * P + 2 * P * j), adv=j)

        def pe_6(pe):
            project(pe, N_MIX2, ya_hi, ya_lo, after=LO_SPLITS[5])
            begin_stage(pe, 6)
            with pe.Fori(0, 3) as j:
                for b in range(2):
                    project(pe, N_MIX2 + 1 + b, ya_hi, ya_lo, adv=j)
            project(pe, N_OUT1 - 1, ya_hi, ya_lo)
            end_stage(pe, 6)

        def act_6(act):
            begin_stage(act, 6)
            with act.Fori(0, 4) as j:
                for b in range(2):
                    split_hi(act, N_MIX2 + b + 1, adv=j)
                    act.wait_ge(g_loaded6[b], 16 * j + 16)
                    act.activation(gate6[:, b, :], gate6[:, b, :], ACT.Sigmoid,
                                   bias=vec1[:, VEC1["b_gate"][0] + 8:VEC1["b_gate"][1]][:, bass.ds(2 * j + b, 1)]
                                   ).then_inc(gate6_done, 1)
                    act.wait_ge(gate6_used, 2 * j + b + 3)
                    act.activation(row(ha_hi, 2 * j + b), row(merged, 2 * j + b), ACT.Copy).then_inc(x_hi_done, 1)
            end_stage(act, 6)

        def dve_6(dve):
            begin_stage(dve, 6)
            dve.drain().then_inc(gate6_used, 2)
            with dve.Fori(0, 4) as j:
                for b in range(2):
                    n = N_MIX2 + b
                    split_lo(dve, n + 1, adv=j)
                    dve.wait_ge(gate6_done, 2 * j + b + 1)
                    projected(dve, n, adv=j)
                    dve.tensor_tensor(gate6[:, b, :], acc[:, n % 2, :], gate6[:, b, :], ALU.mult).then_inc(acc_free[n % 2], 1)
                    dve.drain()
                    dve.wait_ge(mix_loaded[b], 16 * j + 16)
                    dve.tensor_tensor(row(merged, 2 * j + b), gate6[:, b, :], mix_before[:, b, :], ALU.add)
                    dve.drain().then_inc(gate6_used, 1)
                    dve.wait_ge(x_hi_done, SPLITS[6] + 2 * j + b + 1)
                    dve.tensor_tensor(row(ha_lo, 2 * j + b), row(merged, 2 * j + b), row(ha_hi, 2 * j + b).bitcast(F32),
                                      ALU.subtract).then_inc(x_lo_done, 1)
            end_stage(dve, 6)

        def pool_6(pool):
            begin_stage(pool, 6)
            for s in late_saved:
                pool.wait_ge(s, LATE_SAVED)
            with pool.Fori(0, 4) as j:
                for b in range(2):
                    wait_here(pool, gate6_used, 2 * j + b + 1)
                    pool.dma_start(gate6[:, b, :], row(ga_scr, 2 * j + b)).then_inc(g_loaded6[b], 16)
                    pool.dma_start(mix_before[:, b, :], row(merged_scr, 2 * j + b)).then_inc(mix_loaded[b], 16)
            end_stage(pool, 6)

        res = Region(at_ya, at_ya + big)("res", [P, KT, T])
        ar = Region(at_arena + big, arena_end)
        xt_tile = ar("xt_tile", [P, 2, T])
        ar = arena()
        sq7 = ar("sq7", [P, 2, T])
        sums7 = ar("sums7", [P, 2, T])
        root89 = ar("root89", [P, T])
        rstd89 = ar("rstd89", [P, T])
        at_rest8 = at_arena + big + 2 * T * 4
        root8 = Region(at_ya + big, at_ya + 2 * big)("root8", [P, T])
        norm7 = Norm(2)
        xt_loaded, res_done = [sem("xt_loaded0"), sem("xt_loaded1")], sem("res_done")
        squares_added = sem("squares_added")

        def sp_7(sp):
            with sp.Fori(0, 4) as j:
                for b in range(2):
                    load_w(sp, N_OUT1 + b, cols(io["w_out"], b * P + 2 * P * j), adv=j)

        def pe_7(pe):
            project(pe, N_OUT1, ha_hi, ha_lo, after=LO_SPLITS[6])
            begin_stage(pe, 7)
            with pe.Fori(0, 3) as j:
                for b in range(2):
                    project(pe, N_OUT1 + 1 + b, ha_hi, ha_lo, adv=j)
            project(pe, N_SMALL2 - 1, ha_hi, ha_lo)
            pe.wait_ge(dve_steps, 5)
            for i in (1, 0):
                for h in range(2):
                    mm = pe.matmul(work[:, 2 * i + h, :], ones[:, :], sums7[:, i, h * HALF:(h + 1) * HALF],
                                   start=True, stop=True)
                mm.then_inc(norm7.summed, 1)
            end_stage(pe, 7)

        def act_7(act):
            begin_stage(act, 7)

            def squares(f):
                act.wait_ge(res_done, f + 3)
                act.wait_ge(squares_added, f + 1)
                act.activation(sq7[:, 0, :], row(res, f), ACT.Square)
                act.activation(sq7[:, 1, :], row(res, f), ACT.Square, scale=dcol(vec1, VEC1, "final_norm_w", f)
                               ).then_inc(norm7.squared, 1)

            with act.Fori(0, 3) as j:
                for b in range(2):
                    split_hi(act, N_OUT1 + b + 1, adv=j)
                    squares(2 * j + b)
            split_hi(act, N_SMALL2 - 1)
            squares(KT - 2)
            act.wait_ge(w_part, 3 * 16)
            split_hi(act, N_SMALL2)
            squares(KT - 1)
            for i, (root, bank, eps) in enumerate(((root89, 2, eps2_col), (root8, 0, eps_col))):
                act.wait_ge(norm7.summed, norm7.tiles + i + 1)
                act.activation(root[:, :], work[:, bank:bank + 2, :], ACT.Sqrt, bias=eps[:, :],
                               scale=1.0 / D).then_inc(norm7.rooted, 1)
            end_stage(act, 7)

        def dve_7(dve):
            begin_stage(dve, 7)
            dve.drain().then_inc(res_done, 2)
            dve.memset(sums7[:, :, :], 0.0)
            dve.drain().then_inc(squares_added, 1)
            with dve.Fori(0, 4) as j:
                for b in range(2):
                    n = N_OUT1 + b
                    split_lo(dve, n + 1, adv=j)
                    projected(dve, n, adv=j)
                    dve.wait_ge(xt_loaded[b], 16 * j + 16)
                    dve.scalar_tensor_tensor(row(res, 2 * j + b), acc[:, n % 2, :], ada[:, 16:24][:, bass.ds(2 * j + b, 1)],
                                             xt_tile[:, b, :], ALU.mult, ALU.add).then_inc(acc_free[n % 2], 1)
                    dve.drain().then_inc(res_done, 1)
                    dve.wait_ge(norm7.squared, norm7.tiles + 2 * j + b + 1)
                    dve.tensor_tensor(sums7[:, :, :], sums7[:, :, :], sq7[:, :, :], ALU.add).then_inc(squares_added, 1)
            dve.drain()
            dve.scalar_tensor_tensor(sums7[:, 1, :], sums7[:, 0, :], EPS, sums7[:, 1, :], ALU.mult, ALU.add)
            dve.drain().then_inc(dve_steps, 1)
            dve.wait_ge(norm7.rooted, norm7.use + 1)
            dve.reciprocal(rstd89[:, :], root89[:, :])
            end_stage(dve, 7)

        def pool_7(pool):
            begin_stage(pool, 7)
            with pool.Fori(0, 4) as j:
                for b in range(2):
                    wait_here(pool, res_done, 2 * j + b + 1)
                    pool.dma_start(xt_tile[:, b, :], row(xt_scr, 2 * j + b)).then_inc(xt_loaded[b], 16)
            end_stage(pool, 7)

        ar = Region(at_rest8, arena_end)
        h2_tile = ar("h2_tile", [P, 2, T])
        w_norm2 = ar("w_norm2", [P, KT])
        h2_done, res_saved = sem("h2_done"), sem("res_saved")

        def sp_8(sp):
            wait_here(sp, lo_done, N_SMALL2 - 1)
            sp.dma_start(w_raw[:, N_SMALL2 % 2, :, 0:32], cols(w_in2f, MI, 32)).then_inc(w_loaded[N_SMALL2 % 2], 16)
            sp.dma_start(w_raw[:, N_SMALL2 % 2, :, 32:64], cols(w_in2f, MF, 32)).then_inc(w_part, 16)
            sp.dma_start(w_raw[:, N_SMALL2 % 2, :, 64:P], cols(w_in2f, GA, 64)).then_inc(w_part, 16)
            load_w(sp, N_MG, cols(w_in2f, MG))
            sp.wait_ge(res_done, KT + 2)
            sp.dma_start(res_scr, res[:, :, :]).then_inc(res_saved, 16)

        w_in2f = w_in2.rearrange("a d c -> (a d) c")

        def pe_8(pe):
            begin_stage(pe, 8)
            project(pe, N_SMALL2, ha_hi, ha_lo, after=LO_SPLITS[8])
            end_stage(pe, 8)

        def act_8(act):
            begin_stage(act, 8)
            for f in range(KT):
                act.wait_ge(h2_done, f + 1)
                act.activation(ha_hi[:, f, :], h2_tile[:, f % 2, :], ACT.Copy).then_inc(x_hi_done, 1)
            split_hi(act, N_MG)
            end_stage(act, 8)

        def dve_8(dve):
            begin_stage(dve, 8)
            dve.tensor_tensor(w_norm2[:, :], vec1[:, VEC1["final_norm_w"][0]:VEC1["final_norm_w"][1]],
                              vec2[:, VEC2["norm_g_2"][0]:VEC2["norm_g_2"][1]], ALU.mult)
            dve.drain()

            def h2(f):
                dve.scalar_tensor_tensor(h2_tile[:, f % 2, :], res[:, f, :], w_norm2[:, f:f + 1], rstd89[:, :],
                                         ALU.mult, ALU.mult).then_inc(h2_done, 1)

            h2(0)
            for f in range(KT):
                if f + 1 < KT:
                    h2(f + 1)
                dve.wait_ge(x_hi_done, SPLITS[8] + f + 1)
                dve.tensor_tensor(ha_lo[:, f, :], h2_tile[:, f % 2, :], ha_hi[:, f, :].bitcast(F32),
                                  ALU.subtract).then_inc(x_lo_done, 1)
                dve.drain()
            split_lo(dve, N_MG)
            end_stage(dve, 8)

        def pool_8(pool):
            begin_stage(pool, 8)
            end_stage(pool, 8)

        b_gla = Region(at_arena, arena_end)("b_gla", [P, NCHUNK, 1 + CHUNK])
        keep = Region(at_arena + (NCHUNK * (1 + CHUNK) * 4 + 31) // 32 * 32, arena_end)
        B_tok = keep("B_tok", [P, NT, 8])
        em_tok = keep("em_tok", [P, NT, 8])
        PAD = 3
        nxt = keep("nxt", [P, 4, T + 8])
        nxt_t = nxt[:, :, PAD:PAD + T]
        at_arena2 = keep.at
        y2 = Region(at_ya + big, at_ya + 2 * big)("y2", [P, KT, T])
        ar = Region(at_arena2, arena_end)
        spa = {k: ar(f"spa_{k}", [P, T]) for k in ("u", "e", "relu", "s", "s2", "p")}
        bias_rows = ar("bias_rows", [P, 3 * P])
        bias_tile = ar("bias_tile", [P, BANDW])
        bias_moved = sem("bias_moved")
        rel_rev = io["rel_bias_2"].rearrange("a h r -> (a h) r")
        ar = Region(at_ya, at_ya + big)
        spm = {k: ar(f"spm_{k}", [32, T]) for k in ("u", "e", "relu", "s", "s2", "p")}
        ga_t = Region(ar.at, at_ya + big)("ga_t", [P, T])
        ig9 = ar("ig9", [32, T])
        f9 = ar("f9", [32, T])
        m9, em9 = spm["relu"], spm["s2"]
        softplus_ml, softplus_al = Softplus(1), Softplus(2)
        gates_read, alpha_mul, m_ready, em_ready = sem("gates_read"), sem("alpha_mul"), sem("m_ready"), sem("em_ready")
        ab_ready, turned9 = sem("ab_ready"), sem("turned9")

        def sp_9(sp):
            for j in range(1, PAIRS):
                load_w(sp, N_MG + j, cols(w_in2f, MG + P * j))
            for j in range(2):
                load_w(sp, N_GG + j, cols(w_in2f, GG + P * j))

        def act_9(act):
            begin_stage(act, 9)

            def silu_gate(n, i):
                if n > N_MG + 1:
                    split_hi(act, n + 1)
                projected(act, n)
                act.activation(y2[:, i, :], acc[:, n % 2, :], ACT.Silu).then_inc(acc_free[n % 2], 1)

            act.wait_ge(res_saved, 16)
            act.activation(ig9[:, :], acc[0:32, N_SMALL2 % 2, :], ACT.Identity, bias=gate_bias2[0:32, :])
            act.activation(ga_t[64:64 + GLA_RANK, :], acc[64:64 + GLA_RANK, N_SMALL2 % 2, :], ACT.Copy)
            act.drain().then_inc(gates_read, 1)
            split_hi(act, N_MG + 1)
            softplus_ml.act(act, spm["u"][:, :], spm["e"][:, :], spm["relu"][:, :])
            silu_gate(N_MG, 3)
            split_hi(act, N_MG + 2)
            softplus_al.act(act, spa["u"][:, :], spa["e"][:, :], spa["relu"][:, :])
            for j in range(1, PAIRS):
                silu_gate(N_MG + j, 3 + j)
            split_hi(act, N_GG + 1)
            act.wait_ge(m_ready, 1)
            act.activation(em9[:, :], m9[:, :], ACT.Exp, scale=-1.0).then_inc(em_ready, 1)
            projected(act, N_GG)
            act.activation(y2[:, 6, :], acc[:, N_GG % 2, :], ACT.Silu).then_inc(acc_free[N_GG % 2], 1)
            act.wait_ge(turned9, 1)
            for dst, bank in ((B_tok, 2), (em_tok, 3)):
                act.activation(dst[:, :, :], work[:, bank, 0:NT * 32].rearrange("p (t h) -> p t h", h=32)[:, :, 0:8], ACT.Copy)
            silu_gate(N_GG + 1, 7)
            for i in range(4):
                n = N_BAND + i
                split_hi(act, n + 1)
                projected(act, n)
                act.activation(nxt_t[:, i, :], acc[:, n % 2, :], ACT.Copy).then_inc(acc_free[n % 2], 1)
            act.drain().then_inc(nxt_ready, 4)
            end_stage(act, 9)

        def pe_9(pe):
            begin_stage(pe, 9)
            project(pe, N_MG, ha_hi, ha_lo)
            pe.wait_ge(gates_read, 1)
            for h in range(2):
                mm = pe.matmul(work[:, h, :], w_alpha[64:64 + GLA_RANK, :],
                               ga_t[64:64 + GLA_RANK, h * HALF:(h + 1) * HALF], start=True, stop=True)
            mm.then_inc(alpha_mul, 1)
            for j in range(1, PAIRS):
                project(pe, N_MG + j, ha_hi, ha_lo)
            project(pe, N_GG, ha_hi, ha_lo)
            pe.wait_ge(ab_ready, 1)
            pe.wait_ge(em_ready, 1)
            for src, bank in ((spm["u"], 2), (em9, 3)):
                for i in range(NT):
                    mm = pe.transpose(work[:, bank, i * 32:(i + 1) * 32], src[:, i * P:(i + 1) * P], ident[0:32, 0:32])
            mm.then_inc(turned9, 1)
            project(pe, N_GG + 1, ha_hi, ha_lo)
            for i in range(4):
                project(pe, N_BAND + i, ha_hi, ha_lo)
            end_stage(pe, 9)

        def dve_9(dve):
            begin_stage(dve, 9)
            dve.wait_ge(gates_read, 1)
            dve.tensor_scalar(spm["u"][:, :], acc[32:64, N_SMALL2 % 2, :], gate_bias2[32:64, :], -1.0, ALU.add,
                              ALU.mult).then_inc(acc_free[N_SMALL2 % 2], 1)
            dve.drain().then_inc(softplus_ml.ready, 1)
            split_lo(dve, N_MG + 1)
            softplus_ml.dve_ratio(dve, *(spm[k][:, :] for k in ("e", "s", "s2")))
            split_lo(dve, N_MG + 2)
            dve.wait_ge(alpha_mul, 1)
            dve.tensor_scalar(spa["u"][:, :], work[:, 0:2, :].rearrange("p a b -> p (a b)"),
                              vec2[:, VEC2["b_alpha_2"][0]:VEC2["b_alpha_2"][1]], -1.0, ALU.add, ALU.mult)
            dve.drain().then_inc(softplus_al.ready, 1)
            softplus_ml.dve_series(dve, *(spm[k][:, :] for k in ("relu", "s", "s2", "p")))
            dve.drain()
            lf = spm["e"]
            dve.tensor_scalar(lf[:, :], spm["p"][:, :], -1.0, None, ALU.mult)
            dve.drain()
            dve.tensor_tensor_scan(f9[:, :], lf[:, :], zero_col[0:32, :].to_broadcast([32, T]), 0.0, ALU.add, ALU.add)
            dve.tensor_tensor_scan(m9[:, :], lf[:, :], ig9[:, :], 0.0, ALU.add, ALU.max).then_inc(m_ready, 1)
            dve.drain()
            split_lo(dve, N_GG)
            dve.tensor_tensor(spm["u"][:, :], ig9[:, :], f9[:, :], ALU.subtract)
            dve.tensor_tensor(spm["s"][:, :], f9[:, :], m9[:, :], ALU.subtract)
            dve.drain().then_inc(ab_ready, 1)
            softplus_al.dve_ratio(dve, *(spa[k][:, :] for k in ("e", "s", "s2")))
            split_lo(dve, N_GG + 1)
            softplus_al.dve_series(dve, *(spa[k][:, :] for k in ("relu", "s", "s2", "p")))
            split_lo(dve, N_BAND)
            dve.drain()
            la = spa["u"]
            dve.tensor_scalar(la[:, :], spa["p"][:, :], -1.0 / GLA_TAU, None, ALU.mult)
            dve.drain()
            for c in range(NCHUNK):
                dve.tensor_tensor_scan(b_gla[:, c, 1:1 + CHUNK], la[:, c * CHUNK:(c + 1) * CHUNK],
                                       zero_col[:, :].to_broadcast([P, CHUNK]), 0.0, ALU.add, ALU.add)
            for i in range(4):
                split_lo(dve, N_BAND + i + 1)
            end_stage(dve, 9)

        def pool_9(pool):
            begin_stage(pool, 9)
            pool.dma_start(root8_scr, root8[:, :]).then_inc(sums_saved, 16)
            pool.memset(b_gla[:, :, 0:1], 0.0)
            pool.memset(nxt[:, :, 0:PAD], 0.0)
            with pool.Fori(0, ML_HEADS) as h:
                pool.dma_start(bias_rows[:, P - 1:3 * P - 1],
                               rel_rev[bass.ds(h, 1), 0:2 * P].rearrange("a r -> (a r)").partition_broadcast(P)
                               ).then_inc(bias_moved, 16)
                wait_here(pool, bias_moved, 64 * h + 16)
                pool.tensor_copy(bias_rows[:, 0:P - 1], bias_rows[:, P - 1:P].to_broadcast([P, P - 1]))
                pool.tensor_copy(bias_rows[:, 3 * P - 1:3 * P], bias_rows[:, P - 1:P])
                pool.tensor_copy(bias_tile[:, 0:3 * P], bias_rows[:, P - 1:P].to_broadcast([P, 3 * P]))
                pool.drain()
                pool.dma_start(skew_scr.rearrange("(q w) -> q w", w=3 * P), bias_rows[:, :]).then_inc(bias_moved, 16)
                wait_here(pool, bias_moved, 64 * h + 32)
                pool.dma_start(bias_tile[:, 3 * P:BANDW],
                               skew_scr[P - 1:P - 1 + P * (3 * P - 1)].rearrange("(q w) -> q w", w=3 * P - 1)[:, 0:2 * P]
                               ).then_inc(bias_moved, 16)
                wait_here(pool, bias_moved, 64 * h + 48)
                pool.memset(bias_tile[0:HD, BANDW - HD:BANDW], MASKED)
                pool.memset(bias_tile[HD:P, 0:HD], MASKED)
                pool.drain()
                pool.dma_start(bias_scr[bass.ds(h, 1), :, :].rearrange("a q w -> q (a w)"), bias_tile[:, :]
                               ).then_inc(bias_moved, 16)
                wait_here(pool, bias_moved, 64 * h + 64)
            pool.wait_ge(ab_ready, 1)
            pool.dma_start(ml_a_scr, spm["s"][0:8, :]).then_inc(sums_saved, 16)
            pool.wait_ge(sums_saved, 64)
            end_stage(pool, 9)

        ar = Region(at_arena2, arena_end)
        bq = ar("bq", [P, T])
        bk = ar("bk", [P, T])
        bv_tok = ar("bv_tok", [P, NT, P])
        band_max = ar("band_max", [P, 2 * NT])
        band_sum = ar("band_sum", [P, 2 * NT])
        band_inv = ar("band_inv", [P, 2 * NT])
        ar = Region(at_ya, at_ya + big)
        band_bias = ar("band_bias", [P, 2, BANDW])
        band_p = ar("band_p", [P, 2, BANDW])
        band_pt = ar("band_pt", [P, 2, BAND_TILES, P])
        att_tok = ar("att_tok", [P, 2 * NT, HD])
        BU = 2 * NT
        FILLS = FILLS2 + 4 * FOX_HEADS
        bias_loaded, band_gated = sem("bias_loaded"), sem("band_gated")
        V5, U5 = FOX_HEADS, FOX_HEADS * NT
        C5 = FOX_HEADS * FC
        N5 = 4 * (FOX_HEADS + 1)
        tok_done, feat_turned = sem("tok_done"), sem("feat_turned")
        HD_SCALE = float(HD) ** -0.5

        def band_tiles(u):
            return min(u // 2, BAND_TILES - 1) + 1

        def band_chunks(u):
            first = sum(1 if band_tiles(v) <= 4 else 2 for v in range(u))
            n = band_tiles(u)
            return [(first, 0, n)] if n <= 4 else [(first, 0, 3), (first + 1, 3, n)]

        BC = band_chunks(BU)[0][0]

        def sp_10(sp):
            for i, off in enumerate((AQ, AK, AV, AG)):
                load_w(sp, N_BAND + i, cols(w_in2f, off))
            with sp.Fori(0, PAIRS - 1) as p:
                for i, off in enumerate((AQ, AK, AV, AG)):
                    load_w(sp, N_BAND + 4 + i, cols(w_in2f, off + P + P * p), adv=2 * p)

        def pool_10(pool):
            begin_stage(pool, 10)
            with pool.Fori(0, PAIRS) as p:
                wait_here(pool, band_gated, p + 1)
                pool.dma_start(band_bias[:, :, :], bias_scr[bass.ds(2 * p, 2), :, :].rearrange("h q w -> q h w")
                               ).then_inc(bias_loaded, 16)
            end_stage(pool, 10)

        def pe_10(pe):
            begin_stage(pe, 10)
            with pe.Fori(0, PAIRS) as p:

                def fill(q):
                    project_part(pe, N_BAND + 4 + q // 4, q % 4, FILLS + 4 * p + q // 4, adv=2 * p)

                def scores(u):
                    m, r = divmod(u, 2)
                    k0 = m + 1 - band_tiles(u)
                    for c, a, b in band_chunks(u):
                        if c >= 2:
                            pe.wait_ge(logits_done, C5 + BC * p + c - 1)
                        pe.matmul(work[:, c % 2, 0:(b - a) * P], bq[r * HD:(r + 1) * HD, m * P:(m + 1) * P],
                                  bk[r * HD:(r + 1) * HD, (k0 + a) * P:(k0 + b) * P], start=True, stop=True).then_inc(qk_done, 1)

                def turn_probs(u):
                    pe.wait_ge(exp_done, U5 + BU * p + u + 1)
                    for c, a, b in band_chunks(u):
                        if c >= 2:
                            pe.wait_ge(p_copied, C5 + BC * p + c - 1)
                        for t in range(a, b):
                            mm = pe.transpose(work[:, 2 + c % 2, (t - a) * P:(t - a + 1) * P], band_p[:, u % 2, t * P:(t + 1) * P],
                                              ident[:, :])
                        mm.then_inc(p_turned, 1)

                def weigh_values(u):
                    m, r = divmod(u, 2)
                    n = band_tiles(u)
                    for c, a, b in band_chunks(u):
                        pe.wait_ge(p_copied, C5 + BC * p + c + 1)
                        for t in range(a, b):
                            mm = pe.matmul(acc[:, 1, u * HD:(u + 1) * HD], band_pt[:, u % 2, t, :],
                                           bv_tok[:, m + 1 - n + t, r * HD:(r + 1) * HD], start=(t == 0), stop=(t == n - 1))
                    mm.then_inc(pv_done, 1)

                pe.wait_ge(band_gated, p + 1)
                pe.wait_ge(nxt_ready, N5 + 4 * p + 4)
                for b in range(NT):
                    mm = pe.transpose(work[:, 2 + b // 4, (b % 4) * P:(b % 4 + 1) * P], nxt_t[:, 2, b * P:(b + 1) * P], ident[:, :])
                mm.then_inc(v_turned, 1)
                pe.wait_ge(taken, V5 + p + 1)
                scores(0)
                scores(1)
                fill(0)
                pe.wait_ge(v_ready, V5 + p + 1)
                for u in range(BU):
                    if 0 < u < BU - 1:
                        fill(u)
                    turn_probs(u)
                    if u + 2 < BU:
                        scores(u + 2)
                    weigh_values(u)
                fill(BU - 1)
                pe.wait_ge(tok_done, p + 1)
                for b in range(NT):
                    mm = pe.transpose(work[:, 2 + b // 4, (b % 4) * P:(b % 4 + 1) * P], att_tok[:, 2 * b:2 * b + 2, :], ident[:, :])
                mm.then_inc(feat_turned, 1)
            end_stage(pe, 10)

        def act_10(act):
            begin_stage(act, 10)
            with act.Fori(0, PAIRS) as p:

                def exps(u):
                    act.wait_ge(max_done, U5 + BU * p + u + 1)
                    w = band_tiles(u) * P
                    act.activation(band_p[:, u % 2, 0:w], band_p[:, u % 2, 0:w], ACT.Exp, bias=band_max[:, u:u + 1],
                                   accum_out=band_sum[:, u:u + 1]).then_inc(exp_done, 1)

                def read_next(h):
                    i, half = divmod(h, 2)
                    read_half(act, N_BAND + 4 + i, half, FILLS + 4 * p + i, nxt_t[:, i, :], adv=2 * p)

                act.activation(row(y2, p), nxt_t[:, 3, :], ACT.Silu)
                act.wait_ge(v_turned, V5 + p + 1)
                act.activation(bv_tok[:, :, :], work[:, 2:4, :], ACT.Copy).then_inc(v_ready, 1)
                act.wait_ge(taken, V5 + p + 1)
                exps(0)
                for u in range(BU):
                    if u % 4 == 1:
                        split_hi(act, N_BAND + 5 + u // 4, adv=2 * p)
                    if u + 1 < BU:
                        exps(u + 1)
                    for c, a, b in band_chunks(u):
                        act.wait_ge(p_turned, C5 + BC * p + c + 1)
                        act.activation(band_pt[:, u % 2, a:b, :], work[:, 2 + c % 2, 0:(b - a) * P], ACT.Copy).then_inc(p_copied, 1)
                    if u % 2 == 1:
                        read_next(u // 2)
                act.drain().then_inc(nxt_ready, 4)
            end_stage(act, 10)

        def dve_10(dve):
            begin_stage(dve, 10)
            dve.drain().then_inc(band_gated, 1)
            with dve.Fori(0, PAIRS) as p:
                dve.wait_ge(nxt_ready, N5 + 4 * p + 4)
                dve.tensor_copy(bq[:, :], nxt_t[:, 0, :])
                dve.tensor_copy(bk[:, :], nxt_t[:, 1, :])
                dve.drain().then_inc(taken, 1)
                dve.wait_ge(bias_loaded, 16 * p + 16)
                for u in range(BU):
                    if u >= 2:
                        dve.wait_ge(p_turned, C5 + BC * p + band_chunks(u - 1)[0][0])
                    w = band_tiles(u) * P
                    for c, a, b in band_chunks(u):
                        dve.wait_ge(qk_done, C5 + BC * p + c + 1)
                        dve.scalar_tensor_tensor(band_p[:, u % 2, a * P:b * P], work[:, c % 2, 0:(b - a) * P], HD_SCALE,
                                                 band_bias[:, u % 2, BANDW - w + a * P:BANDW - w + b * P],
                                                 ALU.mult, ALU.add).then_inc(logits_done, 1)
                    dve.drain()
                    dve.tensor_reduce(band_max[:, u:u + 1], band_p[:, u % 2, 0:w], AX.X, ALU.max,
                                      negate=True).then_inc(max_done, 1)
                    if u % 4 == 2:
                        split_lo(dve, N_BAND + 5 + u // 4, adv=2 * p)
                dve.wait_ge(pv_done, U5 + BU * p + BU)
                dve.reciprocal(band_inv[:, :], band_sum[:, :])
                dve.drain()
                dve.tensor_tensor(att_tok[:, :, :], acc[:, 1, :].rearrange("p (u d) -> p u d", d=HD),
                                  band_inv[:, :].unsqueeze(2).to_broadcast([P, BU, HD]), ALU.mult).then_inc(tok_done, 1)
                dve.wait_ge(feat_turned, p + 1)
                dve.tensor_tensor(row(y2, p), work[:, 2:4, :].rearrange("p a b -> p (a b)"), row(y2, p), ALU.mult)
                dve.drain().then_inc(band_gated, 1)
            end_stage(dve, 10)

        ar = Region(at_arena2, arena_end)
        ml_conv = ar("ml_conv", [P, 2, T])
        mq_t = ar("mq_t", [P, T])
        mk_t = ar("mk_t", [P, T])
        mv_tok = ar("mv_tok", [P, 2 * NT, HD + 1])
        den = ar("den", [P, 2 * NT])
        den_abs = ar("den_abs", [P, 2 * NT])
        ss11 = ar("ss11", [P, 2 * NT])
        root11 = ar("root11", [P, 2 * NT])
        ar = Region(at_ya, at_ya + big)
        BLOCKS = NT * (NT + 1) // 2
        at_pt = ar.at
        ml_pt = ar("ml_pt", [P, BLOCKS, P])
        h_sq = Region(at_pt, ar.at)("h_sq", [P, 2 * NT, HD])
        so = ar("so", [P, T])
        h_tok = ar("h_tok", [P, 2 * NT, HD])
        ar = Region(at_arena2 + 20 * T + 512, arena_end)
        a_bc = ar("a_bc", [P, 2, T])
        abc_loaded, ml_gated = sem("abc_loaded"), sem("ml_gated")
        ml_conved, mqk_ready, so_ready = sem("ml_conved"), sem("mqk_ready"), sem("so_ready")
        d_done, pt_done, pt_masked = sem("d_done"), sem("pt_done"), sem("pt_masked")
        V10, U10, C10, FILLS10 = V5 + PAIRS, U5 + PAIRS * BU, C5 + PAIRS * BC, FILLS + PAIRS * 4
        ss_ready, root_ready = sem("ss_ready"), sem("root_ready")
        SLOTS = HALF // (HD + 1)
        out_banks = [acc[:, 1, 0:HALF], acc[:, 1, HALF:2 * HALF], work[:, 2, :]]
        START_FILLS = 5
        FILL_UNITS = [2, 3, 5, 6, 7, 9, 10, 11]
        LAST_FILLS = 16 - START_FILLS - len(FILL_UNITS)

        def pt_row(jb):
            at = jb * NT - jb * (jb - 1) // 2
            return ml_pt[:, at:at + NT - jb, :].rearrange("p a b -> p (a b)")

        def ml_chunks(u):
            widths = [(NT - v % NT) * P for v in range(u + 1)]
            first = sum((w + HALF - 1) // HALF for w in widths[:-1])
            return [(first + i, a, min(a + HALF, widths[-1])) for i, a in enumerate(range(0, widths[-1], HALF))]

        MC = 2 * sum(((NT - jb) * P + HALF - 1) // HALF for jb in range(NT))

        def slot_groups():
            for g in range(0, 2 * NT, SLOTS):
                n = min(SLOTS, 2 * NT - g)
                yield slice(g, g + n), n, out_banks[g // SLOTS][:, 0:n * (HD + 1)].rearrange("p (u e) -> p u e", e=HD + 1)

        def sp_11(sp):
            for i, off in enumerate((MQ, MK, MV, MO)):
                load_w(sp, N_ML + i, cols(w_in2f, off))
            with sp.Fori(0, PAIRS - 1) as p:
                for i, off in enumerate((MQ, MK, MV, MO)):
                    load_w(sp, N_ML + 4 + i, cols(w_in2f, off + P + P * p), adv=2 * p)

        def pool_11(pool):
            begin_stage(pool, 11)
            pool.memset(mv_tok[:, :, HD:HD + 1], 1.0)
            zero_fill = pool.to_reg(0.0)
            with pool.Fori(0, PAIRS) as p:
                wait_here(pool, ml_gated, p + 1)
                for r in range(2):
                    pool.dma_start(a_bc[:, r, :], ml_a_scr[bass.ds(2 * p + r, 1), :].rearrange("a t -> (a t)").partition_broadcast(P)
                                   ).then_inc(abc_loaded, 16)
                wait_here(pool, so_ready, p + 1)
                pool.tensor_tensor(row(y2, 3 + p), row(y2, 3 + p), so[:, :], ALU.mult)
                for u in range(BU):
                    wait_here(pool, pt_done, MC * p + ml_chunks(u)[0][0] + 1)
                    diag = pt_row(u % NT)[:, 0:P]
                    pool.affine_select(out=diag, in_=diag, compare_op=ALU.is_ge, fill=zero_fill, base=0,
                                       pattern=[[1, P]], channel_multiplier=-1).then_inc(pt_masked, 1)
            end_stage(pool, 11)

        def pe_11(pe):
            begin_stage(pe, 11)
            with pe.Fori(0, PAIRS) as p:

                def fill(q):
                    project_part(pe, N_ML + 4 + q // 4, q % 4, FILLS10 + 4 * p + q // 4, adv=2 * p)

                def scores(u):
                    r, jb = divmod(u, NT)
                    for c, a, b in ml_chunks(u):
                        if c >= 2:
                            pe.wait_ge(pt_done, MC * p + c - 1)
                        pe.matmul(work[:, c % 2, 0:b - a], mk_t[r * HD:(r + 1) * HD, jb * P:(jb + 1) * P],
                                  mq_t[r * HD:(r + 1) * HD, jb * P + a:jb * P + b], start=True, stop=True).then_inc(qk_done, 1)

                def weigh_values(u):
                    r, tb = divmod(u, NT)
                    s = 2 * tb + r
                    o = out_banks[s // SLOTS][:, s % SLOTS * (HD + 1):(s % SLOTS + 1) * (HD + 1)]
                    for jb in range(tb + 1):
                        mm = pe.matmul(o, pt_row(jb)[:, (tb - jb) * P:(tb - jb + 1) * P], mv_tok[:, 2 * jb + r, :],
                                       start=(jb == 0), stop=(jb == tb))
                    mm.then_inc(pv_done, 1)

                pe.wait_ge(ml_gated, p + 1)
                pe.wait_ge(nxt_ready, N5 + 4 * (PAIRS + 1) + 4 * p)
                for b in range(NT):
                    mm = pe.transpose(work[:, 2 + b // 4, (b % 4) * P:(b % 4 + 1) * P], nxt_t[:, 2, b * P:(b + 1) * P], ident[:, :])
                mm.then_inc(v_turned, 1)
                for q in range(START_FILLS):
                    fill(q)
                pe.wait_ge(mqk_ready, 2 * p + 2)
                scores(0)
                scores(1)
                pe.wait_ge(v_ready, V10 + p + 1)
                for u in range(BU):
                    if u in FILL_UNITS and u != NT - 1:
                        fill(START_FILLS + FILL_UNITS.index(u))
                    pe.wait_ge(pt_masked, BU * p + u + 1)
                    pe.wait_ge(pt_done, MC * p + ml_chunks(u)[-1][0] + 1)
                    if u == NT - 1:
                        weigh_values(u)
                        fill(START_FILLS + FILL_UNITS.index(u))
                    if u + 2 < BU:
                        scores(u + 2)
                    if u != NT - 1:
                        weigh_values(u)
                for q in range(16 - LAST_FILLS, 16):
                    fill(q)
                pe.wait_ge(tok_done, PAIRS + p + 1)
                for b in range(NT):
                    mm = pe.transpose(acc[:, 1, b * P:(b + 1) * P], h_tok[:, 2 * b:2 * b + 2, :], ident[:, :])
                mm.then_inc(feat_turned, 1)
            end_stage(pe, 11)

        def act_11(act):
            begin_stage(act, 11)
            with act.Fori(0, PAIRS) as p:

                def read_next(h):
                    i, half = divmod(h, 2)
                    read_half(act, N_ML + 4 + i, half, FILLS10 + 4 * p + i, nxt_t[:, i, :], adv=2 * p)

                def exps(u):
                    r, jb = divmod(u, NT)
                    if u == NT:
                        act.wait_ge(pv_done, U10 + BU * p + NT)
                    act.activation(pt_row(jb), a_bc[:, r, jb * P:], ACT.Exp, bias=B_tok[:, jb, :][:, bass.ds(2 * p + r, 1)]
                                   ).then_inc(d_done, 1)

                split_hi(act, N_ML + 5, adv=2 * p)
                act.activation(so[:, :], nxt_t[:, 3, :], ACT.Sigmoid).then_inc(so_ready, 1)
                act.wait_ge(v_turned, V10 + p + 1)
                act.activation(mv_tok[:, :, 0:HD], work[:, 2:4, :].rearrange("p a (b d) -> p (a b) d", d=HD),
                               ACT.Copy).then_inc(v_ready, 1)
                for i, dst in enumerate((mq_t, mk_t)):
                    act.wait_ge(ml_conved, 2 * p + i + 1)
                    act.activation(dst[:, :], ml_conv[:, i, :], ACT.Silu).then_inc(mqk_ready, 1)
                    read_next(i)
                act.wait_ge(abc_loaded, 32 * p + 32)
                exps(0)
                exps(1)
                for u in range(BU):
                    if u + 2 < BU:
                        exps(u + 2)
                    if u in (1, 6, 11):
                        split_hi(act, N_ML + 6 + u // 5, adv=2 * p)
                    if u in FILL_UNITS[::2]:
                        read_next(2 + FILL_UNITS.index(u) // 2)
                read_next(6)
                act.wait_ge(ss_ready, p + 1)
                act.activation(root11[:, :], ss11[:, :], ACT.Sqrt, bias=eps_col[:, :], scale=1.0 / HD).then_inc(root_ready, 1)
                read_next(7)
                act.drain().then_inc(nxt_ready, 4)
            for a in range(2):
                act.drain().then_inc(acc_free[a], 4 * PAIRS)
            end_stage(act, 11)

        def dve_11(dve):
            begin_stage(dve, 11)
            dve.drain().then_inc(ml_gated, 1)
            with dve.Fori(0, PAIRS) as p:
                dve.wait_ge(nxt_ready, N5 + 4 * (PAIRS + 1) + 4 * p)
                for i in range(2):
                    conv_taps(dve, ml_conv[:, i, :], lambda k: nxt[:, i, k:k + T],
                              lambda k: vec2[:, VEC2["conv_w_2"][0] + 2 * PAIRS * k + PAIRS * i:][:, bass.ds(p, 1)]
                              ).then_inc(ml_conved, 1)
                    if i == 0:
                        split_lo(dve, N_ML + 5, adv=2 * p)
                for u in range(BU):
                    dve.wait_ge(d_done, BU * p + u + 1)
                    for c, a, b in ml_chunks(u):
                        dve.wait_ge(qk_done, C10 + MC * p + c + 1)
                        pt = pt_row(u % NT)[:, a:b]
                        dve.scalar_tensor_tensor(pt, work[:, c % 2, 0:b - a], HD_SCALE, pt, ALU.mult, ALU.mult
                                                 ).then_inc(pt_done, 1)
                    if u in (2, 7, 12):
                        split_lo(dve, N_ML + 6 + u // 5, adv=2 * p)
                dve.wait_ge(pv_done, U10 + BU * p + BU)
                for us, n, out11 in slot_groups():
                    dve.tensor_copy(den[:, us], out11[:, :, HD])
                dve.drain()
                dve.scalar_tensor_tensor(den_abs[:, :], den[:, :], -1.0, den[:, :], ALU.mult, ALU.max)
                dve.drain()
                dve.tensor_tensor(den[:, :].rearrange("p (t r) -> p t r", r=2), den_abs[:, :].rearrange("p (t r) -> p t r", r=2),
                                  em_tok[:, :, bass.ds(2 * p, 2)], ALU.max)
                dve.drain()
                dve.reciprocal(den_abs[:, :], den[:, :])
                dve.drain()
                for us, n, out11 in slot_groups():
                    dve.tensor_tensor(h_tok[:, us, :], out11[:, :, 0:HD],
                                      den_abs[:, us].unsqueeze(2).to_broadcast([P, n, HD]), ALU.mult)
                dve.drain()
                dve.tensor_tensor(h_sq[:, :, :], h_tok[:, :, :], h_tok[:, :, :], ALU.mult)
                dve.drain()
                dve.tensor_reduce(ss11[:, :], h_sq[:, :, :], AX.X, ALU.add).then_inc(ss_ready, 1)
                dve.wait_ge(root_ready, p + 1)
                dve.reciprocal(den[:, :], root11[:, :])
                dve.drain()
                dve.tensor_tensor(h_tok[:, :, :], h_tok[:, :, :], den[:, :].unsqueeze(2).to_broadcast([P, 2 * NT, HD]),
                                  ALU.mult).then_inc(tok_done, 1)
                dve.wait_ge(feat_turned, PAIRS + p + 1)
                dve.wait_ge(pt_masked, BU * p + BU)
                dve.scalar_tensor_tensor(row(y2, 3 + p), acc[:, 1, :], dcol(vec2, VEC2, "ml_norm_g_2", p), row(y2, 3 + p),
                                         ALU.mult, ALU.mult)
                dve.drain().then_inc(ml_gated, 1)
            end_stage(dve, 11)

        ar = Region(at_arena2, arena_end)
        gq_t = ar("gq_t", [P, T])
        gv_tok = ar("gv_tok", [P, NCHUNK, GLA_HEADS * GLA_DV])
        in_ha = Region(at_ha, at_ya)
        e_b = in_ha("e_b", [P, T])
        e_q = in_ha("e_q", [P, T])
        e_end = in_ha("e_end", [P, T])
        e_k = in_ha("e_k", [P, 2, NSUB, CHUNK])
        k_ref = in_ha("k_ref", [P, 2, NSUB, CHUNK])
        q_own = in_ha("q_own", [P, 2, NSUB, GLA_HEADS, SUB])
        q_dec = ar("q_dec", [P, 2, CHUNK])
        k_dec = ar("k_dec", [P, 2, CHUNK])
        k_tok = ar("k_tok", [P, 2, P])
        att_gla = ar("att_gla", [P, 2, GLA_HEADS, CHUNK])
        s_gla = ar("s_gla", [P, GLA_HEADS * GLA_DV])
        kv_own = ar("kv_own", [P, GLA_HEADS * GLA_DV])
        own = ar("own", [P, GLA_HEADS * GLA_DV])
        ss12 = ar("ss12", [P, NCHUNK * GLA_HEADS])
        root12 = ar("root12", [P, NCHUNK * GLA_HEADS])
        inv12 = ar("inv12", [P, NCHUNK * GLA_HEADS])
        o_tok = in_ha("o_tok", [P, NCHUNK, GLA_HEADS * GLA_DV])
        o_sq = in_ha("o_sq", [P, NCHUNK, GLA_HEADS * GLA_DV])
        gk_t, gv_t = nxt_t[:, 1, :], nxt_t[:, 2:4, :]
        own_ready, decay_args, decays_ready = sem("own_ready"), sem("decay_args"), sem("decays_ready")
        karg_done, kexp_done, chunk_ready, kdec_ready = sem("karg_done"), sem("kexp_done"), sem("chunk_ready"), sem("kdec_ready")
        kdec_turned, ktok_ready, gkv_done = sem("kdec_turned"), sem("ktok_ready"), sem("gkv_done")
        qdec_ready = sem("qdec_ready")
        gatt_done, gatt_masked, go_done, gstate_done, go_copied = (sem("gatt_done"), sem("gatt_masked"), sem("go_done"),
                                                                   sem("gstate_done"), sem("go_copied"))
        V11 = V10 + PAIRS
        b_now = b_gla[:, :, 1:1 + CHUNK]
        b_ref = b_gla[:, :, 0:CHUNK].rearrange("p c (s t) -> p c s t", t=SUB)[:, :, :, 0:1]
        NXT_READY = N5 + 4 * (2 * PAIRS + 1)
        res_back = sem("res_back")

        w_out2 = io["w_out_2"].rearrange("a e d -> (a e) d")

        def at_chunk(x, c):
            return x[:, bass.ds(c * CHUNK, CHUNK)]

        def sp_12(sp):
            for i, off in enumerate((GQ, GK, GV, GV + P)):
                load_w(sp, N_GLA + i, cols(w_in2f, off))
            for i in range(2):
                load_w(sp, N_OUT2 + i, cols(w_out2, i * P))
            sp.wait_ge(stage_done, 4 * 12)
            sp.dma_start(res[:, :, :], res_scr).then_inc(res_back, 16)

        def pool_12(pool):
            begin_stage(pool, 12)
            pool.memset(own[:, :], 0.0)
            pool.memset(s_gla[:, :], 0.0)
            pool.drain()
            for h in range(GLA_HEADS):
                pool.memset(own[h * GLA_DK:(h + 1) * GLA_DK, h * GLA_DV:(h + 1) * GLA_DV], 1.0)
                pool.drain()
            pool.drain().then_inc(own_ready, 1)
            pool.wait_ge(decays_ready, 2)

            def decay_ends(c, b):
                pool.tensor_tensor(k_dec[:, b, :], at_chunk(gk_t, c), at_chunk(e_end, c), ALU.mult).then_inc(kdec_ready, 1)
                pool.tensor_tensor(q_dec[:, b, :], at_chunk(gq_t, c), at_chunk(e_b, c), ALU.mult).then_inc(qdec_ready, 1)

            decay_ends(0, 0)
            decay_ends(1, 1)
            with pool.Fori(0, NCHUNK // 2 - 1) as i:
                for b in range(2):
                    wait_here(pool, go_done, 2 * i + b + 1)
                    decay_ends(2 * i + b + 2, b)
            end_stage(pool, 12)

        def pe_12(pe):
            begin_stage(pe, 12)
            pe.wait_ge(nxt_ready, NXT_READY)
            for c in range(NCHUNK):
                for i in range(2):
                    at = c * 2 + i
                    mm = pe.transpose(work[:, at // 4, at % 4 * P:(at % 4 + 1) * P], gv_t[:, i, c * P:(c + 1) * P], ident[:, :])
            mm.then_inc(v_turned, 1)
            pe.wait_ge(v_ready, V11 + 1)

            def turn_keys(c, b):
                pe.wait_ge(kdec_ready, c + 1)
                if not (isinstance(c, int) and c == 0):
                    pe.wait_ge(ktok_ready, c)
                pe.transpose(work[:, 3, 0:P], k_dec[:, b, :], ident[:, :]).then_inc(kdec_turned, 1)

            def attend(c, b):
                pe.wait_ge(chunk_ready, c + 1)
                for s in range(NSUB):
                    mm = pe.matmul(accf[:, b * HALF + s * GLA_HEADS * SUB:b * HALF + (s + 1) * GLA_HEADS * SUB], k_ref[:, b, s, :],
                                   q_own[:, b, s, :, :], start=True, stop=True)
                mm.then_inc(gatt_done, 1)

            def sum_keys(c, b):
                pe.wait_ge(ktok_ready, c + 1)
                pe.wait_ge(gstate_done, c + 1)
                pe.matmul(work[:, 2, 0:GLA_HEADS * GLA_DV], k_tok[:, b, :], row(gv_tok, c), start=True, stop=True
                          ).then_inc(gkv_done, 1)

            def outputs(c, b):
                pe.wait_ge(gatt_masked, c + 1)
                pe.wait_ge(qdec_ready, c + 1)
                pe.wait_ge(go_copied, c + 1)
                o = work[:, b, 0:GLA_HEADS * GLA_DV]
                for h in range(GLA_HEADS):
                    v = slice(h * GLA_DV, (h + 1) * GLA_DV)
                    pe.matmul(o[:, v], q_dec[:, b, :], s_gla[:, v], start=True, stop=False)
                    mm = pe.matmul(o[:, v], att_gla[:, b, h, :], row(gv_tok, c)[:, v], start=False, stop=True)
                mm.then_inc(go_done, 1)

            def chunk(c, b, ahead=True):
                if ahead:
                    turn_keys(c + 1, 1 - b)
                    attend(c + 1, 1 - b)
                sum_keys(c, b)
                outputs(c, b)

            turn_keys(0, 0)
            attend(0, 0)
            with pe.Fori(0, NCHUNK // 2 - 1) as i:
                for b in range(2):
                    chunk(2 * i + b, b)
            chunk(NCHUNK - 2, 0)
            chunk(NCHUNK - 1, 1, ahead=False)
            pe.wait_ge(tok_done, 2 * PAIRS + 1)
            for i in range(2):
                for c in range(NCHUNK):
                    mm = pe.transpose(work[:, 2 * i + c // 4, c % 4 * P:(c % 4 + 1) * P], o_tok[:, c, i * P:(i + 1) * P], ident[:, :])
            mm.then_inc(feat_turned, 1)
            end_stage(pe, 12)

        def act_12(act):
            begin_stage(act, 12)
            act.drain().then_inc(go_copied, 2)
            act.activation(gq_t[:, :], nxt_t[:, 0, :], ACT.Copy, scale=float(GLA_DK) ** -0.5)

            def exp_keys(c, b):
                act.wait_ge(karg_done, c + 1)
                act.activation(e_k[:, b, :, :], e_k[:, b, :, :], ACT.Exp).then_inc(kexp_done, 1)

            def copy_keys(c, b):
                act.wait_ge(kdec_turned, c + 1)
                act.activation(k_tok[:, b, :], work[:, 3, 0:P], ACT.Copy).then_inc(ktok_ready, 1)

            def copy_outputs(c, b):
                act.wait_ge(go_done, c + 1)
                act.activation(row(o_tok, c), work[:, b, 0:GLA_HEADS * GLA_DV], ACT.Copy)
                act.activation(row(o_sq, c), work[:, b, 0:GLA_HEADS * GLA_DV], ACT.Square).then_inc(go_copied, 1)

            exp_keys(0, 0)
            act.wait_ge(decay_args, 1)
            act.activation(e_q[:, :], e_q[:, :], ACT.Exp)
            act.drain().then_inc(decays_ready, 1)
            act.wait_ge(decay_args, 2)
            act.activation(e_end[:, :], e_end[:, :], ACT.Exp)
            act.activation(e_b[:, :].rearrange("p (c t) -> p c t", t=CHUNK), b_now, ACT.Exp)
            act.drain().then_inc(decays_ready, 1)
            exp_keys(1, 1)
            act.wait_ge(v_turned, V11 + 1)
            act.activation(gv_tok[:, :, :], work[:, :, :], ACT.Copy).then_inc(v_ready, 1)
            copy_keys(0, 0)
            exp_keys(2, 0)
            exp_keys(3, 1)
            with act.Fori(0, NCHUNK // 2 - 2) as i:
                for b in range(2):
                    copy_keys(2 * i + b + 1, 1 - b)
                    exp_keys(2 * i + b + 4, b)
                    copy_outputs(2 * i + b, b)
            for c in range(NCHUNK - 4, NCHUNK):
                if c + 1 < NCHUNK:
                    copy_keys(c + 1, (c + 1) % 2)
                copy_outputs(c, c % 2)
            act.wait_ge(ss_ready, PAIRS + 1)
            act.activation(root12[:, :], ss12[:, :], ACT.Sqrt, bias=eps_col[:, :], scale=1.0 / GLA_DV).then_inc(root_ready, 1)
            end_stage(act, 12)

        def dve_12(dve):
            begin_stage(dve, 12)
            dve.drain().then_inc(gstate_done, 1)
            sub = dict(t=SUB)
            own_rows = own[:, :].rearrange("p (h v) -> p h v", v=GLA_DV)[:, :, 0:1]

            def key_args(c, b):
                b_c = b_gla[:, bass.ds(c, 1), :].rearrange("p a t -> p (a t)")
                r_c = b_c[:, 0:CHUNK].rearrange("p (s t) -> p s t", t=SUB)[:, :, 0:1]
                dve.tensor_tensor(e_k[:, b, :, :], r_c.to_broadcast([P, NSUB, CHUNK]),
                                  b_c[:, 1:1 + CHUNK].unsqueeze(1).to_broadcast([P, NSUB, CHUNK]), ALU.subtract).then_inc(karg_done, 1)

            def operands(c, b):
                dve.wait_ge(kexp_done, c + 1)
                dve.scalar_tensor_tensor(k_ref[:, b, :, :], e_k[:, b, :, :], KEY_CAP,
                                         at_chunk(gk_t, c).unsqueeze(1).to_broadcast([P, NSUB, CHUNK]), ALU.min, ALU.mult)
                dve.tensor_tensor(q_own[:, b, :, :, :],
                                  at_chunk(e_q, c).rearrange("p (s t) -> p s t", t=SUB).unsqueeze(2).to_broadcast([P, NSUB, GLA_HEADS, SUB]),
                                  own_rows.unsqueeze(1).to_broadcast([P, NSUB, GLA_HEADS, SUB]), ALU.mult)
                dve.drain().then_inc(chunk_ready, 1)

            def mask_weights(c, b):
                dve.wait_ge(gatt_done, c + 1)
                dve.tensor_tensor(att_gla[:, b, :, :].rearrange("p h (s t) -> p s h t", t=SUB),
                                  accf[:, b * HALF:(b + 1) * HALF].rearrange("p (s h t) -> p s h t", s=NSUB, h=GLA_HEADS),
                                  causal01[:, :].rearrange("p (s t) -> p s t", t=SUB).unsqueeze(2).to_broadcast([P, NSUB, GLA_HEADS, SUB]),
                                  ALU.mult).then_inc(gatt_masked, 1)

            def update_state(c, b):
                dve.wait_ge(gkv_done, c + 1)
                dve.tensor_tensor(kv_own[:, :], work[:, 2, 0:GLA_HEADS * GLA_DV], own[:, :], ALU.mult)
                dve.drain()
                dve.wait_ge(go_done, c + 1)
                dve.scalar_tensor_tensor(s_gla[:, :], s_gla[:, :], at_chunk(e_b, c)[:, CHUNK - 1:CHUNK], kv_own[:, :],
                                         ALU.mult, ALU.add)
                dve.drain().then_inc(gstate_done, 1)

            key_args(0, 0)
            dve.tensor_tensor(e_q[:, :].rearrange("p (c s t) -> p c s t", s=NSUB, **sub), b_now.rearrange("p c (s t) -> p c s t", **sub),
                              b_ref.to_broadcast([P, NCHUNK, NSUB, SUB]), ALU.subtract).then_inc(decay_args, 1)
            dve.tensor_tensor(e_end[:, :].rearrange("p (c t) -> p c t", t=CHUNK), b_gla[:, :, CHUNK:CHUNK + 1].to_broadcast([P, NCHUNK, CHUNK]),
                              b_now, ALU.subtract).then_inc(decay_args, 1)
            key_args(1, 1)
            dve.wait_ge(own_ready, 1)
            dve.wait_ge(decays_ready, 1)
            dve.tensor_tensor(e_q[:, :], e_q[:, :], gq_t[:, :], ALU.mult)
            dve.drain()
            for c in range(2):
                operands(c, c)
                key_args(c + 2, c)
            with dve.Fori(0, NCHUNK // 2 - 2) as i:
                for b in range(2):
                    c = 2 * i + b
                    mask_weights(c, b)
                    operands(c + 2, b)
                    key_args(c + 4, b)
                    update_state(c, b)
            for c in range(NCHUNK - 4, NCHUNK):
                mask_weights(c, c % 2)
                if c + 2 < NCHUNK:
                    operands(c + 2, c % 2)
                update_state(c, c % 2)
            heads = dict(d=GLA_DV)
            for c0, c1 in ((0, NCHUNK - 2), (NCHUNK - 2, NCHUNK)):
                dve.wait_ge(go_copied, c1 + 2)
                e = dve.tensor_reduce(ss12[:, c0 * GLA_HEADS:c1 * GLA_HEADS],
                                      o_sq[:, c0:c1, :].rearrange("p c (h d) -> p (c h) d", **heads), AX.X, ALU.add)
            e.then_inc(ss_ready, 1)
            dve.wait_ge(root_ready, PAIRS + 1)
            dve.reciprocal(inv12[:, :], root12[:, :])
            dve.drain()
            o_h = o_tok[:, :, :].rearrange("p c (h d) -> p (c h) d", **heads)
            dve.tensor_tensor(o_h, o_h, inv12[:, :].unsqueeze(2).to_broadcast([P, NCHUNK * GLA_HEADS, GLA_DV]), ALU.mult
                              ).then_inc(tok_done, 1)
            dve.wait_ge(feat_turned, 2 * PAIRS + 1)
            for i in range(2):
                g_col = vec2[:, VEC2["gla_norm_g_2"][0] + i:][:, 0:1]
                dve.scalar_tensor_tensor(y2[:, 6 + i, :], work[:, 2 * i:2 * i + 2, :].rearrange("p a b -> p (a b)"), g_col,
                                         y2[:, 6 + i, :], ALU.mult, ALU.mult)
            end_stage(dve, 12)

        ar = Region(at_arena + 4 * T * 4, arena_end)
        root8_back = ar("root8_back", [P, T])
        rstd8 = ar("rstd8", [P, T])

        def sp_13(sp):
            with sp.Fori(0, 3) as j:
                for b in range(2):
                    load_w(sp, N_OUT2 + 2 + b, cols(w_out2, (2 + b) * P + 2 * P * j), adv=j)

        def pool_13(pool):
            begin_stage(pool, 13)
            pool.dma_start(root8_back[:, :], root8_scr).then_inc(g_loaded, 16)
            pool.dma_start(final_g[:, :], io["final_g_2"].partition_broadcast(P)).then_inc(g_loaded, 16)
            end_stage(pool, 13)

        def pe_13(pe):
            begin_stage(pe, 13)
            project(pe, N_OUT2, ha_hi, ha_lo, after=LO_SPLITS[13])
            with pe.Fori(0, 3) as j:
                for b in range(2):
                    project(pe, N_OUT2 + 1 + b, ha_hi, ha_lo, adv=j)
            project(pe, N_TILES - 1, ha_hi, ha_lo)
            end_stage(pe, 13)

        def act_13(act):
            begin_stage(act, 13)
            for k in range(KT):
                act.activation(ha_hi[:, k, :], y2[:, k, :], ACT.Copy).then_inc(x_hi_done, 1)
            with act.Fori(0, 3) as j:
                for b in range(2):
                    split_hi(act, N_OUT2 + b + 1, adv=j)
            split_hi(act, N_TILES - 1)
            end_stage(act, 13)

        def dve_13(dve):
            begin_stage(dve, 13)
            for k in range(KT):
                dve.wait_ge(x_hi_done, SPLITS[13] + k + 1)
                dve.tensor_tensor(ha_lo[:, k, :], y2[:, k, :], ha_hi[:, k, :].bitcast(F32), ALU.subtract).then_inc(x_lo_done, 1)

            def add_residual(n, f, adv=0):
                x = row(res, f)
                dve.scalar_tensor_tensor(x, x, dcol(vec1, VEC1, "final_norm_w", f), rstd8[:, :], ALU.mult, ALU.mult)
                dve.drain()
                projected(dve, n, adv=adv)
                dve.tensor_tensor(x, acc[:, n % 2, :], x, ALU.add).then_inc(acc_free[n % 2], 1)

            split_lo(dve, N_OUT2 + 1)
            dve.wait_ge(res_back, 16)
            dve.wait_ge(g_loaded, 32)
            dve.reciprocal(rstd8[:, :], root8_back[:, :])
            dve.drain()
            add_residual(N_OUT2, 0)
            with dve.Fori(0, 3) as j:
                for b in range(2):
                    split_lo(dve, N_OUT2 + 2 + b, adv=j)
                    add_residual(N_OUT2 + 1 + b, 2 * j + b + 1, adv=j)
            add_residual(N_TILES - 1, KT - 1)
            end_stage(dve, 13)

        ar = Region(at_arena, arena_end)
        final_g = ar("final_g", [P, D])
        x2_sq = ar("x2_sq", [P, 2, D])
        ss14 = ar("ss14", [P, NT])
        root14 = ar("root14", [P, NT])
        inv14 = ar("inv14", [P, NT])
        out_tok = Region(at_ya + big, at_ya + 2 * big)("out_tok", [P, NT, D])
        g_loaded, x2_turned, x2_rooted, out_ready, stored = (sem("g_loaded"), sem("x2_turned"),
                                                                        sem("x2_rooted"), sem("out_ready"), sem("stored"))
        banks14 = [acc[:, 0, :], acc[:, 1, :], work[:, 0:2, :].rearrange("p a b -> p (a b)"),
                   work[:, 2:4, :].rearrange("p a b -> p (a b)")]

        def sp_14(sp):
            dst = out.rearrange("a (t p) d -> p (a t) d", p=P)
            for i in range(NT):
                sp.wait_ge(out_ready, i + 1)
                sp.dma_start(dst[:, i, :], out_tok[:, i, :]).then_inc(stored, 16)
            sp.wait_ge(stored, 16 * NT)

        def pool_14(pool):
            begin_stage(pool, 14)
            end_stage(pool, 14)

        def pe_14(pe):
            begin_stage(pe, 14)
            for i in range(NT):
                if i >= 4:
                    pe.wait_ge(out_ready, i - 3)
                for f in range(KT):
                    mm = pe.transpose(banks14[i % 4][:, f * P:(f + 1) * P], res[:, f, i * P:(i + 1) * P], ident[:, :])
                mm.then_inc(x2_turned, 1)
            end_stage(pe, 14)

        def act_14(act):
            begin_stage(act, 14)
            for i in range(NT):
                act.wait_ge(x2_turned, i + 1)
                act.activation(x2_sq[:, i % 2, :], banks14[i % 4], ACT.Square, accum_out=ss14[:, i:i + 1])
                act.drain()
                act.activation(root14[:, i:i + 1], ss14[:, i:i + 1], ACT.Sqrt, bias=eps_col[:, :], scale=1.0 / D).then_inc(x2_rooted, 1)
            end_stage(act, 14)

        def dve_14(dve):
            begin_stage(dve, 14)
            for i in range(NT):
                dve.wait_ge(x2_rooted, i + 1)
                dve.reciprocal(inv14[:, i:i + 1], root14[:, i:i + 1])
                dve.drain()
                dve.scalar_tensor_tensor(out_tok[:, i, :], banks14[i % 4], inv14[:, i:i + 1], final_g[:, :],
                                         ALU.mult, ALU.mult).then_inc(out_ready, 1)
            end_stage(dve, 14)

        block = ctx.enter_context(nc.Block())

        @block.sync
        def _(sp):
            sp_0(sp)
            sp_1(sp)
            sp_2(sp)
            sp_3(sp)
            sp_4(sp)
            sp_5(sp)
            sp_6(sp)
            sp_7(sp)
            sp_8(sp)
            sp_9(sp)
            sp_10(sp)
            sp_11(sp)
            sp_12(sp)
            sp_13(sp)
            sp_14(sp)

        @block.scalar
        def _(act):
            act_0(act)
            act_1(act)
            act_2(act)
            act_3(act)
            act_4(act)
            act_5(act)
            act_6(act)
            act_7(act)
            act_8(act)
            act_9(act)
            act_10(act)
            act_11(act)
            act_12(act)
            act_13(act)
            act_14(act)

        @block.tensor
        def _(pe):
            pe_0(pe)
            pe_1(pe)
            pe_2(pe)
            pe_3(pe)
            pe_4(pe)
            pe_5(pe)
            pe_6(pe)
            pe_7(pe)
            pe_8(pe)
            pe_9(pe)
            pe_10(pe)
            pe_11(pe)
            pe_12(pe)
            pe_13(pe)
            pe_14(pe)

        @block.vector
        def _(dve):
            dve_0(dve)
            dve_1(dve)
            dve_2(dve)
            dve_3(dve)
            dve_4(dve)
            dve_5(dve)
            dve_6(dve)
            dve_7(dve)
            dve_8(dve)
            dve_9(dve)
            dve_10(dve)
            dve_11(dve)
            dve_12(dve)
            dve_13(dve)
            dve_14(dve)

        @block.gpsimd
        def _(pool):
            pool_0(pool)
            pool_1(pool)
            pool_2(pool)
            pool_3(pool)
            pool_4(pool)
            pool_5(pool)
            pool_6(pool)
            pool_7(pool)
            pool_8(pool)
            pool_9(pool)
            pool_10(pool)
            pool_11(pool)
            pool_12(pool)
            pool_13(pool)
            pool_14(pool)


_INS = ["x", "c", "w_ada", "b_ada", "norm_w", "w_in", "conv_w", "conv_b", "dt_bias", "a_log", "d_skip",
        "ssm_norm_w", "b_f", "b_gate", "w_proj_ssm", "w_proj_att", "w_out", "final_norm_w", "norm_g_2",
        "w_in_2", "b_gates_2", "conv_w_2", "w_alpha_2", "b_alpha_2", "rel_bias_2", "ml_norm_g_2",
        "gla_norm_g_2", "w_out_2", "final_g_2"]


def kernel(**inputs):
    import numpy as np
    import concourse.bacc as bacc
    from concourse.bass_utils import run_bass_kernel_spmd

    arrays = {name: np.ascontiguousarray(inputs[name]) for name in _INS}
    arrays["rel_bias_2"] = np.ascontiguousarray(arrays["rel_bias_2"][:, :, ::-1])
    nc = bacc.Bacc("TRN2", target_bir_lowering=False, num_devices=1)
    io = {name: nc.dram_tensor(f"in_{name}", a.shape, F32, kind="ExternalInput").ap() for name, a in arrays.items()}
    out = nc.dram_tensor("out", [1, T, D], F32, kind="ExternalOutput").ap()
    build(nc, io, out)
    r = run_bass_kernel_spmd(nc, [{f"in_{name}": a for name, a in arrays.items()}], core_ids=[0])
    return r.results[0]["out"]
```
